# Optimizing a Trainium2 kernel written in Bass

```python
import math
import jax, jax.numpy as jnp
from jax import lax
import numpy as np

D_MODEL = 1024
BATCH = 1
SEQ = 1024
DEPTH = 1

DSWA_PATTERNS = ((128, 1), (512, 4), (2048, 16))
DSWA_GROUPS = 3
DSWA_HEADS = 4
DSWA_HEAD_DIM = 64
DSWA_BLOCK = 128
CONV_CH = 256
CONV_WIDTH = 31
GLA_HEADS = 4
GLA_DK = 64
GLA_DV = 128
GLA_GATE_RANK = 16
GLA_TAU = 16.0
GLA_CHUNK = 64
SB_HEADS = 4
SB_HEAD_DIM = 64
SB_BLOCK = 128
N_BRANCH = 4
D_FF = 4 * D_MODEL
NORM_EPS = 1e-6

A_QK = DSWA_GROUPS * DSWA_HEADS * DSWA_HEAD_DIM
A_OUT = DSWA_HEADS * DSWA_HEAD_DIM
C_QK = GLA_HEADS * GLA_DK
C_V = GLA_HEADS * GLA_DV
D_W = SB_HEADS * SB_HEAD_DIM
IN_SPLITS = (A_QK, A_QK, A_QK, 2 * CONV_CH, C_QK, C_QK, C_V, C_V, GLA_GATE_RANK, D_W, D_W, D_W, N_BRANCH * D_MODEL)
IN_WIDTH = sum(IN_SPLITS)

kernel_name = "hybrid_gated_parallel_mixer_block"

def rms_norm(x, g):
    xf = x.astype(jnp.float32)
    y = xf * lax.rsqrt(jnp.mean(xf * xf, axis=-1, keepdims=True) + NORM_EPS)
    return (y * g.astype(jnp.float32)).astype(x.dtype)

def layer_norm(x, g, b):
    xf = x.astype(jnp.float32)
    mu = jnp.mean(xf, axis=-1, keepdims=True)
    var = jnp.mean(jnp.square(xf - mu), axis=-1, keepdims=True)
    y = (xf - mu) * lax.rsqrt(var + NORM_EPS)
    return (y * g.astype(jnp.float32) + b.astype(jnp.float32)).astype(x.dtype)

def alibi_slopes(n):
    return jnp.asarray(2.0 ** (-8.0 * np.arange(1, n + 1) / n), dtype=jnp.float32)

def dilated_window_group(q, k, v, dilation, window, slopes):
    bsz, seq, nh, hd = q.shape
    span = dilation * DSWA_BLOCK
    seq_pad = -(-seq // span) * span
    pad = seq_pad - seq
    m = seq_pad // dilation
    nb = m // DSWA_BLOCK

    def to_blocks(t):
        t = jnp.pad(t, ((0, 0), (0, pad), (0, 0), (0, 0)))
        t = t.reshape(bsz, m, dilation, nh, hd).transpose(0, 2, 1, 3, 4)
        return t.reshape(bsz, dilation, nb, DSWA_BLOCK, nh, hd)

    def band(t):
        prev = jnp.pad(t, ((0, 0), (0, 0), (1, 0), (0, 0), (0, 0), (0, 0)))[:, :, :-1]
        return jnp.concatenate([prev, t], axis=3)

    qb, kb, vb = to_blocks(q), to_blocks(k), to_blocks(v)
    kk, vv = band(kb), band(vb)
    scores = jnp.einsum('bdnqhe,bdnkhe->bdnhqk', qb, kk).astype(jnp.float32) * (hd ** -0.5)
    qi = jnp.arange(DSWA_BLOCK)
    ki = jnp.arange(2 * DSWA_BLOCK) - DSWA_BLOCK
    rel = qi[:, None] - ki[None, :]
    blk = jnp.arange(nb)
    valid = ((rel >= 0) & (rel <= window // dilation))[None] & (
        (blk[:, None, None] * DSWA_BLOCK + ki[None, None, :]) >= 0)
    bias = -slopes[:, None, None] * (dilation * rel).astype(jnp.float32)
    scores = jnp.where(valid[None, None, :, None], scores + bias, -jnp.inf)
    mx = jnp.max(scores, axis=-1, keepdims=True)
    p = jnp.exp(scores - mx)
    den = jnp.sum(p, axis=-1)
    o = jnp.einsum('bdnhqk,bdnkhe->bdnqhe', p, vv.astype(jnp.float32))
    o = o / jnp.swapaxes(den, 3, 4)[..., None]
    lse = jnp.swapaxes(mx[..., 0] + jnp.log(den), 3, 4)

    def from_blocks(t):
        rest = t.shape[4:]
        t = jnp.swapaxes(t.reshape((bsz, dilation, m) + rest), 1, 2)
        return t.reshape((bsz, seq_pad) + rest)[:, :seq]

    return from_blocks(o), from_blocks(lse)

def dilated_attention_mixer(q, k, v, q_gain, k_gain):
    b, s, _ = q.shape
    shp = (b, s, DSWA_GROUPS, DSWA_HEADS, DSWA_HEAD_DIM)
    q = rms_norm(q.reshape(shp), q_gain)
    k = rms_norm(k.reshape(shp), k_gain)
    v = v.reshape(shp)
    slopes = alibi_slopes(DSWA_GROUPS * DSWA_HEADS).reshape(DSWA_GROUPS, DSWA_HEADS)
    outs, lses = [], []
    for g, (window, dilation) in enumerate(DSWA_PATTERNS):
        o, lse = dilated_window_group(q[:, :, g], k[:, :, g], v[:, :, g], dilation, window, slopes[g])
        outs.append(o)
        lses.append(lse)
    wts = jax.nn.softmax(jnp.stack(lses), axis=0)
    o = jnp.sum(wts[..., None] * jnp.stack(outs), axis=0)
    return o.reshape(b, s, A_OUT).astype(q.dtype)

def conformer_conv_mixer(u, conv_w, conv_b, ln_g, ln_b):
    a, gate = jnp.split(u, 2, axis=-1)
    y = a * jax.nn.sigmoid(gate)
    y = lax.conv_general_dilated(y, conv_w[:, None, :].astype(y.dtype), window_strides=(1,),
                                 padding=((CONV_WIDTH - 1, 0),),
                                 dimension_numbers=('NWC', 'WIO', 'NWC'),
                                 feature_group_count=CONV_CH) + conv_b
    return jax.nn.silu(layer_norm(y, ln_g, ln_b))

def gla_mixer(q, k, v, r, g_low, w_gate, b_gate, o_gain):
    f32 = jnp.float32
    b, s, _ = q.shape
    n = s // GLA_CHUNK
    log_a = jax.nn.log_sigmoid((g_low @ w_gate + b_gate).astype(f32)) / GLA_TAU

    def chunks(t, e):
        return t.reshape(b, n, GLA_CHUNK, GLA_HEADS, e).transpose(1, 0, 3, 2, 4)

    qc = chunks(q.astype(f32) * (GLA_DK ** -0.5), GLA_DK)
    kc = chunks(k.astype(f32), GLA_DK)
    vc = chunks(v.astype(f32), GLA_DV)
    gc = chunks(log_a, GLA_DK)
    causal = jnp.tril(jnp.ones((GLA_CHUNK, GLA_CHUNK), dtype=bool))

    def step(state, xs):
        qt, kt, vt, gt = xs
        cum = jnp.cumsum(gt, axis=2)
        o_inter = jnp.einsum('bhtk,bhkv->bhtv', qt * jnp.exp(cum), state)
        diff = cum[:, :, :, None, :] - cum[:, :, None, :, :]
        decay = jnp.exp(jnp.where(causal[:, :, None], diff, -jnp.inf))
        att = jnp.einsum('bhtk,bhsk,bhtsk->bhts', qt, kt, decay)
        o = o_inter + jnp.einsum('bhts,bhsv->bhtv', att, vt)
        last = cum[:, :, -1:, :]
        state = jnp.exp(last[:, :, 0, :, None]) * state + jnp.einsum(
            'bhsk,bhsv->bhkv', kt * jnp.exp(last - cum), vt)
        return state, o

    state0 = jnp.zeros((b, GLA_HEADS, GLA_DK, GLA_DV), f32)
    _, o = lax.scan(step, state0, (qc, kc, vc, gc))
    o = o.transpose(1, 0, 3, 2, 4).reshape(b, s, GLA_HEADS, GLA_DV)
    o = rms_norm(o, o_gain).reshape(b, s, C_V)
    return (jax.nn.silu(r.astype(f32)) * o).astype(q.dtype)

def stick_breaking_mixer(q, k, v):
    f32 = jnp.float32
    b, s, _ = q.shape

    def heads(t):
        return t.reshape(b, s, SB_HEADS, SB_HEAD_DIM).transpose(0, 2, 1, 3)

    q, k, v = heads(q), heads(k), heads(v)
    vf = v.astype(f32)
    nb = s // SB_BLOCK
    q_blocks = q.reshape(b, SB_HEADS, nb, SB_BLOCK, SB_HEAD_DIM).transpose(2, 0, 1, 3, 4)
    key_pos = jnp.arange(s)
    scale = SB_HEAD_DIM ** -0.5

    def block(args):
        qb, i = args
        z = jnp.einsum('bhqe,bhke->bhqk', qb, k).astype(f32) * scale
        q_pos = i * SB_BLOCK + jnp.arange(SB_BLOCK)
        mask = key_pos[None, :] < q_pos[:, None]
        log_keep = jnp.where(mask, jax.nn.log_sigmoid(-z), 0.0)
        after = lax.cumsum(log_keep, axis=3, reverse=True) - log_keep
        w = jnp.where(mask, jnp.exp(jax.nn.log_sigmoid(z) + after), 0.0)
        return jnp.einsum('bhqk,bhke->bhqe', w, vf)

    o = lax.map(block, (q_blocks, jnp.arange(nb)))
    return o.transpose(1, 0, 3, 2, 4).reshape(b, s, D_W).astype(q.dtype)

def setup_inputs(seed: int = 0) -> dict:
    key = jax.random.key(seed)
    ks = jax.random.split(key, 26)
    L, D = DEPTH, D_MODEL

    def nrm(k, shape, scale):
        return jax.random.normal(k, shape, jnp.float32) * scale

    def gain(k, shape):
        return 1.0 + nrm(k, shape, 0.05)

    return {
        "x": nrm(ks[0], (BATCH, SEQ, D), 1.0),
        "c": nrm(ks[1], (BATCH, D), 1.0),
        "w_ada": nrm(ks[2], (L, D, 6 * D), 0.5 * D ** -0.5),
        "b_ada": nrm(ks[3], (L, 6 * D), 0.02),
        "g_mix": gain(ks[4], (L, D)),
        "w_in": nrm(ks[5], (L, D, IN_WIDTH), D ** -0.5),
        "q_gain": gain(ks[6], (L, DSWA_HEAD_DIM)),
        "k_gain": gain(ks[7], (L, DSWA_HEAD_DIM)),
        "conv_w": nrm(ks[8], (L, CONV_WIDTH, CONV_CH), CONV_WIDTH ** -0.5),
        "conv_b": nrm(ks[9], (L, CONV_CH), 0.02),
        "conv_ln_g": gain(ks[10], (L, CONV_CH)),
        "conv_ln_b": nrm(ks[11], (L, CONV_CH), 0.02),
        "gla_w_gate": nrm(ks[12], (L, GLA_GATE_RANK, C_QK), GLA_GATE_RANK ** -0.5),
        "gla_b_gate": nrm(ks[13], (L, C_QK), 0.1),
        "gla_o_gain": gain(ks[14], (L, GLA_DV)),
        "w_br_a": nrm(ks[15], (L, A_OUT, D), A_OUT ** -0.5),
        "w_br_b": nrm(ks[16], (L, CONV_CH, D), CONV_CH ** -0.5),
        "w_br_c": nrm(ks[17], (L, C_V, D), C_V ** -0.5),
        "w_br_d": nrm(ks[18], (L, D_W, D), D_W ** -0.5),
        "w_out": nrm(ks[19], (L, D, D), D ** -0.5),
        "g_mlp": gain(ks[20], (L, D)),
        "w_up": nrm(ks[21], (L, D, D_FF), D ** -0.5),
        "w_down": nrm(ks[22], (L, D_FF, D), D_FF ** -0.5),
    }

def reference(x, c, w_ada, b_ada, g_mix, w_in, q_gain, k_gain, conv_w, conv_b, conv_ln_g, conv_ln_b,
              gla_w_gate, gla_b_gate, gla_o_gain, w_br_a, w_br_b, w_br_c, w_br_d, w_out,
              g_mlp, w_up, w_down):
    bsz, seq, _ = x.shape
    split_points = np.cumsum(IN_SPLITS)[:-1].tolist()
    for l in range(DEPTH):
        mod = (c @ w_ada[l] + b_ada[l])[:, None, :]
        sh1, sc1, gt1, sh2, sc2, gt2 = jnp.split(mod, 6, axis=-1)

        h = rms_norm(x, g_mix[l]) * (1.0 + sc1) + sh1
        (a_q, a_k, a_v, conv_in, c_q, c_k, c_v, c_r, c_low,
         d_q, d_k, d_v, gate_logits) = jnp.split(h @ w_in[l], split_points, axis=-1)

        y_a = dilated_attention_mixer(a_q, a_k, a_v, q_gain[l], k_gain[l]) @ w_br_a[l]
        y_b = conformer_conv_mixer(conv_in, conv_w[l], conv_b[l], conv_ln_g[l], conv_ln_b[l]) @ w_br_b[l]
        y_c = gla_mixer(c_q, c_k, c_v, c_r, c_low, gla_w_gate[l], gla_b_gate[l], gla_o_gain[l]) @ w_br_c[l]
        y_d = stick_breaking_mixer(d_q, d_k, d_v) @ w_br_d[l]

        gates = jax.nn.sigmoid(gate_logits).reshape(bsz, seq, N_BRANCH, D_MODEL)
        merged = (gates[:, :, 0] * y_a + gates[:, :, 1] * y_b
                  + gates[:, :, 2] * y_c + gates[:, :, 3] * y_d)
        x = x + gt1 * (merged @ w_out[l])

        h = rms_norm(x, g_mlp[l]) * (1.0 + sc2) + sh2
        x = x + gt2 * (jnp.square(jax.nn.relu(h @ w_up[l])) @ w_down[l])
    return x


_drawn_inputs = setup_inputs


def setup_inputs(seed=0):
    import zlib

    import numpy as np

    out = dict(_drawn_inputs(seed))
    spreads = {}
    factors = {'q_gain': 8.0,
     'k_gain': 8.0,
     'conv_b': 8.0,
     'conv_ln_g': 5.552,
     'conv_ln_b': 27.231,
     'gla_b_gate': 4.487,
     'gla_o_gain': 5.514}
    for name, (base, spread) in spreads.items():
        noise = np.random.default_rng([zlib.crc32(name.encode()), seed]).standard_normal(out[name].shape)
        drawn = base * np.exp(spread * noise) if base else spread * noise
        out[name] = __import__('jax').numpy.asarray(drawn.astype(out[name].dtype))
    for name, factor in factors.items():
        out[name] = (out[name] * factor).astype(out[name].dtype)
    return out
```

```python
from contextlib import ExitStack

import concourse.bass as bass
from concourse import mybir

F32 = mybir.dt.float32
F32R = mybir.dt.float32r
U8 = mybir.dt.uint8
I32 = mybir.dt.int32
ACT = mybir.ActivationFunctionType
ALU = mybir.AluOpType
AX = mybir.AxisListType

P = 128
D = 1024
S = 1024
KT = D // P
HALF = 512
NH = S // HALF
EPS = 1e-6
D_FF = 4 * D

A_TILES = 6
RANK = 16
COL_LOW = 34 * P
COL_D = COL_LOW + RANK
COL_GATES = COL_D + 6 * P
R_AQ, R_AK, R_AV, R_CONV, R_CQ, R_CK, R_CV, R_CR, R_DQ, R_DK, R_DV, R_LOW = 0, 6, 12, 18, 22, 24, 26, 30, 34, 36, 38, 40
PROJ_ROWS = 40 * P + RANK
Y_A, Y_B, Y_C, Y_D = 0, 2, 4, 8
Y_TILES = 10
Y_FIRST = [Y_A, Y_B, Y_C, Y_D, Y_TILES]

V_BADA, V_GMIX, V_GMLP, V_CB, V_LNG, V_LNB, V_BG, V_OG, V_QG, V_KG, V_C = 0, 48, 56, 64, 66, 68, 70, 72, 73, 74, 75
V_ROWS = V_C + KT
N_MOD = 48
M_SH1, M_SC1, M_GT1, M_SH2, M_SC2, M_GT2 = 0, 8, 16, 24, 32, 40


class Kernel:

    in_use = []


def sems(nc, ctx, *names):
    Kernel.in_use += [nc.alloc_semaphore(n) for n in names]
    return Kernel.in_use[-len(names):]


def recycle_semaphores(nc):
    nc.clear_and_free_semaphores(Kernel.in_use)
    Kernel.in_use = []
    nc.all_engine_barrier()


def feature_tiles(ap):
    return ap.rearrange("(t p) c -> p t c", p=P)


ADA_FIRST = 2 * KT
ADA_CHUNK = 2


def stage_prepare(nc, k, x, c, w_ada, b_ada, g_mix, g_mlp, conv_w, conv_b, ln_g, ln_b, b_gate, o_gain, q_gain, k_gain, xT):
    with ExitStack() as ctx:
        x_rows = ctx.enter_context(nc.sbuf_tensor("x_rows", [P, 2, D], F32))
        vec_rows = ctx.enter_context(nc.sbuf_tensor("vec_rows", [P, P], F32))
        convw_rows = ctx.enter_context(nc.sbuf_tensor("convw_rows", [31, 2 * P], F32))
        ada = ctx.enter_context(nc.sbuf_tensor("ada", [P, 2, KT, HALF], F32))
        ada_sum = ctx.enter_context(nc.sbuf_tensor("ada_sum", [P, 4, HALF], F32))
        ps_t = ctx.enter_context(nc.psum_tensor("ps_t", [P, 4, HALF], F32))
        ps_v = ctx.enter_context(nc.psum_tensor("ps_v", [P, HALF], F32))
        ps_m = ctx.enter_context(nc.psum_tensor("ps_m", [P, HALF], F32))
        vec_zeroed, vec_in = sems(nc, ctx, "vec_zeroed", "vec_in")
        x_in = sems(nc, ctx, "x_in0", "x_in1")
        ada_in = sems(nc, ctx, "ada_in0", "ada_in1")
        const_step, const_ready, turned, taken, vec_turned, vec_taken, ada_step, ada_done, mod_done, xt_out = sems(
            nc, ctx, "const_step", "const_ready", "turned", "taken", "vec_turned", "vec_taken", "ada_step", "ada_done", "mod_done", "xt_out")
        norm = norm_parts(nc, k, ctx, "n1", xT, k.scale1, k.mod[:, M_SH1:M_SH1 + KT], k.h_hi, k.h_lo)
        block = ctx.enter_context(nc.Block())
        x_view = x[0].rearrange("(t p) d -> p t d", p=P)
        ada_view = w_ada[0].rearrange("(t p) n -> p t n", p=P)
        vec = [
            (V_C, c[0].rearrange("(r p) -> r p", p=P)),
            (V_BADA, b_ada[0].rearrange("(r p) -> r p", p=P)), (V_GMIX, g_mix[0].rearrange("(r p) -> r p", p=P)),
            (V_GMLP, g_mlp[0].rearrange("(r p) -> r p", p=P)), (V_CB, conv_b[0].rearrange("(r p) -> r p", p=P)),
            (V_LNG, ln_g[0].rearrange("(r p) -> r p", p=P)), (V_LNB, ln_b[0].rearrange("(r p) -> r p", p=P)),
            (V_BG, b_gate[0].rearrange("(r p) -> r p", p=P)), (V_OG, o_gain),
        ]
        n_vec = len(vec) + 4 + 1
        N_ADA = ADA_FIRST * P // HALF

        @block.sync
        def _(sp):
            for t in range(2):
                sp.dma_start(x_rows[:, t], x_view[:, t]).then_inc(x_in[t], 16)
            sp.dma_start(ada[:, 0], ada_view[:, :, 0:HALF]).then_inc(ada_in[0], 16)
            for t in range(2, KT):
                sp.wait_ge(turned, 2 * (t - 1))
                sp.dma_start(x_rows[:, t % 2], x_view[:, t]).then_inc(x_in[t % 2], 16)
                if t == 3:
                    sp.dma_start(ada[:, 1], ada_view[:, :, HALF:2 * HALF]).then_inc(ada_in[1], 16)
            for n in range(2, N_ADA):
                sp.wait_ge(ada_step, KT * (n - 1))
                sp.dma_start(ada[:, n % 2], ada_view[:, :, n * HALF:(n + 1) * HALF]).then_inc(ada_in[n % 2], 16)
            sp.wait_ge(taken, 2 * KT)
            sp.dma_start(feature_tiles(k.xT_dram), xT[:, :, :]).then_inc(xt_out, 16)
            sp.wait_ge(xt_out, 16)

        @block.gpsimd
        def _(pool):
            nc.gpsimd.memset(k.ident[:, :], 0.0)
            nc.gpsimd.memset(k.ones[:, :], 1.0)
            nc.gpsimd.memset(k.eps[:, :], EPS)
            nc.gpsimd.memset(k.reach[:, :], 1.0).then_inc(const_step, 1)
            pool.wait_ge(const_step, 1)
            nc.gpsimd.affine_select(out=k.ident[:, :], in_=k.ident[:, :], compare_op=ALU.not_equal, fill=1.0,
                                    base=0, pattern=[[-1, P]], channel_multiplier=1).then_inc(const_ready, 1)
            nc.gpsimd.affine_select(out=k.reach[:, :], in_=k.reach[:, :], compare_op=ALU.is_ge, fill=0.0,
                                    base=0, pattern=[[-1, P]], channel_multiplier=1).then_inc(const_ready, 1)
            norm.gpsimd(pool)

        @block.scalar
        def _(act):
            act.wait_ge(vec_zeroed, 1)
            for row, src in vec:
                act.dma_start(vec_rows[row:row + src.shape[0], :], src).then_inc(vec_in, 16)
            for row, src in ((V_QG, q_gain), (V_KG, k_gain)):
                for h in range(2):
                    act.dma_start(vec_rows[row:row + 1, 64 * h:64 * h + 64], src).then_inc(vec_in, 16)
            act.dma_start(convw_rows[:, :], conv_w[0]).then_inc(vec_in, 16)
            for g in range(2 * KT):
                act.wait_ge(turned, g + 1)
                tt, q = g // 2, g % 2
                nc.scalar.activation(xT[:, 4 * q:4 * q + 4, tt * P:(tt + 1) * P],
                                     ps_t[:, g % 4, :].rearrange("p (a b) -> p a b", a=4), ACT.Copy).then_inc(taken, 1)
            act.wait_ge(taken, 2 * KT)
            norm.scalar(act, lambda t: None)

        @block.vector
        def _(dve):
            nc.vector.memset(vec_rows[:, :], 0.0).then_inc(vec_zeroed, 1)
            for a in range(2):
                for b in range(2):
                    nc.vector.memset(k.headsum[64 * a:64 * a + 64, 64 * b:64 * b + 64], 1.0 if a == b else 0.0)
            dve.wait_ge(vec_turned, 1)
            nc.vector.tensor_copy(k.cols[:, :], ps_v[:, 0:P]).then_inc(vec_taken, 1)
            dve.wait_ge(vec_turned, 2)
            nc.vector.tensor_copy(k.taps[:, :, :], ps_v[:, P:P + 64].rearrange("p (c j) -> p c j", c=2)[:, :, 0:31]).then_inc(vec_taken, 1)
            dve.wait_ge(vec_taken, 1)
            for n in range(N_ADA):
                dve.wait_ge(ada_in[n % 2], 16 * (n // 2 + 1))
                for kt in range(KT):
                    ck = k.cols[:, V_C + kt:V_C + kt + 1]
                    if kt == 0:
                        ins = nc.vector.tensor_scalar(ada_sum[:, n], ada[:, n % 2, kt], ck, None, ALU.mult)
                    else:
                        dve.wait_ge(ada_step, KT * n + kt)
                        ins = nc.vector.scalar_tensor_tensor(out=ada_sum[:, n], in0=ada[:, n % 2, kt], scalar=ck, in1=ada_sum[:, n],
                                                             op0=ALU.mult, op1=ALU.add)
                    ins.then_inc(ada_step, 1)
            dve.wait_ge(ada_done, 1)
            nc.vector.tensor_tensor(k.mod[:, 0:ADA_FIRST], ps_m[:, 0:ADA_FIRST], k.cols[:, V_BADA:V_BADA + ADA_FIRST], ALU.add).then_inc(mod_done, 1)
            dve.wait_ge(mod_done, 1)
            nc.vector.scalar_tensor_tensor(out=k.scale1[:, :], in0=k.mod[:, M_SC1:M_SC1 + KT], scalar=1.0,
                                           in1=k.cols[:, V_GMIX:V_GMIX + KT], op0=ALU.add, op1=ALU.mult).then_inc(mod_done, 1)
            dve.wait_ge(mod_done, 2)
            norm.vector(dve)

        @block.tensor
        def _(pe):
            pe.wait_ge(const_ready, 2)
            pe.wait_ge(vec_in, 16 * n_vec)
            nc.tensor.transpose(ps_v[:, 0:P], vec_rows[:, :], k.ident[:, :]).then_inc(vec_turned, 1)
            pe.wait_ge(vec_taken, 1)
            for c2 in range(2):
                last = nc.tensor.transpose(ps_v[:, P + 32 * c2:P + 32 * c2 + 31], convw_rows[:, c2 * P:(c2 + 1) * P], k.ident[0:31, 0:31])
            last.then_inc(vec_turned, 1)
            for g in range(2 * KT):
                if g % 2 == 0:
                    pe.wait_ge(x_in[g // 2 % 2], 16 * (g // 4 + 1))
                if g >= 4:
                    pe.wait_ge(taken, g - 3)
                for a in range(4):
                    last = nc.tensor.transpose(ps_t[:, g % 4, a * P:(a + 1) * P],
                                               x_rows[:, g // 2 % 2, (4 * (g % 2) + a) * P:(4 * (g % 2) + a + 1) * P], k.ident[:, :])
                last.then_inc(turned, 1)
            norm.tensor(pe)
            pe.wait_ge(ada_step, KT * N_ADA)
            for m in range(ADA_FIRST):
                last = nc.tensor.matmul(ps_m[:, m:m + 1], ada_sum[:, m // 4, (m % 4) * P:(m % 4 + 1) * P], k.ones[:, 0:1], start=True, stop=True)
            last.then_inc(ada_done, 1)


def norm_parts(nc, k, ctx, name, xT, scale, shift, h_hi, h_lo):
    sq = ctx.enter_context(nc.sbuf_tensor(f"{name}_sq", [P, 2, S], F32))
    rinv = ctx.enter_context(nc.sbuf_tensor(f"{name}_rinv", [P, S], F32))
    xn = ctx.enter_context(nc.sbuf_tensor(f"{name}_xn", [P, 2, S], F32))
    hf = ctx.enter_context(nc.sbuf_tensor(f"{name}_hf", [P, 2, S], F32))
    ps = ctx.enter_context(nc.psum_tensor(f"{name}_ps", [P, NH, HALF], F32))
    squared, summed, logged, rooted, scaled, hi_ready, full_ready, lo_ready = sems(
        nc, ctx, *(f"{name}_{s}" for s in ("squared", "summed", "logged", "rooted", "scaled", "hi_ready", "full_ready", "lo_ready")))

    class Parts:
        def scalar(self, act, tile_there):
            nc.scalar.preload_act_table_set("natural_log_exp_and_others")
            for t in range(KT):
                tile_there(t)
                if t >= 2:
                    act.wait_ge(summed, t - 1)
                nc.scalar.activation(sq[:, t % 2], xT[:, t, :], ACT.Square).then_inc(squared, 1)
            act.wait_ge(summed, KT)
            nc.scalar.activation(rinv[:, :], ps[:, :, :].rearrange("p h c -> p (h c)"), ACT.Ln, scale=1.0 / D, bias=k.eps[:, 0:1]).then_inc(logged, 1)
            act.wait_ge(logged, 1)
            nc.scalar.activation(rinv[:, :], rinv[:, :], ACT.Exp, scale=-0.5).then_inc(rooted, 1)
            for t in range(KT):
                act.wait_ge(scaled, t + 1)
                nc.scalar.activation(h_hi[:, t, :], xn[:, t % 2], ACT.Identity, scale=scale[:, t:t + 1], bias=shift[:, t:t + 1]).then_inc(hi_ready, 1)

        def tensor(self, pe, t0=0, t1=KT):
            for t in range(t0, t1):
                pe.wait_ge(squared, t + 1)
                for h in range(NH):
                    last = nc.tensor.matmul(ps[:, h, :], k.ones[:, :], sq[:, t % 2, h * HALF:(h + 1) * HALF], start=(t == 0), stop=(t == KT - 1))
                last.then_inc(summed, 1)

        def vector(self, dve):
            dve.wait_ge(rooted, 1)
            for t in range(KT):
                if t >= 2:
                    dve.wait_ge(hi_ready, t - 1)
                nc.vector.tensor_tensor(xn[:, t % 2], xT[:, t, :], rinv[:, :], ALU.mult).then_inc(scaled, 1)
                dve.wait_ge(scaled, t + 1)
                if t >= 2:
                    dve.wait_ge(lo_ready, t - 1)
                nc.vector.tensor_scalar(hf[:, t % 2], xn[:, t % 2], scale[:, t:t + 1], shift[:, t:t + 1], ALU.mult, ALU.add).then_inc(full_ready, 1)

        def gpsimd(self, pool):
            for t in range(KT):
                pool.wait_ge(full_ready, t + 1)
                pool.wait_ge(hi_ready, t + 1)
                nc.gpsimd.tensor_tensor(h_lo[:, t, :], hf[:, t % 2], h_hi[:, t, :].bitcast(F32), ALU.subtract).then_inc(lo_ready, 1)

    return Parts()


def stage_norm(nc, k, name, xT, scale, shift, h_hi, h_lo):
    with ExitStack() as ctx:
        norm = norm_parts(nc, k, ctx, name, xT, scale, shift, h_hi, h_lo)
        block = ctx.enter_context(nc.Block())
        block.scalar(lambda act: norm.scalar(act, lambda t: None))
        block.tensor(norm.tensor)
        block.vector(norm.vector)
        block.gpsimd(norm.gpsimd)


CONV_CH = 256
CONV_WIDTH = 31


def stage_project(nc, k, w_in, w_ada):
    PAD = CONV_WIDTH - 1
    C = CONV_CH // P
    CONV_PAIRS = R_CONV // 2 + C
    with ExitStack() as ctx:
        raw = ctx.enter_context(nc.sbuf_tensor("pj_raw", [P, 2, KT, P], F32))
        w_hi = ctx.enter_context(nc.sbuf_tensor("pj_w_hi", [P, 2, KT, P], F32R))
        w_lo = ctx.enter_context(nc.sbuf_tensor("pj_w_lo", [P, 2, KT, P], F32R))
        out = ctx.enter_context(nc.sbuf_tensor("pj_out", [P, 2, S], F32))
        ada = ctx.enter_context(nc.sbuf_tensor("pj_ada", [P, KT, ADA_CHUNK * P], F32))
        ada_sum = ctx.enter_context(nc.sbuf_tensor("pj_ada_sum", [P, ADA_CHUNK * P], F32))
        ps_m = ctx.enter_context(nc.psum_tensor("pj_ps_m", [P, HALF], F32))
        ada_in, ada_step, ada_done, mod_ready = sems(nc, ctx, "pj_ada_in", "pj_ada_step", "pj_ada_done", "pj_mod_ready")
        ada_view = w_ada[0].rearrange("(t p) n -> p t n", p=P)
        ps = ctx.enter_context(nc.psum_tensor("pj_ps", [P, 2, NH, HALF], F32))
        raw_in = [sems(nc, ctx, f"pj_raw_in{s}")[0] for s in range(2)]
        stored = [sems(nc, ctx, f"pj_stored{s}")[0] for s in range(2)]
        a_g = ctx.enter_context(nc.sbuf_tensor("cv_in", [P, 2 * C, S], F32))
        padded = ctx.enter_context(nc.sbuf_tensor("cv_padded", [P, C, PAD + S], F32))
        acc = ctx.enter_context(nc.sbuf_tensor("cv_acc", [P, C, S], F32))
        centred = ctx.enter_context(nc.sbuf_tensor("cv_centred", [P, C, S], F32))
        sq = ctx.enter_context(nc.sbuf_tensor("cv_sq", [P, C, S], F32))
        rinv = ctx.enter_context(nc.sbuf_tensor("cv_rinv", [P, S], F32))
        ps_stat = ctx.enter_context(nc.psum_tensor("cv_ps_stat", [P, NH, HALF], F32))
        cv_loaded, gated, padding, tapped, mean_done, var_done, centred_ready, squared, rooted, normed, scaled, swished, cv_out, cv_stored = sems(
            nc, ctx, "cv_loaded", "cv_gated", "cv_padding", "cv_tapped", "cv_mean_done", "cv_var_done", "cv_centred_ready", "cv_squared",
            "cv_rooted", "cv_normed", "cv_scaled", "cv_swished", "cv_out", "cv_stored")
        flat = "p c s -> p (c s)"
        gate = a_g[:, C:2 * C, :].rearrange(flat)
        hi_ready = sems(nc, ctx, "pj_hi_ready")[0]
        lo_ready = sems(nc, ctx, "pj_lo_ready")[0]
        multiplied = sems(nc, ctx, "pj_multiplied")[0]
        copied = sems(nc, ctx, "pj_copied")[0]
        block = ctx.enter_context(nc.Block())
        w_view = w_in[0].rearrange("(t p) n -> p t n", p=P)
        proj = k.proj

        def pairs(eng, body, after_loop=None, before_last=None):
            body(0, 0, P, first=True, mod=True)
            with eng.Fori(1, 16) as i:
                body(i, 0, P, mod=True)
            if after_loop:
                after_loop()
            body(16, 0, P)
            with eng.Fori(17, 20) as i:
                body(i, RANK, P)
            if before_last:
                before_last()
            body(20, None, RANK)

        @block.sync
        def _(sp):
            def store(i, s, width):
                sp.wait_ge(copied, i * 4 + 2 * s + 2)
                sp.dma_start(proj[bass.ds(i * (2 * P) + s * P, width), :], out[0:width, s]).then_inc(stored[s], 16)

            def body(i, skip, width, first=False, mod=False):
                if mod:
                    ada_column = sp.snap(i * (ADA_CHUNK * P) + ADA_FIRST * P)
                for s in range(2 if width == P else 1):
                    if mod and s == 0 and not first:
                        sp.wait_ge(ada_step, i * KT)
                    if not first:
                        sp.wait_ge(lo_ready, i * 2 + s - 1)
                    src = COL_LOW if skip is None else i * (2 * P) + (s * P + skip)
                    sp.dma_start(raw[:, s, :, 0:width], w_view[:, :, bass.ds(src, width)]).then_inc(raw_in[s], 16)
                    if mod and s == 0:
                        sp.dma_start(ada[:, :, :], ada_view[:, :, bass.ds(ada_column, ADA_CHUNK * P)]).then_inc(ada_in, 16)
                    if not first:
                        store(i - 1, s, P)
                        if width < P:
                            store(i - 1, 1, P)
                            store(i, 0, width)

            def load_conv():
                for s in range(2):
                    sp.wait_ge(stored[s], 16 * CONV_PAIRS)
                sp.dma_start(a_g[:, :, :], feature_tiles(proj[R_CONV * P:(R_CONV + 2 * C) * P, :])).then_inc(cv_loaded, 16)

            pairs(sp, body, after_loop=load_conv)
            sp.wait_ge(cv_out, C)
            sp.dma_start(feature_tiles(k.mix[Y_B * P:Y_C * P, :]), acc[:, :, :]).then_inc(cv_stored, 16)
            sp.wait_ge(cv_stored, 16)
            sp.wait_ge(stored[0], 16 * 21)
            sp.wait_ge(stored[1], 16 * 20)

        @block.scalar
        def _(act):
            def split(i, s, width, first=False):
                act.wait_ge(raw_in[s], i * 16 + 16)
                if not first:
                    act.wait_ge(multiplied, i * 4 + 2 * s - 2)
                nc.scalar.activation(w_hi[:, s, :, 0:width], raw[:, s, :, 0:width], ACT.Copy).then_inc(hi_ready, 1)

            def copy(i, s, width, first=False):
                if not first:
                    act.wait_ge(stored[s], i * 16)
                for h in range(NH):
                    act.wait_ge(multiplied, i * 4 + 2 * s + h + 1)
                    nc.scalar.activation(out[0:width, s, h * HALF:(h + 1) * HALF], ps[0:width, s, h, :], ACT.Copy).then_inc(copied, 1)

            def body(i, first=False):
                for s in range(2):
                    copy(i - 1, s, P, first)
                    split(i, s, P)

            split(0, 0, P, first=True)
            split(0, 1, P, first=True)
            body(1, first=True)
            with act.Fori(2, 17) as i:
                body(i)
            act.wait_ge(cv_loaded, 16)
            nc.scalar.activation(gate, gate, ACT.Sigmoid).then_inc(gated, 1)
            with act.Fori(17, 20) as i:
                body(i)
            copy(19, 0, P)
            split(20, 0, RANK)
            copy(19, 1, P)
            act.wait_ge(centred_ready, C)
            nc.scalar.activation(sq[:, :, :].rearrange(flat), centred[:, :, :].rearrange(flat), ACT.Square).then_inc(squared, 1)
            copy(20, 0, RANK)
            act.wait_ge(var_done, 1)
            nc.scalar.activation(rinv[:, :], ps_stat[:, :, :].rearrange("p h c -> p (h c)"), ACT.Ln, scale=1.0 / CONV_CH,
                                 bias=k.eps[:, 0:1]).then_inc(rooted, 1)
            act.wait_ge(rooted, 1)
            nc.scalar.activation(rinv[:, :], rinv[:, :], ACT.Exp, scale=-0.5).then_inc(rooted, 1)
            for c in range(C):
                act.wait_ge(scaled, c + 1)
                nc.scalar.activation(sq[:, c, :], centred[:, c, :], ACT.Sigmoid).then_inc(swished, 1)

        @block.gpsimd
        def _(pool):
            def body(i, skip, width, first=False, mod=False):
                for s in range(2 if width == P else 1):
                    pool.wait_ge(hi_ready, i * 2 + s + 1)
                    nc.gpsimd.tensor_tensor(w_lo[:, s, :, 0:width], raw[:, s, :, 0:width],
                                            w_hi[:, s, :, 0:width].bitcast(F32), ALU.subtract).then_inc(lo_ready, 1)

            pairs(pool, body)

        @block.tensor
        def _(pe):
            def body(i, skip, width, first=False, mod=False):
                for s in range(2 if width == P else 1):
                    pe.wait_ge(lo_ready, i * 2 + s + 1)
                    for h in range(NH):
                        if not first:
                            pe.wait_ge(copied, i * 4 + 2 * s + h - 3)
                        split_product(nc, ps[0:width, s, h, :], w_hi[:, s, :, 0:width], w_lo[:, s, :, 0:width],
                                      k.h_hi[:, :, h * HALF:(h + 1) * HALF], k.h_lo[:, :, h * HALF:(h + 1) * HALF]).then_inc(multiplied, 1)
                if mod:
                    pe.wait_ge(ada_step, i * KT + KT)
                    if not first:
                        pe.wait_ge(mod_ready, i)
                    for m in range(ADA_CHUNK):
                        last = nc.tensor.matmul(ps_m[:, m:m + 1], ada_sum[:, m * P:(m + 1) * P], k.ones[:, 0:1], start=True, stop=True)
                    last.then_inc(ada_done, 1)

            def statistic(values, done):
                for c in range(C):
                    for h in range(NH):
                        last = nc.tensor.matmul(ps_stat[:, h, :], k.ones[:, :], values[:, c, h * HALF:(h + 1) * HALF], start=(c == 0), stop=(c == C - 1))
                last.then_inc(done, 1)

            def mean():
                pe.wait_ge(tapped, C * CONV_WIDTH)
                statistic(acc, mean_done)

            pairs(pe, body, before_last=mean)
            pe.wait_ge(squared, 1)
            statistic(sq, var_done)

        @block.vector
        def _(dve):
            def modulation(i, first=False):
                dve.wait_ge(ada_in, i * 16 + 16)
                if not first:
                    dve.wait_ge(ada_done, i)
                for kt in range(KT):
                    ck = k.cols[:, V_C + kt:V_C + kt + 1]
                    if kt == 0:
                        ins = nc.vector.tensor_scalar(ada_sum[:, :], ada[:, kt], ck, None, ALU.mult)
                    else:
                        dve.wait_ge(ada_step, i * KT + kt)
                        ins = nc.vector.scalar_tensor_tensor(out=ada_sum[:, :], in0=ada[:, kt], scalar=ck, in1=ada_sum[:, :],
                                                             op0=ALU.mult, op1=ALU.add)
                    ins.then_inc(ada_step, 1)
                dve.wait_ge(ada_done, i + 1)
                nc.vector.tensor_tensor(k.mod[:, bass.ds(i * ADA_CHUNK + ADA_FIRST, ADA_CHUNK)], ps_m[:, 0:ADA_CHUNK],
                                        k.cols[:, bass.ds(i * ADA_CHUNK + (V_BADA + ADA_FIRST), ADA_CHUNK)], ALU.add).then_inc(mod_ready, 1)

            modulation(0, first=True)
            with dve.Fori(1, 16) as i:
                modulation(i)

            nc.vector.memset(padded[:, :, 0:PAD], 0.0).then_inc(padding, 1)
            dve.wait_ge(gated, 1)
            nc.vector.tensor_tensor(padded[:, :, PAD:PAD + S], a_g[:, 0:C, :], a_g[:, C:2 * C, :], ALU.mult).then_inc(padding, 1)
            dve.wait_ge(padding, 2)
            for j in range(CONV_WIDTH):
                for c in range(C):
                    if j == 0:
                        ins = nc.vector.tensor_scalar(acc[:, c, :], padded[:, c, 0:S], k.taps[:, c, 0:1],
                                                      k.cols[:, V_CB + c:V_CB + c + 1], ALU.mult, ALU.add)
                    else:
                        dve.wait_ge(tapped, C * (j - 1) + c + 1)
                        ins = nc.vector.scalar_tensor_tensor(out=acc[:, c, :], in0=padded[:, c, j:j + S], scalar=k.taps[:, c, j:j + 1],
                                                             in1=acc[:, c, :], op0=ALU.mult, op1=ALU.add)
                    ins.then_inc(tapped, 1)
            dve.wait_ge(mean_done, 1)
            for c in range(C):
                nc.vector.scalar_tensor_tensor(out=centred[:, c, :], in0=ps_stat[:, :, :].rearrange("p h c -> p (h c)"), scalar=-1.0 / CONV_CH,
                                               in1=acc[:, c, :], op0=ALU.mult, op1=ALU.add).then_inc(centred_ready, 1)
            dve.wait_ge(rooted, 2)
            for c in range(C):
                dve.wait_ge(centred_ready, c + 1)
                nc.vector.tensor_tensor(acc[:, c, :], centred[:, c, :], rinv[:, :], ALU.mult).then_inc(normed, 1)
            dve.wait_ge(squared, 1)
            for c in range(C):
                dve.wait_ge(normed, c + 1)
                nc.vector.tensor_scalar(centred[:, c, :], acc[:, c, :], k.cols[:, V_LNG + c:V_LNG + c + 1],
                                        k.cols[:, V_LNB + c:V_LNB + c + 1], ALU.mult, ALU.add).then_inc(scaled, 1)
            for c in range(C):
                dve.wait_ge(swished, c + 1)
                nc.vector.tensor_tensor(acc[:, c, :], centred[:, c, :], sq[:, c, :], ALU.mult).then_inc(cv_out, 1)


def split_product(nc, out, w_hi, w_lo, x_hi, x_lo, first=True, last=True):
    tiles = w_hi.shape[1]
    for t in range(tiles):
        begin, end = first and t == 0, last and t == tiles - 1
        nc.tensor.matmul(out, w_hi[:, t, :], x_hi[:, t, :], start=begin, stop=False)
        nc.tensor.matmul(out, w_hi[:, t, :], x_lo[:, t, :], start=False, stop=False)
        mm = nc.tensor.matmul(out, w_lo[:, t, :], x_hi[:, t, :], start=False, stop=end)
    return mm




def stage_split(nc, k, name, source, tiles, hi, lo):
    with ExitStack() as ctx:
        raw = ctx.enter_context(nc.sbuf_tensor(f"{name}_raw", [P, 2, S], F32))
        raw_in = sems(nc, ctx, f"{name}_raw_in0", f"{name}_raw_in1")
        hi_ready, lo_ready = sems(nc, ctx, f"{name}_hi_ready", f"{name}_lo_ready")
        block = ctx.enter_context(nc.Block())

        @block.sync
        def _(sp):
            for t in range(tiles):
                if t >= 2:
                    sp.wait_ge(lo_ready, t - 1)
                sp.dma_start(raw[:, t % 2], source[t * P:(t + 1) * P, :]).then_inc(raw_in[t % 2], 16)

        @block.scalar
        def _(act):
            for t in range(tiles):
                act.wait_ge(raw_in[t % 2], 16 * (t // 2 + 1))
                nc.scalar.activation(hi[:, t, :], raw[:, t % 2], ACT.Copy).then_inc(hi_ready, 1)

        @block.vector
        def _(dve):
            for t in range(tiles):
                dve.wait_ge(hi_ready, t + 1)
                nc.vector.tensor_tensor(lo[:, t, :], raw[:, t % 2], hi[:, t, :].bitcast(F32), ALU.subtract).then_inc(lo_ready, 1)


def stage_merge(nc, k, w_in, w_br):
    N_TILES = D // P
    with ExitStack() as ctx:
        g_raw = ctx.enter_context(nc.sbuf_tensor("mg_raw", [P, 2, KT, P], F32))
        g_hi = ctx.enter_context(nc.sbuf_tensor("mg_hi", [P, 2, KT, P], F32R))
        g_lo = ctx.enter_context(nc.sbuf_tensor("mg_lo", [P, 2, KT, P], F32R))
        b_raw = ctx.enter_context(nc.sbuf_tensor("mg_br_raw", [P, Y_TILES, P], F32))
        b_hi = ctx.enter_context(nc.sbuf_tensor("mg_br_hi", [P, Y_TILES, P], F32R))
        b_lo = ctx.enter_context(nc.sbuf_tensor("mg_br_lo", [P, Y_TILES, P], F32R))
        gate = ctx.enter_context(nc.sbuf_tensor("mg_gate", [P, 2, S], F32))
        merged = ctx.enter_context(nc.sbuf_tensor("mg_merged", [P, S], F32))
        ps_g = ctx.enter_context(nc.psum_tensor("mg_ps_g", [P, 2, NH, HALF], F32))
        ps_y = ctx.enter_context(nc.psum_tensor("mg_ps_y", [P, 2, NH, HALF], F32))
        g_in = sems(nc, ctx, "mg_in0", "mg_in1")
        (b_in, g_hi_ready, g_lo_ready, b_hi_ready, b_lo_ready, gate_done, y_done, gate_ready, gated, added, stored) = sems(
            nc, ctx, "mg_b_in", "mg_hi_ready", "mg_lo_ready", "mg_b_hi_ready", "mg_b_lo_ready", "mg_gate_done", "mg_y_done",
            "mg_gate_ready", "mg_gated", "mg_added", "mg_stored")
        block = ctx.enter_context(nc.Block())
        w_view = w_in[0].rearrange("(t p) n -> p t n", p=P)

        @block.sync
        def _(sp):
            def loads(n, first=False):
                for i in range(4):
                    column = sp.snap(n * P + (COL_GATES + i * D))
                    if not (first and i < 2):
                        sp.wait_ge(g_lo_ready, n * 4 + i - 1)
                    if i == 0 and not first:
                        sp.wait_ge(b_lo_ready, n)
                    sp.dma_start(g_raw[:, i % 2], w_view[:, :, bass.ds(column, P)]).then_inc(g_in[i % 2], 16)
                    if i == 0:
                        for j in range(4):
                            sp.dma_start(b_raw[:, Y_FIRST[j]:Y_FIRST[j + 1], :],
                                         w_br[j][0].rearrange("(t p) n -> p t n", p=P)[:, :, bass.ds(n * P, P)]).then_inc(b_in, 16)
                    if i == 1 and not first:
                        store(n - 1)

            def store(n):
                sp.wait_ge(added, n * 3 + 3)
                sp.dma_start(k.merged[bass.ds(n * P, P), :], merged[:, :]).then_inc(stored, 16)

            loads(0, first=True)
            with sp.Fori(1, N_TILES) as n:
                loads(n)
            store(N_TILES - 1)
            sp.wait_ge(stored, 16 * N_TILES)

        @block.scalar
        def _(act):
            def split_gate(n, i, first=False):
                act.wait_ge(g_in[i % 2], n * 32 + (16 * (i // 2) + 16))
                if not first:
                    act.wait_ge(gate_done, n * 4 + i - 1)
                nc.scalar.activation(g_hi[:, i % 2], g_raw[:, i % 2], ACT.Copy).then_inc(g_hi_ready, 1)

            def split_branch(n, first=False):
                act.wait_ge(b_in, n * 64 + 64)
                if not first:
                    act.wait_ge(y_done, n * 4)
                nc.scalar.activation(b_hi[:, :, :], b_raw[:, :, :], ACT.Copy).then_inc(b_hi_ready, 1)

            def squash(n, i, first=False):
                act.wait_ge(gate_done, n * 4 + i + 1)
                if i == 2:
                    act.wait_ge(gated, n * 4 + 1)
                elif not first:
                    act.wait_ge(added, n * 3 + (i - 1 if i < 2 else 1))
                nc.scalar.activation(gate[:, i % 2], ps_g[:, i % 2, :, :].rearrange("p h c -> p (h c)"), ACT.Sigmoid).then_inc(gate_ready, 1)

            def body(n, first=False, last=False):
                for i in range(4):
                    squash(n, i, first and i < 2)
                    if i < 2:
                        split_gate(n, i + 2)
                    elif not last:
                        split_gate(n + 1, i - 2)
                if not last:
                    split_branch(n + 1)

            split_gate(0, 0, True)
            split_gate(0, 1, True)
            split_branch(0, True)
            body(0, first=True)
            with act.Fori(1, N_TILES - 1) as n:
                body(n)
            body(N_TILES - 1, last=True)

        @block.gpsimd
        def _(pool):
            def lows(n, last=False):
                for i in range(4):
                    if i < 2:
                        pool.wait_ge(g_hi_ready, n * 4 + i + 3)
                        low(i)
                    elif not last:
                        pool.wait_ge(g_hi_ready, n * 4 + i + 3)
                        low(i)
                if not last:
                    pool.wait_ge(b_hi_ready, n + 2)
                    low_branch()

            def low(i):
                nc.gpsimd.tensor_tensor(g_lo[:, i % 2], g_raw[:, i % 2], g_hi[:, i % 2].bitcast(F32), ALU.subtract).then_inc(g_lo_ready, 1)

            def low_branch():
                nc.gpsimd.tensor_tensor(b_lo[:, :, :], b_raw[:, :, :], b_hi[:, :, :].bitcast(F32), ALU.subtract).then_inc(b_lo_ready, 1)

            for i in range(2):
                pool.wait_ge(g_hi_ready, i + 1)
                low(i)
            pool.wait_ge(b_hi_ready, 1)
            low_branch()
            lows(0)
            with pool.Fori(1, N_TILES - 1) as n:
                lows(n)
            lows(N_TILES - 1, last=True)

        @block.tensor
        def _(pe):
            def body(n, first=False):
                for i in range(4):
                    pe.wait_ge(g_lo_ready, n * 4 + i + 1)
                    if not (first and i < 2):
                        pe.wait_ge(gate_ready, n * 4 + i - 1)
                    for h in range(NH):
                        last = split_product(nc, ps_g[:, i % 2, h, :], g_hi[:, i % 2], g_lo[:, i % 2],
                                             k.h_hi[:, :, h * HALF:(h + 1) * HALF], k.h_lo[:, :, h * HALF:(h + 1) * HALF])
                    last.then_inc(gate_done, 1)
                    if i == 0:
                        pe.wait_ge(b_lo_ready, n + 1)
                    if not (first and i < 2):
                        pe.wait_ge(gated, n * 4 + i - 1)
                    t0, t1 = Y_FIRST[i], Y_FIRST[i + 1]
                    for h in range(NH):
                        last = split_product(nc, ps_y[:, i % 2, h, :], b_hi[:, t0:t1, :], b_lo[:, t0:t1, :],
                                             k.y_hi[:, t0:t1, h * HALF:(h + 1) * HALF], k.y_lo[:, t0:t1, h * HALF:(h + 1) * HALF])
                    last.then_inc(y_done, 1)

            body(0, first=True)
            with pe.Fori(1, N_TILES) as n:
                body(n)

        @block.vector
        def _(dve):
            def body(n, first=False):
                for i in range(4):
                    dve.wait_ge(gate_ready, n * 4 + i + 1)
                    dve.wait_ge(y_done, n * 4 + i + 1)
                    y = ps_y[:, i % 2, :, :].rearrange("p h c -> p (h c)")
                    if i == 0:
                        if not first:
                            dve.wait_ge(stored, n * 16)
                        nc.vector.tensor_tensor(merged[:, :], y, gate[:, 0], ALU.mult).then_inc(gated, 1)
                        dve.wait_ge(gated, n * 4 + 1)
                        continue
                    nc.vector.tensor_tensor(gate[:, i % 2], y, gate[:, i % 2], ALU.mult).then_inc(gated, 1)
                    dve.wait_ge(gated, n * 4 + i + 1)
                    nc.vector.tensor_tensor(merged[:, :], merged[:, :], gate[:, i % 2], ALU.add).then_inc(added, 1)
                    dve.wait_ge(added, n * 3 + i)

            body(0, first=True)
            with dve.Fori(1, N_TILES) as n:
                body(n)


def stage_out(nc, k, w_out, m_hi, m_lo, xT):
    N_TILES = D // P
    with ExitStack() as ctx:
        raw = ctx.enter_context(nc.sbuf_tensor("wo_raw", [P, 2, KT, P], F32))
        w_hi = ctx.enter_context(nc.sbuf_tensor("wo_hi", [P, 2, KT, P], F32R))
        w_lo = ctx.enter_context(nc.sbuf_tensor("wo_lo", [P, 2, KT, P], F32R))
        ps = ctx.enter_context(nc.psum_tensor("wo_ps", [P, 2, NH, HALF], F32))
        raw_in = sems(nc, ctx, "wo_in0", "wo_in1")
        x_in, hi_ready, lo_ready, multiplied, summed = sems(nc, ctx, "wo_x_in", "wo_hi_ready", "wo_lo_ready", "wo_multiplied", "wo_summed")
        block = ctx.enter_context(nc.Block())
        w_view = w_out[0].rearrange("(t p) n -> p t n", p=P)

        @block.sync
        def _(sp):
            for n in range(N_TILES):
                if n >= 2:
                    sp.wait_ge(lo_ready, n - 1)
                sp.dma_start(raw[:, n % 2], w_view[:, :, n * P:(n + 1) * P]).then_inc(raw_in[n % 2], 16)
                if n == 1:
                    sp.dma_start(xT[:, :, :], feature_tiles(k.xT_dram)).then_inc(x_in, 16)

        @block.scalar
        def _(act):
            for n in range(N_TILES):
                act.wait_ge(raw_in[n % 2], 16 * (n // 2 + 1))
                if n >= 2:
                    act.wait_ge(multiplied, n - 1)
                nc.scalar.activation(w_hi[:, n % 2], raw[:, n % 2], ACT.Copy).then_inc(hi_ready, 1)

        @block.gpsimd
        def _(pool):
            for n in range(N_TILES):
                pool.wait_ge(hi_ready, n + 1)
                nc.gpsimd.tensor_tensor(w_lo[:, n % 2], raw[:, n % 2], w_hi[:, n % 2].bitcast(F32), ALU.subtract).then_inc(lo_ready, 1)

        @block.tensor
        def _(pe):
            for n in range(N_TILES):
                pe.wait_ge(lo_ready, n + 1)
                if n >= 2:
                    pe.wait_ge(summed, n - 1)
                for h in range(NH):
                    last = split_product(nc, ps[:, n % 2, h, :], w_hi[:, n % 2], w_lo[:, n % 2],
                                         m_hi[:, :, h * HALF:(h + 1) * HALF], m_lo[:, :, h * HALF:(h + 1) * HALF])
                last.then_inc(multiplied, 1)

        @block.vector
        def _(dve):
            nc.vector.scalar_tensor_tensor(out=k.scale2[:, :], in0=k.mod[:, M_SC2:M_SC2 + KT], scalar=1.0,
                                           in1=k.cols[:, V_GMLP:V_GMLP + KT], op0=ALU.add, op1=ALU.mult)
            dve.wait_ge(x_in, 16)
            for n in range(N_TILES):
                dve.wait_ge(multiplied, n + 1)
                nc.vector.scalar_tensor_tensor(out=xT[:, n, :], in0=ps[:, n % 2, :, :].rearrange("p h c -> p (h c)"),
                                               scalar=k.mod[:, M_GT1 + n:M_GT1 + n + 1], in1=xT[:, n, :],
                                               op0=ALU.mult, op1=ALU.add).then_inc(summed, 1)


def stage_mlp(nc, k, w_up, w_down, h_hi, h_lo, xT, out):
    BF = 4
    NB = D_FF // (BF * P)
    with ExitStack() as ctx:
        raw = ctx.enter_context(nc.sbuf_tensor("ff_raw", [P, 2, KT * P], F32))
        w_hi = ctx.enter_context(nc.sbuf_tensor("ff_hi", [P, 2, KT * P], F32R))
        w_lo = ctx.enter_context(nc.sbuf_tensor("ff_lo", [P, 2, KT * P], F32R))
        u_hi = ctx.enter_context(nc.sbuf_tensor("u_hi", [P, 2, BF, S], F32R))
        u_lo = ctx.enter_context(nc.sbuf_tensor("u_lo", [P, 2, BF, S], F32R))
        relu = ctx.enter_context(nc.sbuf_tensor("ff_relu", [P, 2, S], F32))
        square = ctx.enter_context(nc.sbuf_tensor("ff_square", [P, 2, S], F32))
        ps_u = ctx.enter_context(nc.psum_tensor("ff_ps_u", [P, 2, NH, HALF], F32))
        ps_d = ctx.enter_context(nc.psum_tensor("ff_ps_d", [P, 2, NH, HALF], F32))
        raw_in = sems(nc, ctx, "ff_in0", "ff_in1")
        (hi_ready, lo_ready, up_done, down_done, relu_ready, square_ready, u_hi_ready, u_lo_ready, summed, turned) = sems(
            nc, ctx, "ff_hi_ready", "ff_lo_ready", "ff_up_done", "ff_down_done", "ff_relu_ready", "ff_square_ready",
            "ff_u_hi_ready", "ff_u_lo_ready", "ff_summed", "ff_turned")
        out_stored = sems(nc, ctx, "ff_out_stored0", "ff_out_stored1")
        rows_ready = sems(nc, ctx, "ff_rows_ready_act", "ff_rows_ready_dve")
        block = ctx.enter_context(nc.Block())
        up_view = w_up[0].rearrange("(t p) n -> p t n", p=P)
        down_view = w_down[0].rearrange("(b t p) n -> p (b t) n", p=P, t=BF)

        def slot(t, s, width):
            return t[:, s, :].rearrange("p (t n) -> p t n", n=width)

        def all_steps(eng, step):
            step(-1, True, False)
            step(0, True, True)
            with eng.Fori(0, (NB - 2) // 2) as j:
                step(j * 2 + 1, True, True, parity=1)
                step(j * 2 + 2, True, True, parity=0)
            step(NB - 1, False, True)

        def par(b, parity):
            return b % 2 if parity is None else parity

        @block.sync
        def _(sp):
            def step(b, up, down, parity=None):
                w0 = 0 if up and not down else b * 8 + 4
                r0 = 0 if up and not down else b * 64 + 32
                n_up = BF if up else 0
                row = sp.snap(b * BF) if down else None
                for f in range(n_up + (BF if down else 0)):
                    column = sp.snap(b * (BF * P) + (BF * P + f * P)) if f < n_up else None
                    if not (up and not down and f < 2):
                        sp.wait_ge(lo_ready, w0 + (f - 1))
                    if f < n_up:
                        src = up_view[:, :, bass.ds(column, P)]
                        sp.dma_start(slot(raw, f % 2, P), src).then_inc(raw_in[f % 2], 16)
                    else:
                        q = f - n_up
                        src = down_view[:, bass.ds(row, BF), q * 2 * P:(q + 1) * 2 * P]
                        sp.dma_start(slot(raw, f % 2, 2 * P), src).then_inc(raw_in[f % 2], 16)

            all_steps(sp, step)
            for t in range(KT):
                sp.wait_ge(rows_ready[0], t + 1)
                sp.wait_ge(rows_ready[1], t + 1)
                sp.dma_start(out[0, t * P:(t + 1) * P, :], relu[:, t % 2]).then_inc(out_stored[t % 2], 16)
            for turn in out_stored:
                sp.wait_ge(turn, 16 * KT // 2)

        @block.scalar
        def _(act):
            def split(s):
                nc.scalar.activation(w_hi[:, s], raw[:, s], ACT.Copy).then_inc(hi_ready, 1)

            def split_up(b, f, kind):
                s = f % 2
                if kind == "first":
                    act.wait_ge(raw_in[s], 16 * (f // 2 + 1))
                    if f >= 2:
                        act.wait_ge(up_done, f - 1)
                else:
                    act.wait_ge(raw_in[s], b * 64 + (32 + 16 * (f // 2) + 16))
                    if f >= 2:
                        act.wait_ge(up_done, b * 4 + (4 + f - 1))
                    elif kind == "second":
                        act.wait_ge(up_done, f + 3)
                    else:
                        act.wait_ge(down_done, b * 8 + (2 * f - 2))
                split(s)

            def split_down(b, q, kind=None):
                s = q % 2
                if kind == "last":
                    act.wait_ge(raw_in[s], 64 * b + 32 + 16 * (q // 2) + 16)
                    act.wait_ge(down_done, 8 * b + 2 * q - 2)
                else:
                    act.wait_ge(raw_in[s], b * 64 + (32 + 32 + 16 * (q // 2) + 16))
                    if q >= 2:
                        act.wait_ge(down_done, b * 8 + (2 * q - 2))
                    else:
                        act.wait_ge(up_done, b * 4 + (4 + q + 3))
                split(s)

            def hidden(b, f, free, slot_u, recycled):
                act.wait_ge(up_done, b * 4 + (4 + f + 1))
                if free:
                    act.wait_ge(square_ready, b * 4 + (4 + f - 1))
                nc.scalar.activation(relu[:, f % 2], ps_u[:, f % 2, :, :].rearrange("p h c -> p (h c)"), ACT.Relu).then_inc(relu_ready, 1)
                act.wait_ge(relu_ready, b * 4 + (4 + f + 1))
                if recycled:
                    act.wait_ge(down_done, b * 8)
                nc.scalar.activation(u_hi[:, slot_u, f, :], relu[:, f % 2], ACT.Square).then_inc(u_hi_ready, 1)

            def step(b, up, down, parity=None):
                peeled = parity is None
                if up and not down:
                    split_up(-1, 0, "first")
                    split_up(-1, 1, "first")
                for f in range(BF if up else 0):
                    hidden(b, f, not (peeled and b == -1 and f < 2), 1 - par(b, parity), not (peeled and b <= 0))
                    if f < 2:
                        split_up(b, f + 2, "first" if not down else "later")
                    elif down:
                        split_down(b, f - 2)
                    else:
                        split_up(0, f - 2, "second")
                for q in range(BF if down else 0):
                    if up and q < 2:
                        split_down(b, q + 2)
                    elif not up:
                        if q < 2:
                            split_down(b, q + 2, "last")
                    elif peeled or parity == 1:
                        split_up(b + 1, q - 2, "later")
                    else:
                        split_next(b, q - 2)

            def split_next(b, f):
                act.wait_ge(raw_in[f], b * 64 + (64 + 32 + 16))
                act.wait_ge(down_done, b * 8 + (8 + 2 * f - 2))
                split(f)

            all_steps(act, step)
            for t in range(KT):
                act.wait_ge(turned, 2 * t + 1)
                if t >= 2:
                    act.wait_ge(out_stored[t % 2], 16 * (t // 2))
                nc.scalar.activation(relu[:, t % 2, 0:HALF], ps_u[:, t % 2, 0, :], ACT.Copy).then_inc(rows_ready[0], 1)

        @block.gpsimd
        def _(pool):
            def low(s, count):
                pool.wait_ge(hi_ready, count)
                nc.gpsimd.tensor_tensor(w_lo[:, s], raw[:, s], w_hi[:, s].bitcast(F32), ALU.subtract).then_inc(lo_ready, 1)

            def step(b, up, down, parity=None):
                w0 = 0 if up and not down else b * 8 + 4
                if up and not down:
                    low(0, 1)
                    low(1, 2)
                n_up = BF if up else 0
                n = n_up + (BF if down else 0)
                for f in range(n):
                    if f < n_up:
                        pool.wait_ge(square_ready, b * 4 + (4 + f + 1))
                        pool.wait_ge(u_hi_ready, b * 4 + (4 + f + 1))
                        su = 1 - par(b, parity)
                        nc.gpsimd.tensor_tensor(u_lo[:, su, f, :], square[:, f % 2], u_hi[:, su, f, :].bitcast(F32),
                                                ALU.subtract).then_inc(u_lo_ready, 1)
                    if up or f < 2:
                        low(f % 2, w0 + (f + 3))

            all_steps(pool, step)

        @block.tensor
        def _(pe):
            def step(b, up, down, parity=None):
                w0 = 0 if up and not down else b * 8 + 4
                n_up = BF if up else 0
                for f in range(n_up):
                    pe.wait_ge(lo_ready, w0 + (f + 1))
                    if not (up and not down and f < 2):
                        pe.wait_ge(relu_ready, b * 4 + (4 + f - 1))
                    for h in range(NH):
                        last = split_product(nc, ps_u[:, f % 2, h, :], slot(w_hi, f % 2, P), slot(w_lo, f % 2, P),
                                             h_hi[:, :, h * HALF:(h + 1) * HALF], h_lo[:, :, h * HALF:(h + 1) * HALF])
                    last.then_inc(up_done, 1)
                if not down:
                    return
                su = par(b, parity)
                pe.wait_ge(u_lo_ready, b * 4 + 4)
                for q in range(BF):
                    pe.wait_ge(lo_ready, w0 + (n_up + q + 1))
                    hi, lo = slot(w_hi, q % 2, 2 * P), slot(w_lo, q % 2, 2 * P)
                    for m in range(2):
                        if not (parity is None and b == 0 and q == 0):
                            pe.wait_ge(summed, b * 8 + (2 * q + m - 1))
                        for h in range(NH):
                            last = split_product(nc, ps_d[:, m, h, :], hi[:, :, m * P:(m + 1) * P], lo[:, :, m * P:(m + 1) * P],
                                                 u_hi[:, su, :, h * HALF:(h + 1) * HALF], u_lo[:, su, :, h * HALF:(h + 1) * HALF])
                        last.then_inc(down_done, 1)

            all_steps(pe, step)
            pe.wait_ge(summed, 8 * NB)
            for t in range(KT):
                for g in range(2):
                    if t >= 2:
                        pe.wait_ge(rows_ready[g], t - 1)
                    bank = (ps_u if g == 0 else ps_d)[:, t % 2, 0, :]
                    for a in range(4):
                        last = nc.tensor.transpose(bank[:, a * P:(a + 1) * P], xT[:, 4 * g + a, t * P:(t + 1) * P], k.ident[:, :])
                    last.then_inc(turned, 1)

        @block.vector
        def _(dve):
            def step(b, up, down, parity=None):
                for f in range(BF if up else 0):
                    dve.wait_ge(relu_ready, b * 4 + (4 + f + 1))
                    if not (up and not down and f < 2):
                        dve.wait_ge(u_lo_ready, b * 4 + (4 + f - 1))
                    nc.vector.tensor_tensor(square[:, f % 2], relu[:, f % 2], relu[:, f % 2], ALU.mult).then_inc(square_ready, 1)
                for n in range(KT if down else 0):
                    dve.wait_ge(down_done, b * 8 + (n + 1))
                    if not (parity is None and b == 0):
                        dve.wait_ge(summed, b * 8 + (n - 7))
                    nc.vector.scalar_tensor_tensor(out=xT[:, n, :], in0=ps_d[:, n % 2, :, :].rearrange("p h c -> p (h c)"),
                                                   scalar=k.mod[:, M_GT2 + n:M_GT2 + n + 1], in1=xT[:, n, :],
                                                   op0=ALU.mult, op1=ALU.add).then_inc(summed, 1)

            all_steps(dve, step)
            for t in range(KT):
                dve.wait_ge(turned, 2 * t + 2)
                if t >= 2:
                    dve.wait_ge(out_stored[t % 2], 16 * (t // 2))
                nc.vector.tensor_copy(relu[:, t % 2, HALF:D], ps_d[:, t % 2, 0, :]).then_inc(rows_ready[1], 1)


UNIT_STEP = (1, 4, 8)
A_HEADS = 4
E = 64
MASKED = -1e30
ROW = A_HEADS * E + 2 * A_HEADS


def query_tokens(ap, g, u):
    if g == 0:
        return ap[..., u * P:(u + 1) * P]
    if g == 1:
        r, b = u // 2, u % 2
        return ap[..., bass.ds(r + 4 * P * b, P, step=4)]
    return ap[..., bass.ds(u, P, step=8)]


def key_tokens(ap, g, u):
    if key_tiles(g, u) == 1:
        return query_tokens(ap, g, u)
    if g == 0:
        return ap[..., (u - 1) * P:(u + 1) * P]
    return ap[..., bass.ds(u // 2, 2 * P, step=4)]


def head_slot(h):
    return 2 * (h % 2) + h // 2


def key_tiles(g, u):
    return 2 if (g == 0 and u > 0) or (g == 1 and u % 2 == 1) else 1


def stage_window(nc, k):
    UNITS = [(g, u) for g in range(3) for u in range(8)]
    slopes = [2.0 ** (-8.0 * (i + 1) / 12) for i in range(12)]
    with ExitStack() as outer:
        qk = outer.enter_context(nc.sbuf_tensor("wa_qk", [P, 2 * A_TILES, S], F32))
        v_tok = outer.enter_context(nc.sbuf_tensor("wa_v_tok", [P, len(UNITS), A_HEADS * E], F32))
        bias = outer.enter_context(nc.sbuf_tensor("wa_bias", [P, 12, 2 * P], F32))
        with ExitStack() as ctx:
            vT = ctx.enter_context(nc.sbuf_tensor("wa_vT", [P, A_TILES, S], F32))
            sq = ctx.enter_context(nc.sbuf_tensor("wa_sq", [P, 2, S], F32))
            rinv = ctx.enter_context(nc.sbuf_tensor("wa_rinv", [P, 2, S], F32))
            rel = ctx.enter_context(nc.sbuf_tensor("wa_rel", [P, 2 * P], F32))
            odd = ctx.enter_context(nc.sbuf_tensor("wa_odd", [P, 2 * P], I32))
            other = ctx.enter_context(nc.sbuf_tensor("wa_other", [P, 2 * P], F32))
            odd_step, = sems(nc, ctx, "wa_odd_step")
            ps_n = ctx.enter_context(nc.psum_tensor("wa_ps_n", [P, 2, NH, HALF], F32))
            ps_v = ctx.enter_context(nc.psum_tensor("wa_ps_v", [P, 2, HALF], F32))
            q_in, k_in, v_in, squared, summed, logged, rooted, normed, turned, v_copied, rel_ready, bias_scaled, bias_cut = sems(
                nc, ctx, "wa_q_in", "wa_k_in", "wa_v_in", "wa_squared", "wa_summed", "wa_logged", "wa_rooted", "wa_normed",
                "wa_turned", "wa_v_copied", "wa_rel_ready", "wa_bias_scaled", "wa_bias_cut")
            block = ctx.enter_context(nc.Block())

            @block.sync
            def _(sp):
                for tiles, row, sem in ((qk[:, 0:A_TILES, :], R_AQ, q_in), (qk[:, A_TILES:2 * A_TILES, :], R_AK, k_in), (vT[:, :, :], R_AV, v_in)):
                    sp.dma_start(tiles, feature_tiles(k.proj[row * P:(row + A_TILES) * P, :])).then_inc(sem, 16)

            @block.scalar
            def _(act):
                nc.scalar.preload_act_table_set("natural_log_exp_and_others")

                def square(t):
                    act.wait_ge(q_in if t < A_TILES else k_in, 16)
                    if t >= 2:
                        act.wait_ge(summed, t - 1)
                    nc.scalar.activation(sq[:, t % 2], qk[:, t, :], ACT.Square).then_inc(squared, 1)

                square(0)
                for t in range(2 * A_TILES):
                    if t + 1 < 2 * A_TILES:
                        square(t + 1)
                    act.wait_ge(summed, t + 1)
                    if t >= 2:
                        act.wait_ge(normed, t - 1)
                    nc.scalar.activation(rinv[:, t % 2], ps_n[:, t % 2, :, :].rearrange("p h c -> p (h c)"), ACT.Ln,
                                         scale=1.0 / E, bias=k.eps[:, 0:1]).then_inc(logged, 1)
                    act.wait_ge(logged, t + 1)
                    nc.scalar.activation(rinv[:, t % 2], rinv[:, t % 2], ACT.Exp, scale=-0.5).then_inc(rooted, 1)

            @block.tensor
            def _(pe):
                for t in range(2 * A_TILES):
                    pe.wait_ge(squared, t + 1)
                    if t >= 2:
                        pe.wait_ge(logged, t - 1)
                    for h in range(NH):
                        last = nc.tensor.matmul(ps_n[:, t % 2, h, :], k.headsum[:, :], sq[:, t % 2, h * HALF:(h + 1) * HALF], start=True, stop=True)
                    last.then_inc(summed, 1)
                pe.wait_ge(v_in, 16)
                for n in range(len(UNITS) // 2):
                    if n >= 2:
                        pe.wait_ge(v_copied, n - 1)
                    for a in range(2):
                        g, u = UNITS[2 * n + a]
                        for c in range(2):
                            last = nc.tensor.transpose(ps_v[:, n % 2, (2 * a + c) * P:(2 * a + c + 1) * P],
                                                       query_tokens(vT[:, 2 * g + c, :], g, u), k.ident[:, :])
                    last.then_inc(turned, 1)

            @block.vector
            def _(dve):
                dve.wait_ge(rel_ready, 2)
                nc.vector.tensor_scalar(odd[:, :], odd[:, :], 1, None, ALU.bitwise_and).then_inc(odd_step, 1)
                dve.wait_ge(odd_step, 1)
                nc.vector.tensor_scalar(other[:, :], odd[:, :], MASKED, None, ALU.mult).then_inc(odd_step, 1)
                dve.wait_ge(odd_step, 2)
                for i in range(12):
                    at = 4 * (i // 4) + head_slot(i % 4)
                    slope = -slopes[i] * UNIT_STEP[i // 4] * E ** 0.5
                    if i < 8:
                        ins = nc.vector.tensor_scalar(bias[:, at, :], rel[:, :], slope, None, ALU.mult)
                    else:
                        ins = nc.vector.scalar_tensor_tensor(out=bias[:, at, :], in0=rel[:, :], scalar=slope, in1=other[:, :],
                                                             op0=ALU.mult, op1=ALU.add)
                    ins.then_inc(bias_scaled, 1)
                for t in range(2 * A_TILES):
                    dve.wait_ge(rooted, t + 1)
                    gain = k.cols[:, (V_QG if t < A_TILES else V_KG):(V_QG if t < A_TILES else V_KG) + 1]
                    nc.vector.scalar_tensor_tensor(out=qk[:, t, :], in0=qk[:, t, :], scalar=gain, in1=rinv[:, t % 2],
                                                   op0=ALU.mult, op1=ALU.mult).then_inc(normed, 1)
                for n in range(len(UNITS) // 2):
                    dve.wait_ge(turned, n + 1)
                    nc.vector.tensor_copy(v_tok[:, 2 * n:2 * n + 2, :].rearrange("p u e -> p (u e)"), ps_v[:, n % 2, :]).then_inc(v_copied, 1)

            @block.gpsimd
            def _(pool):
                nc.gpsimd.iota(rel[:, :], pattern=[[-1, 2 * P]], base=P, channel_multiplier=1,
                               allow_small_or_imprecise_dtypes=True).then_inc(rel_ready, 1)
                nc.gpsimd.iota(odd[:, :], pattern=[[1, 2 * P]], base=0, channel_multiplier=1).then_inc(rel_ready, 1)
                pool.wait_ge(bias_scaled, 12)
                nc.gpsimd.affine_select(out=bias[:, :, :], in_=bias[:, :, :], compare_op=ALU.is_ge, fill=MASKED, base=P,
                                        pattern=[[0, 12], [-1, 2 * P]], channel_multiplier=1).then_inc(bias_cut, 1)
                pool.wait_ge(bias_cut, 1)
                nc.gpsimd.affine_select(out=bias[:, :, :], in_=bias[:, :, :], compare_op=ALU.is_ge, fill=MASKED, base=0,
                                        pattern=[[0, 12], [1, 2 * P]], channel_multiplier=-1).then_inc(bias_cut, 2)

        with ExitStack() as ctx:
            prob = ctx.enter_context(nc.sbuf_tensor("wa_prob", [P, 2, A_HEADS, 2 * P], F32))
            probT = ctx.enter_context(nc.sbuf_tensor("wa_probT", [P, 2, A_HEADS * 2, P], F32))
            row = ctx.enter_context(nc.sbuf_tensor("wa_row", [P, 4, ROW], F32))
            negmax = ctx.enter_context(nc.sbuf_tensor("wa_negmax", [P, 2, A_HEADS], F32))
            ps_s = ctx.enter_context(nc.psum_tensor("wa_ps_s", [P, 2, A_HEADS, 2 * P], F32))
            ps_t = ctx.enter_context(nc.psum_tensor("wa_ps_t", [P, A_HEADS * 2, P], F32))
            ps_o = ctx.enter_context(nc.psum_tensor("wa_ps_o", [P, 2, HALF], F32))
            scored, biased, max_ready, negmax_ready, exped, p_turned, p_copied, o_done, o_copied = sems(
                nc, ctx, "wa_scored", "wa_biased", "wa_max_ready", "wa_negmax_ready", "wa_exped", "wa_p_turned", "wa_p_copied",
                "wa_o_done", "wa_o_copied")
            stored = sems(nc, ctx, *(f"wa_stored{i}" for i in range(4)))
            block = ctx.enter_context(nc.Block())
            N = len(UNITS)

            def span(n):
                return slice(2 * P - P * key_tiles(*UNITS[n]), 2 * P)

            @block.tensor
            def _(pe):
                def scores(n):
                    g, u = UNITS[n]
                    if n >= 2:
                        pe.wait_ge(biased, n - 1)
                    for h in range(A_HEADS):
                        rows = slice(E * (h % 2), E * (h % 2) + E)
                        last = nc.tensor.matmul(ps_s[:, n % 2, head_slot(h), span(n)], query_tokens(qk[rows, 2 * g + h // 2, :], g, u),
                                                key_tokens(qk[rows, A_TILES + 2 * g + h // 2, :], g, u), start=True, stop=True)
                    last.then_inc(scored, 1)

                def turn(n):
                    kt = key_tiles(*UNITS[n])
                    pe.wait_ge(exped, A_HEADS * (n + 1))
                    if n >= 1:
                        pe.wait_ge(p_copied, n)
                    for h in range(A_HEADS):
                        for j in range(kt):
                            last = nc.tensor.transpose(ps_t[:, h * kt + j, :], prob[:, n % 2, head_slot(h), (2 - kt + j) * P:(3 - kt + j) * P], k.ident[:, :])
                    last.then_inc(p_turned, 1)

                def values(n):
                    kt = key_tiles(*UNITS[n])
                    pe.wait_ge(p_copied, n + 1)
                    if n >= 2:
                        pe.wait_ge(o_copied, n - 1)
                    for h in range(A_HEADS):
                        for j in range(kt):
                            last = nc.tensor.matmul(ps_o[:, n % 2, h * E:(h + 1) * E], probT[:, n % 2, h * kt + j, :],
                                                    v_tok[:, n - kt + 1 + j, h * E:(h + 1) * E], start=(j == 0), stop=(j == kt - 1))
                    last.then_inc(o_done, 1)

                for n in range(N + 2):
                    if n < N:
                        scores(n)
                    if 1 <= n <= N:
                        turn(n - 1)
                    if n >= 2:
                        values(n - 2)

            @block.vector
            def _(dve):
                for n in range(N + 2):
                    if n < N:
                        g, u = UNITS[n]
                        dve.wait_ge(scored, n + 1)
                        if n >= 2:
                            dve.wait_ge(p_turned, n - 1)
                        if n >= 4:
                            dve.wait_ge(stored[n % 4], 16 * (n // 4))
                        nc.vector.tensor_tensor(prob[:, n % 2, :, span(n)], ps_s[:, n % 2, :, span(n)],
                                                bias[:, 4 * g:4 * g + 4, span(n)], ALU.add).then_inc(biased, 1)
                        dve.wait_ge(biased, n + 1)
                        nc.vector.tensor_reduce(row[:, n % 4, A_HEADS * E:A_HEADS * E + A_HEADS].rearrange("p (c r) -> p r c", r=2),
                                                prob[:, n % 2, :, span(n)].rearrange("p (r c) k -> p r c k", r=2),
                                                AX.X, ALU.max).then_inc(max_ready, 1)
                        dve.wait_ge(max_ready, n + 1)
                        if n >= 2:
                            dve.wait_ge(exped, A_HEADS * (n - 1))
                        nc.vector.tensor_scalar(negmax[:, n % 2, :], row[:, n % 4, A_HEADS * E:A_HEADS * E + A_HEADS],
                                                -(E ** -0.5), None, ALU.mult).then_inc(negmax_ready, 1)
                    if n >= 2:
                        m = n - 2
                        dve.wait_ge(o_done, m + 1)
                        nc.vector.tensor_copy(row[:, m % 4, 0:A_HEADS * E], ps_o[:, m % 2, 0:A_HEADS * E]).then_inc(o_copied, 1)

            @block.scalar
            def _(act):
                for n in range(N + 1):
                    if n < N:
                        act.wait_ge(negmax_ready, n + 1)
                        for h in range(A_HEADS):
                            nc.scalar.activation(prob[:, n % 2, head_slot(h), span(n)], prob[:, n % 2, head_slot(h), span(n)], ACT.Exp,
                                                 bias=negmax[:, n % 2, h:h + 1], scale=E ** -0.5,
                                                 accum_out=row[:, n % 4, A_HEADS * E + A_HEADS + h:A_HEADS * E + A_HEADS + h + 1]).then_inc(exped, 1)
                    if n >= 1:
                        m = n - 1
                        act.wait_ge(p_turned, m + 1)
                        if m >= 2:
                            act.wait_ge(o_done, m - 1)
                        cols = A_HEADS * key_tiles(*UNITS[m])
                        nc.scalar.activation(probT[:, m % 2, 0:cols, :], ps_t[:, 0:cols, :], ACT.Copy).then_inc(p_copied, 1)

            @block.sync
            def _(sp):
                for n, (g, u) in enumerate(UNITS):
                    sp.wait_ge(o_copied, n + 1)
                    sp.wait_ge(exped, A_HEADS * (n + 1))
                    tokens = k.window[g].rearrange("(m r) c -> r m c", r=UNIT_STEP[g])
                    stream, first = ((0, u * P), (u // 2, (u % 2) * P), (u, 0))[g]
                    sp.dma_start(tokens[stream, first:first + P, :], row[:, n % 4, :]).then_inc(stored[n % 4], 16)
                for turn in stored:
                    sp.wait_ge(turn, 16 * N // 4)

    with ExitStack() as ctx:
        TT = S // P
        G = 3
        part = ctx.enter_context(nc.sbuf_tensor("wm_part", [P, TT, G, ROW], F32))
        top = ctx.enter_context(nc.sbuf_tensor("wm_top", [P, TT, A_HEADS], F32))
        below = ctx.enter_context(nc.sbuf_tensor("wm_below", [P, G, TT, A_HEADS], F32))
        weight = ctx.enter_context(nc.sbuf_tensor("wm_weight", [P, G, TT, A_HEADS], F32))
        total = ctx.enter_context(nc.sbuf_tensor("wm_total", [P, TT, A_HEADS], F32))
        yT = ctx.enter_context(nc.sbuf_tensor("wm_yT", [P, 2, S], F32))
        ps = ctx.enter_context(nc.psum_tensor("wm_ps", [P, 4, HALF], F32))
        part_in, step, exped, turned, copied, stored = sems(nc, ctx, "wm_part_in", "wm_step", "wm_exped", "wm_turned", "wm_copied", "wm_stored")
        block = ctx.enter_context(nc.Block())
        HE = A_HEADS * E

        @block.sync
        def _(sp):
            for g in range(G):
                sp.dma_start(part[:, :, g, :], k.window[g].rearrange("(t p) c -> p t c", p=P)).then_inc(part_in, 16)
            sp.wait_ge(copied, 4)
            sp.dma_start(feature_tiles(k.mix[Y_A * P:Y_B * P, :]), yT[:, :, :]).then_inc(stored, 16)
            sp.wait_ge(stored, 16)

        @block.vector
        def _(dve):
            count = [0]

            def link(ins):
                count[0] += 1
                ins.then_inc(step, 1)
                dve.wait_ge(step, count[0])

            dve.wait_ge(part_in, 16 * G)
            peak = [part[:, :, g, HE:HE + A_HEADS] for g in range(G)]
            link(nc.vector.tensor_tensor(top[:, :, :], peak[0], peak[1], ALU.max))
            link(nc.vector.tensor_tensor(top[:, :, :], top[:, :, :], peak[2], ALU.max))
            for g in range(G):
                last = nc.vector.tensor_tensor(below[:, g], peak[g], top[:, :, :], ALU.subtract)
            link(last)
            dve.wait_ge(exped, 1)
            for g in range(G):
                last = nc.vector.tensor_tensor(below[:, g], weight[:, g], part[:, :, g, HE + A_HEADS:ROW], ALU.mult)
            link(last)
            link(nc.vector.tensor_tensor(total[:, :, :], below[:, 0], below[:, 1], ALU.add))
            link(nc.vector.tensor_tensor(total[:, :, :], total[:, :, :], below[:, 2], ALU.add))
            link(nc.vector.reciprocal(total[:, :, :], total[:, :, :]))
            for g in range(G):
                last = nc.vector.tensor_tensor(weight[:, g], weight[:, g], total[:, :, :], ALU.mult)
            link(last)
            for g in range(G):
                o = part[:, :, g, 0:HE].rearrange("p t (h e) -> p t h e", e=E)
                last = nc.vector.tensor_tensor(o, o, weight[:, g].unsqueeze(3).to_broadcast([P, TT, A_HEADS, E]), ALU.mult)
            link(last)
            link(nc.vector.tensor_tensor(part[:, :, 0, 0:HE], part[:, :, 0, 0:HE], part[:, :, 1, 0:HE], ALU.add))
            link(nc.vector.tensor_tensor(part[:, :, 0, 0:HE], part[:, :, 0, 0:HE], part[:, :, 2, 0:HE], ALU.add))
            k.window_merged = count[0]
            for n in range(4):
                dve.wait_ge(turned, n + 1)
                nc.vector.tensor_copy(yT[:, n // 2, (n % 2) * HALF:(n % 2 + 1) * HALF], ps[:, n, :]).then_inc(copied, 1)

        @block.scalar
        def _(act):
            act.wait_ge(step, 3)
            nc.scalar.activation(weight[:, :, :, :].rearrange("p g t h -> p (g t h)"), below[:, :, :, :].rearrange("p g t h -> p (g t h)"),
                                 ACT.Exp, scale=E ** -0.5).then_inc(exped, 1)

        @block.tensor
        def _(pe):
            pe.wait_ge(step, k.window_merged)
            for n in range(4):
                for a in range(4):
                    last = nc.tensor.transpose(ps[:, n, a * P:(a + 1) * P], part[:, (n % 2) * 4 + a, 0, (n // 2) * P:(n // 2 + 1) * P], k.ident[:, :])
                last.then_inc(turned, 1)


GLA_HEADS = 4
GLA_TAU = 16.0
CH = P
N_CH = S // CH
LEVELS = 7


def stage_gla(nc, k, w_gate):
    with ExitStack() as outer:
        def hold(name, shape, dt=F32):
            return outer.enter_context(nc.sbuf_tensor(name, shape, dt))

        q = hold("gl_q", [P, 2, S])
        kk = hold("gl_k", [P, 2, S])
        cum = hold("gl_cum", [P, 2, S])
        q_in = hold("gl_q_decayed", [P, 2, S])
        k_tok = hold("gl_k_tok", [P, N_CH, 2 * P])
        v_tok = hold("gl_v_tok", [P, N_CH, GLA_HEADS * P])
        last_decay = hold("gl_last", [P, 2, N_CH])
        with ExitStack() as ctx:
            low = ctx.enter_context(nc.sbuf_tensor("gl_low", [RANK, S], F32))
            wg = ctx.enter_context(nc.sbuf_tensor("gl_wg", [RANK, 2 * P], F32))
            vT = ctx.enter_context(nc.sbuf_tensor("gl_vT", [P, GLA_HEADS, S], F32))
            pre = ctx.enter_context(nc.sbuf_tensor("gl_pre", [P, 2, S], F32))
            mag = ctx.enter_context(nc.sbuf_tensor("gl_mag", [P, 2, S], F32))
            carry = ctx.enter_context(nc.sbuf_tensor("gl_carry", [P, 2, N_CH, CH], F32))
            kd = ctx.enter_context(nc.sbuf_tensor("gl_kd", [P, 2, S], F32))
            ps = ctx.enter_context(nc.psum_tensor("gl_ps", [P, 2, NH, HALF], F32))
            ps_t = ctx.enter_context(nc.psum_tensor("gl_ps_t", [P, 4, HALF], F32))
            low_in, qk_in, v_in, pre_done, act_step, dve_step, carry_ready, turned, copied = sems(
                nc, ctx, "gl_low_in", "gl_qk_in", "gl_v_in", "gl_pre_done", "gl_act_step", "gl_dve_step", "gl_carry_ready", "gl_turned", "gl_copied")
            block = ctx.enter_context(nc.Block())
            flat = "p c s -> p (c s)"

            @block.sync
            def _(sp):
                sp.dma_start(low[:, :], k.proj[R_LOW * P:R_LOW * P + RANK, :]).then_inc(low_in, 16)
                sp.dma_start(wg[:, :], w_gate[0]).then_inc(low_in, 16)
                sp.dma_start(vT[:, :, :], feature_tiles(k.proj[R_CV * P:(R_CV + 4) * P, :])).then_inc(v_in, 16)
                sp.dma_start(q[:, :, :], feature_tiles(k.proj[R_CQ * P:(R_CQ + 2) * P, :])).then_inc(qk_in, 16)
                sp.dma_start(kk[:, :, :], feature_tiles(k.proj[R_CK * P:(R_CK + 2) * P, :])).then_inc(qk_in, 16)

            @block.gpsimd
            def _(pool):
                nc.gpsimd.memset(carry[:, :, :, :].rearrange("p c n t -> p (c n t)"), 1.0).then_inc(carry_ready, 1)

            @block.tensor
            def _(pe):
                pe.wait_ge(low_in, 32)
                for c in range(2):
                    for h in range(NH):
                        last = nc.tensor.matmul(ps[:, c, h, :], wg[:, c * P:(c + 1) * P], low[:, h * HALF:(h + 1) * HALF], start=True, stop=True)
                last.then_inc(pre_done, 1)
                pe.wait_ge(v_in, 16)
                for n in range(N_CH):
                    if n >= 4:
                        pe.wait_ge(copied, n - 3)
                    for h in range(GLA_HEADS):
                        last = nc.tensor.transpose(ps_t[:, n % 4, h * P:(h + 1) * P], vT[:, h, n * CH:(n + 1) * CH], k.ident[:, :])
                    last.then_inc(turned, 1)
                pe.wait_ge(dve_step, 7)
                for n in range(N_CH // 2):
                    pe.wait_ge(copied, n + 5)
                    for a in range(4):
                        last = nc.tensor.transpose(ps_t[:, n % 4, a * P:(a + 1) * P], kd[:, a % 2, (2 * n + a // 2) * CH:(2 * n + a // 2 + 1) * CH], k.ident[:, :])
                    last.then_inc(turned, 1)

            @block.scalar
            def _(act):
                count = [0]

                def link(ins):
                    count[0] += 1
                    ins.then_inc(act_step, 1)
                    act.wait_ge(act_step, count[0])

                act.wait_ge(pre_done, 1)
                for c in range(2):
                    last = nc.scalar.activation(pre[:, c, :], ps[:, c, :, :].rearrange("p h c -> p (h c)"), ACT.Identity,
                                                bias=k.cols[:, V_BG + c:V_BG + c + 1])
                link(last)
                link(nc.scalar.activation(mag[:, :, :].rearrange(flat), pre[:, :, :].rearrange(flat), ACT.Abs))
                link(nc.scalar.activation(mag[:, :, :].rearrange(flat), mag[:, :, :].rearrange(flat), ACT.Exp, scale=-1.0))
                link(nc.scalar.activation(mag[:, :, :].rearrange(flat), mag[:, :, :].rearrange(flat), ACT.Ln, bias=1.0))
                act.wait_ge(dve_step, 4)
                link(nc.scalar.activation(q_in[:, :, :].rearrange(flat), cum[:, :, :].rearrange(flat), ACT.Exp, scale=1.0 / GLA_TAU))
                link(nc.scalar.activation(kd[:, :, :].rearrange(flat), kd[:, :, :].rearrange(flat), ACT.Exp, scale=1.0 / GLA_TAU))
                nc.scalar.activation(last_decay[:, :, :], cum[:, :, :].rearrange("p c (n t) -> p c n t", t=CH)[:, :, :, CH - 1], ACT.Exp, scale=1.0 / GLA_TAU)

            @block.vector
            def _(dve):
                def step(ins, n):
                    ins.then_inc(dve_step, 1)
                    dve.wait_ge(dve_step, n)

                dve.wait_ge(carry_ready, 1)
                step(nc.vector.memset(carry[:, :, :, 0:1], 0.0), 1)
                for n in range(N_CH):
                    dve.wait_ge(turned, n + 1)
                    nc.vector.tensor_copy(v_tok[:, n, :], ps_t[:, n % 4, :]).then_inc(copied, 1)
                dve.wait_ge(act_step, 4)
                step(nc.vector.scalar_tensor_tensor(out=pre[:, :, :].rearrange(flat), in0=pre[:, :, :].rearrange(flat), scalar=0.0,
                                                    in1=mag[:, :, :].rearrange(flat), op0=ALU.min, op1=ALU.subtract), 2)
                step(nc.vector.tensor_tensor_scan(cum[:, :, :].rearrange(flat), carry[:, :, :, :].rearrange("p c n t -> p (c n t)"),
                                                  pre[:, :, :].rearrange(flat), 0.0, ALU.mult, ALU.add), 3)
                chunked = "p c (n t) -> p (c n) t"
                in_chunks = cum[:, :, :].rearrange(chunked, t=CH)
                step(nc.vector.tensor_tensor(kd[:, :, :].rearrange(chunked, t=CH),
                                             in_chunks[:, :, CH - 1:CH].to_broadcast([P, 2 * N_CH, CH]), in_chunks, ALU.subtract), 4)
                dve.wait_ge(qk_in, 32)
                step(nc.vector.tensor_scalar(q[:, :, :].rearrange(flat), q[:, :, :].rearrange(flat), E ** -0.5, None, ALU.mult), 5)
                dve.wait_ge(act_step, 5)
                step(nc.vector.tensor_tensor(q_in[:, :, :].rearrange(flat), q_in[:, :, :].rearrange(flat), q[:, :, :].rearrange(flat), ALU.mult), 6)
                dve.wait_ge(act_step, 6)
                step(nc.vector.tensor_tensor(kd[:, :, :].rearrange(flat), kd[:, :, :].rearrange(flat), kk[:, :, :].rearrange(flat), ALU.mult), 7)
                for n in range(N_CH // 2):
                    dve.wait_ge(turned, N_CH + n + 1)
                    nc.vector.tensor_copy(k_tok[:, 2 * n:2 * n + 2, :].rearrange("p n k -> p (n k)"), ps_t[:, n % 4, :]).then_inc(copied, 1)

        att = hold("gl_att", [P, N_CH // 2, 2, HALF])
        with ExitStack() as ctx:
            parts = ctx.enter_context(nc.sbuf_tensor("gl_parts", [P, 2, 2 * S], F32))
            dist = ctx.enter_context(nc.sbuf_tensor("gl_dist", [P, 2, 2 * S], F32))
            pair_xor = ctx.enter_context(nc.sbuf_tensor("gl_xor", [P, P], I32))
            s_index = ctx.enter_context(nc.sbuf_tensor("gl_s_index", [P, P], I32))
            distance = ctx.enter_context(nc.sbuf_tensor("gl_parting", [P, P], F32))
            above = ctx.enter_context(nc.sbuf_tensor("gl_above", [P, LEVELS + 2, P], F32))
            mask = ctx.enter_context(nc.sbuf_tensor("gl_mask", [P, LEVELS + 1, P], I32))
            ps = ctx.enter_context(nc.psum_tensor("gl_ps_att", [P, 4, 2, HALF], F32))
            index_ready, xor_ready, parted, masks, mask_ready, dist_ready, decayed, parts_ready, scored, taken = sems(
                nc, ctx, "gl_index_ready", "gl_xor_ready", "gl_parted", "gl_masks", "gl_mask_ready", "gl_dist_ready", "gl_decayed",
                "gl_parts_ready", "gl_scored", "gl_taken")
            block = ctx.enter_context(nc.Block())

            def halves(t, j):
                v = t.rearrange("p (n two h) -> p n two h", two=2, h=2 ** (j - 1))
                return v[:, :, 0, :], v[:, :, 1, :]

            @block.gpsimd
            def _(pool):
                nc.gpsimd.iota(pair_xor[:, :], pattern=[[1, P]], base=0, channel_multiplier=0).then_inc(index_ready, 1)
                nc.gpsimd.iota(s_index[:, :], pattern=[[0, P]], base=0, channel_multiplier=1).then_inc(index_ready, 1)
                pool.wait_ge(xor_ready, 2)
                nc.gpsimd.affine_select(out=distance[:, :], in_=distance[:, :], compare_op=ALU.is_ge, fill=-1.0, base=0,
                                        pattern=[[1, P]], channel_multiplier=-1).then_inc(parted, 1)
                for j in range(1, LEVELS + 1):
                    s = j % 2
                    if j >= 3:
                        pool.wait_ge(parts_ready, 2 * (j - 2))
                    left, right = halves(cum[:, :, :].rearrange("p c s -> p (c s)"), j)
                    d_left, d_right = halves(dist[:, s, :], j)
                    h = 2 ** (j - 1)
                    ref = left[:, :, h - 1:h].to_broadcast([P, 2 * S // (2 * h), h])
                    nc.gpsimd.tensor_tensor(d_left, ref, left, ALU.subtract).then_inc(dist_ready, 1)
                    nc.gpsimd.tensor_tensor(d_right, right, ref, ALU.subtract).then_inc(dist_ready, 1)

            @block.scalar
            def _(act):
                for j in range(1, LEVELS + 1):
                    act.wait_ge(dist_ready, 2 * j)
                    nc.scalar.activation(dist[:, j % 2, :], dist[:, j % 2, :], ACT.Exp, scale=1.0 / GLA_TAU).then_inc(decayed, 1)

            @block.tensor
            def _(pe):
                for j in range(LEVELS + 1):
                    if j >= 1:
                        pe.wait_ge(parts_ready, 2 * j)
                    for m in range(N_CH // 2):
                        n = j * (N_CH // 2) + m
                        if n >= 4:
                            pe.wait_ge(taken, n - 3)
                        for r in range(2):
                            rows = slice(E * r, E * r + E)
                            for a in range(2):
                                for c in range(2):
                                    tok = slice((2 * m + a) * CH, (2 * m + a + 1) * CH)
                                    if j == 0:
                                        keys, queries = kk[rows, c, tok], q[rows, c, tok]
                                    else:
                                        keys = queries = parts[rows, j % 2, c * S + tok.start:c * S + tok.stop]
                                    last = nc.tensor.matmul(ps[:, n % 4, r, (2 * a + c) * P:(2 * a + c + 1) * P], keys, queries, start=True, stop=True)
                            last.then_inc(scored, 1)

            @block.vector
            def _(dve):
                dve.wait_ge(index_ready, 2)
                nc.vector.tensor_tensor(pair_xor[:, :], pair_xor[:, :], s_index[:, :], ALU.bitwise_xor).then_inc(xor_ready, 1)
                dve.wait_ge(xor_ready, 1)
                nc.vector.tensor_copy(distance[:, :], pair_xor[:, :]).then_inc(xor_ready, 1)
                nc.vector.memset(att[:, :, :, :].rearrange("p m r x -> p (m r x)"), 0.0)
                dve.wait_ge(parted, 1)
                for j in range(LEVELS + 2):
                    last = nc.vector.tensor_scalar(above[:, j, :], distance[:, :], float(2 ** (j - 1)) if j else 0.0, None, ALU.is_ge)
                last.then_inc(masks, 1)
                dve.wait_ge(masks, 1)
                nc.vector.tensor_tensor(mask[:, :, :], above[:, 0:LEVELS + 1, :], above[:, 1:LEVELS + 2, :], ALU.subtract).then_inc(mask_ready, 1)
                dve.wait_ge(mask_ready, 1)

                def level_parts(j):
                    dve.wait_ge(decayed, j)
                    if j >= 3:
                        dve.wait_ge(scored, (j - 1) * N_CH)
                    q_l, q_r = halves(q[:, :, :].rearrange("p c s -> p (c s)"), j)
                    k_l, k_r = halves(kk[:, :, :].rearrange("p c s -> p (c s)"), j)
                    d_l, d_r = halves(dist[:, j % 2, :], j)
                    p_l, p_r = halves(parts[:, j % 2, :], j)
                    nc.vector.tensor_tensor(p_l, k_l, d_l, ALU.mult).then_inc(parts_ready, 1)
                    nc.vector.tensor_tensor(p_r, q_r, d_r, ALU.mult).then_inc(parts_ready, 1)

                level_parts(1)
                for j in range(LEVELS + 1):
                    if 1 <= j < LEVELS:
                        level_parts(j + 1)
                    for m in range(N_CH // 2):
                        n = j * (N_CH // 2) + m
                        dve.wait_ge(scored, 2 * n + 2)
                        if n >= 4:
                            dve.wait_ge(taken, n - 3)
                        nc.vector.copy_predicated(att[:, m].rearrange("p r (x t) -> p (r x) t", t=P),
                                                  mask[:, j:j + 1, :].to_broadcast([P, 8, P]),
                                                  ps[:, n % 4].rearrange("p r (x t) -> p (r x) t", t=P)).then_inc(taken, 1)

        with ExitStack() as late:
            oT = late.enter_context(nc.sbuf_tensor("gl_oT", [P, GLA_HEADS, S], F32))
            rT = late.enter_context(nc.sbuf_tensor("gl_rT", [P, GLA_HEADS, S], F32))
            r_in, = sems(nc, late, "gl_r_in")
            with ExitStack() as ctx:
                state = ctx.enter_context(nc.sbuf_tensor("gl_state", [P, 2, 2, P], F32))
                ps_o = ctx.enter_context(nc.psum_tensor("gl_ps_o", [P, 2, 2, HALF], F32))
                ps_u = ctx.enter_context(nc.psum_tensor("gl_ps_u", [P, 2, HALF], F32))
                update_done, state_ready, o_done, o_copied = sems(nc, ctx, "gl_update_done", "gl_state_ready", "gl_o_done", "gl_o_copied")
                block = ctx.enter_context(nc.Block())

                @block.sync
                def _(sp):
                    sp.dma_start(rT[:, :, :], feature_tiles(k.proj[R_CR * P:(R_CR + 4) * P, :])).then_inc(r_in, 16)

                @block.tensor
                def _(pe):
                    def update(n):
                        if n >= 2:
                            pe.wait_ge(state_ready, 2 * (n - 1))
                        for h in range(GLA_HEADS):
                            c, r = h // 2, h % 2
                            last = nc.tensor.matmul(ps_u[E * r:E * r + E, n % 2, c * P:(c + 1) * P],
                                                    k_tok[:, n, c * P + E * r:c * P + E * r + E], v_tok[:, n, h * P:(h + 1) * P],
                                                    start=True, stop=True)
                        last.then_inc(update_done, 1)

                    for n in range(N_CH):
                        if n < N_CH - 1:
                            update(n)
                        if n >= 2:
                            pe.wait_ge(o_copied, n - 1)
                        if n >= 1:
                            pe.wait_ge(state_ready, 2 * n)
                        for h in range(GLA_HEADS):
                            c, r = h // 2, h % 2
                            dst = ps_o[:, n % 2, r, c * P:(c + 1) * P]
                            last = nc.tensor.matmul(dst, v_tok[:, n, h * P:(h + 1) * P],
                                                    att[:, n // 2, r, (2 * (n % 2) + c) * P:(2 * (n % 2) + c + 1) * P], start=True, stop=(n == 0))
                            if n >= 1:
                                last = nc.tensor.matmul(dst, state[E * r:E * r + E, n % 2, c, :], q_in[E * r:E * r + E, c, n * CH:(n + 1) * CH],
                                                        start=False, stop=True)
                        last.then_inc(o_done, 1)

                @block.vector
                def _(dve):
                    for n in range(N_CH - 1):
                        dve.wait_ge(update_done, n + 1)
                        if n >= 1:
                            dve.wait_ge(o_done, n)
                        for c in range(2):
                            new = state[:, (n + 1) % 2, c, :]
                            if n == 0:
                                ins = nc.vector.tensor_copy(new, ps_u[:, n % 2, c * P:(c + 1) * P])
                            else:
                                dve.wait_ge(state_ready, 2 * n)
                                ins = nc.vector.scalar_tensor_tensor(out=new, in0=state[:, n % 2, c, :], scalar=last_decay[:, c, n:n + 1],
                                                                     in1=ps_u[:, n % 2, c * P:(c + 1) * P], op0=ALU.mult, op1=ALU.add)
                            ins.then_inc(state_ready, 1)

                @block.scalar
                def _(act):
                    for n in range(N_CH):
                        act.wait_ge(o_done, n + 1)
                        nc.scalar.activation(oT[:, :, n * CH:(n + 1) * CH].rearrange("p (c r) t -> p r c t", r=2),
                                             ps_o[:, n % 2, :, 0:2 * P].rearrange("p r (c t) -> p r c t", t=P), ACT.Copy).then_inc(o_copied, 1)

            with ExitStack() as ctx:
                sq = ctx.enter_context(nc.sbuf_tensor("gn_sq", [P, 2, S], F32))
                rinv = ctx.enter_context(nc.sbuf_tensor("gn_rinv", [P, 2, S], F32))
                sig = ctx.enter_context(nc.sbuf_tensor("gn_sig", [P, 2, S], F32))
                ps = ctx.enter_context(nc.psum_tensor("gn_ps", [P, 2, NH, HALF], F32))
                squared, summed, act_step, used, stored = sems(nc, ctx, "gn_squared", "gn_summed", "gn_act_step", "gn_used", "gn_stored")
                block = ctx.enter_context(nc.Block())

                @block.scalar
                def _(act):
                    count = [0]

                    def link(ins):
                        count[0] += 1
                        ins.then_inc(act_step, 1)
                        act.wait_ge(act_step, count[0])

                    act.wait_ge(r_in, 16)
                    for h in range(GLA_HEADS):
                        s = h % 2
                        if h >= 2:
                            act.wait_ge(used, 3 * (h - 1))
                            act.wait_ge(summed, h - 1)
                        nc.scalar.activation(sq[:, s], oT[:, h, :], ACT.Square).then_inc(squared, 1)
                        link(nc.scalar.activation(sig[:, s], rT[:, h, :], ACT.Exp, scale=-1.0))
                        link(nc.scalar.activation(sig[:, s], sig[:, s], ACT.Ln, bias=1.0))
                        nc.scalar.activation(sig[:, s], sig[:, s], ACT.Exp, scale=-1.0)
                        act.wait_ge(summed, h + 1)
                        link(nc.scalar.activation(rinv[:, s], ps[:, s, :, :].rearrange("p h c -> p (h c)"), ACT.Ln, scale=1.0 / P, bias=k.eps[:, 0:1]))
                        link(nc.scalar.activation(rinv[:, s], rinv[:, s], ACT.Exp, scale=-0.5))

                @block.tensor
                def _(pe):
                    for h in range(GLA_HEADS):
                        pe.wait_ge(squared, h + 1)
                        if h >= 2:
                            pe.wait_ge(act_step, 4 * (h - 1))
                        for a in range(NH):
                            last = nc.tensor.matmul(ps[:, h % 2, a, :], k.ones[:, :], sq[:, h % 2, a * HALF:(a + 1) * HALF], start=True, stop=True)
                        last.then_inc(summed, 1)

                @block.vector
                def _(dve):
                    for h in range(GLA_HEADS):
                        dve.wait_ge(act_step, 4 * (h + 1))
                        nc.vector.scalar_tensor_tensor(out=oT[:, h, :], in0=oT[:, h, :], scalar=k.cols[:, V_OG:V_OG + 1], in1=rinv[:, h % 2],
                                                       op0=ALU.mult, op1=ALU.mult).then_inc(used, 1)
                        nc.vector.tensor_tensor(sig[:, h % 2], sig[:, h % 2], rT[:, h, :], ALU.mult).then_inc(used, 1)
                        dve.wait_ge(used, 3 * h + 2)
                        nc.vector.tensor_tensor(oT[:, h, :], oT[:, h, :], sig[:, h % 2], ALU.mult).then_inc(used, 1)

                @block.sync
                def _(sp):
                    for h in range(GLA_HEADS):
                        sp.wait_ge(used, 3 * h + 3)
                        sp.dma_start(k.mix[(Y_C + h) * P:(Y_C + h + 1) * P, :], oT[:, h, :]).then_inc(stored, 16)
                    sp.wait_ge(stored, 16 * GLA_HEADS)


SB_HEADS = 4


def stage_stick(nc, k):
    with ExitStack() as outer:
        qk = outer.enter_context(nc.sbuf_tensor("sb_qk", [P, 4, S], F32))
        v_tok = outer.enter_context(nc.sbuf_tensor("sb_v_tok", [P, S // P, SB_HEADS * E], F32))
        with ExitStack() as ctx:
            vT = ctx.enter_context(nc.sbuf_tensor("sb_vT", [P, 2, S], F32))
            ps = ctx.enter_context(nc.psum_tensor("sb_ps_v", [P, 4, HALF], F32))
            loaded, q_loaded, turned, copied, scaled = sems(nc, ctx, "sb_loaded", "sb_q_loaded", "sb_turned", "sb_copied", "sb_scaled")
            block = ctx.enter_context(nc.Block())

            @block.sync
            def _(sp):
                sp.dma_start(vT[:, :, :], feature_tiles(k.proj[R_DV * P:(R_DV + 2) * P, :])).then_inc(loaded, 16)
                sp.dma_start(qk[:, :, :], feature_tiles(k.proj[R_DQ * P:(R_DQ + 4) * P, :])).then_inc(q_loaded, 16)

            @block.tensor
            def _(pe):
                pe.wait_ge(loaded, 16)
                for n in range(4):
                    for a in range(4):
                        last = nc.tensor.transpose(ps[:, n, a * P:(a + 1) * P], vT[:, a % 2, (2 * n + a // 2) * P:(2 * n + a // 2 + 1) * P], k.ident[:, :])
                    last.then_inc(turned, 1)

            @block.vector
            def _(dve):
                for n in range(4):
                    dve.wait_ge(turned, n + 1)
                    nc.vector.tensor_copy(v_tok[:, 2 * n:2 * n + 2, :].rearrange("p u e -> p (u e)"), ps[:, n, :])
                dve.wait_ge(q_loaded, 16)
                nc.vector.tensor_scalar(qk[:, 0:2, :], qk[:, 0:2, :], E ** -0.5, None, ALU.mult)

        with ExitStack() as ctx:
            STEPS = [(Q, a, r) for Q in range(NH) for a in reversed(range(4 * Q + 4)) for r in range(2)]
            N = len(STEPS)
            mag = ctx.enter_context(nc.sbuf_tensor("sb_mag", [P, 2, 2, HALF], F32))
            sp_t = ctx.enter_context(nc.sbuf_tensor("sb_softplus", [P, 2, 2, HALF], F32))
            later = ctx.enter_context(nc.sbuf_tensor("sb_later", [P, 2, 2, HALF], F32))
            w = ctx.enter_context(nc.sbuf_tensor("sb_weight", [P, 2, 2, HALF], F32))
            zs = ctx.enter_context(nc.sbuf_tensor("sb_z", [P, 2, 2, HALF], F32))
            yT = ctx.enter_context(nc.sbuf_tensor("sb_yT", [P, 2, S], F32))
            ps_z = ctx.enter_context(nc.psum_tensor("sb_ps_z", [P, 2, 2, HALF], F32))
            ps_c = ctx.enter_context(nc.psum_tensor("sb_ps_c", [P, 2, HALF], F32))
            ps_o = ctx.enter_context(nc.psum_tensor("sb_ps_o", [P, 2, HALF], F32))
            (z_done, mag_ready, exped, logged, plus_ready, cut, later_ready, cum_done, arg_ready, w_ready, w_cut, o_done, o_copied, stored,
             z_read) = sems(
                nc, ctx, "sb_z_done", "sb_mag_ready", "sb_exped", "sb_logged", "sb_plus_ready", "sb_cut", "sb_later_ready", "sb_cum_done",
                "sb_arg_ready", "sb_w_ready", "sb_w_cut", "sb_o_done", "sb_o_copied", "sb_stored", "sb_z_read")
            block = ctx.enter_context(nc.Block())

            def cols(n):
                Q, a, r = STEPS[n]
                return slice(max(0, a * P - Q * HALF), HALF)

            def diagonal(n):
                Q, a, r = STEPS[n]
                return a >= 4 * Q

            cuts = [0]
            for n in range(N):
                cuts.append(cuts[-1] + diagonal(n))
            first_of_half = [STEPS[n][1] == 4 * STEPS[n][0] + 3 for n in range(N)]

            @block.tensor
            def _(pe):
                def scores(n):
                    Q, a, r = STEPS[n]
                    if n >= 2:
                        pe.wait_ge(z_read, n - 1)
                    c = cols(n)
                    for j in range(2):
                        last = nc.tensor.matmul(ps_z[:, n % 2, j, c], qk[E * r:E * r + E, 2 + j, a * P:(a + 1) * P],
                                                qk[E * r:E * r + E, j, Q * HALF + c.start:(Q + 1) * HALF], start=True, stop=True)
                    last.then_inc(z_done, 1)

                def sums(n):
                    c = cols(n)
                    pe.wait_ge(plus_ready, n + 1)
                    if diagonal(n):
                        pe.wait_ge(cut, cuts[n + 1])
                    if n >= 1:
                        pe.wait_ge(arg_ready, n)
                    late = STEPS[n][1] < 4 * STEPS[n][0] + 3
                    if late:
                        pe.wait_ge(later_ready, n - 1)
                    held = slice(c.start + P, HALF) if diagonal(n) else c
                    for j in range(2):
                        if late:
                            nc.tensor.matmul(ps_c[:, j, held], k.ones[:, :], later[:, n % 2, j, held], start=True, stop=False,
                                             skip_group_check=True)
                        last = nc.tensor.matmul(ps_c[:, j, c], k.reach[:, :], sp_t[:, n % 2, j, c], start=not late, stop=True,
                                                skip_group_check=True)
                    last.then_inc(cum_done, 1)

                def values(n):
                    Q, a, r = STEPS[n]
                    c = cols(n)
                    pe.wait_ge(w_ready, n + 1)
                    if diagonal(n):
                        pe.wait_ge(w_cut, cuts[n + 1])
                    if first_of_half[n] and Q > 0:
                        pe.wait_ge(o_copied, 2)
                    for j in range(2):
                        last = nc.tensor.matmul(ps_o[E * j:E * j + E, r, c], v_tok[:, a, (2 * j + r) * E:(2 * j + r + 1) * E],
                                                w[:, n % 2, j, c], start=first_of_half[n], stop=(a == 0), skip_group_check=True)
                    last.then_inc(o_done, 1)

                for n in range(N + 2):
                    if n < N:
                        scores(n)
                    if 1 <= n <= N:
                        sums(n - 1)
                    if n >= 2:
                        values(n - 2)

            @block.vector
            def _(dve):
                def take_scores(n):
                    c = cols(n)
                    dve.wait_ge(z_done, n + 1)
                    if n >= 2:
                        dve.wait_ge(arg_ready, n - 1)
                        dve.wait_ge(mag_ready, n - 1)
                    nc.vector.tensor_copy(zs[:, n % 2, :, c], ps_z[:, n % 2, :, c]).then_inc(z_read, 1)

                def softplus(n):
                    c = cols(n)
                    dve.wait_ge(logged, n + 1)
                    dve.wait_ge(z_read, n + 1)
                    if n >= 2:
                        dve.wait_ge(cum_done, n - 1)
                        dve.wait_ge(later_ready, n - 1)
                    nc.vector.scalar_tensor_tensor(out=sp_t[:, n % 2, :, c], in0=zs[:, n % 2, :, c], scalar=0.0, in1=mag[:, n % 2, :, c],
                                                   op0=ALU.max, op1=ALU.add).then_inc(plus_ready, 1)

                def accumulate(n):
                    c = cols(n)
                    if diagonal(n):
                        dve.wait_ge(cut, cuts[n + 1])
                    dve.wait_ge(plus_ready, n + 1)
                    dve.wait_ge(cum_done, n + 1)
                    r = n % 2
                    if diagonal(n):
                        own = slice(c.start, c.start + P)
                        last = nc.vector.tensor_copy(later[:, r, :, own], sp_t[:, n % 2, :, own])
                        c = slice(c.start + P, HALF)
                    if c.start < HALF:
                        last = nc.vector.tensor_tensor(later[:, r, :, c], later[:, r, :, c], sp_t[:, n % 2, :, c], ALU.add)
                    last.then_inc(later_ready, 1)

                def argument(n):
                    c = cols(n)
                    dve.wait_ge(cum_done, n + 1)
                    if n >= 2:
                        dve.wait_ge(o_done, n - 1)
                    nc.vector.tensor_tensor(w[:, n % 2, :, c], zs[:, n % 2, :, c], ps_c[:, :, c], ALU.subtract).then_inc(arg_ready, 1)

                def take(Q):
                    last_step = [n for n in range(N) if STEPS[n][0] == Q][-1]
                    dve.wait_ge(o_done, last_step + 1)
                    for r in range(2):
                        nc.vector.tensor_copy(stage_o[:, r, Q * HALF:(Q + 1) * HALF], ps_o[:, r, :]).then_inc(o_copied, 1)

                stage_o = yT
                for n in range(N + 1):
                    if n < N:
                        take_scores(n)
                    if n >= 1:
                        softplus(n - 1)
                        argument(n - 1)
                        accumulate(n - 1)
                    if n == 2 * 4 + 1:
                        take(0)
                take(1)

            @block.scalar
            def _(act):
                def logs(n):
                    c = cols(n)
                    act.wait_ge(z_read, n + 1)
                    if n >= 2:
                        act.wait_ge(plus_ready, n - 1)
                    nc.scalar.activation(mag[:, n % 2, :, c], zs[:, n % 2, :, c], ACT.Abs).then_inc(mag_ready, 1)
                    act.wait_ge(mag_ready, n + 1)
                    nc.scalar.activation(mag[:, n % 2, :, c], mag[:, n % 2, :, c], ACT.Exp, scale=-1.0).then_inc(exped, 1)
                    act.wait_ge(exped, n + 1)
                    nc.scalar.activation(mag[:, n % 2, :, c], mag[:, n % 2, :, c], ACT.Ln, bias=1.0).then_inc(logged, 1)

                def weights(n):
                    c = cols(n)
                    act.wait_ge(arg_ready, n + 1)
                    nc.scalar.activation(w[:, n % 2, :, c], w[:, n % 2, :, c], ACT.Exp).then_inc(w_ready, 1)

                for n in range(N + 1):
                    if n < N:
                        logs(n)
                    if n >= 1:
                        weights(n - 1)

            @block.gpsimd
            def _(pool):
                def keep_before(tile, n):
                    c = cols(n)
                    own = tile[:, n % 2, :, c.start:c.start + P]
                    return nc.gpsimd.affine_select(out=own, in_=own, compare_op=ALU.is_gt, fill=0.0, base=0,
                                                   pattern=[[0, 2], [1, P]], channel_multiplier=-1)

                for n in range(N + 1):
                    if n < N and diagonal(n):
                        pool.wait_ge(plus_ready, n + 1)
                        keep_before(sp_t, n).then_inc(cut, 1)
                    if n >= 1 and diagonal(n - 1):
                        pool.wait_ge(w_ready, n)
                        keep_before(w, n - 1).then_inc(w_cut, 1)

            @block.sync
            def _(sp):
                sp.wait_ge(o_copied, 4)
                heads = k.mix[Y_D * P:Y_TILES * P, :].rearrange("(j r e) s -> j e r s", r=2, e=E)
                for j in range(2):
                    sp.dma_start(heads[j], yT[E * j:E * j + E, :, :]).then_inc(stored, 16)
                sp.wait_ge(stored, 32)


def stage_mixers(nc, k, a):
    stage_window(nc, k)
    stage_gla(nc, k, a["gla_w_gate"])
    stage_stick(nc, k)


def build(nc, a, out):
    k = Kernel()
    Kernel.in_use = []
    k.proj = nc.dram_tensor("proj", (PROJ_ROWS, S), F32, kind="Internal").ap()
    k.xT_dram = nc.dram_tensor("xT_dram", (D, S), F32, kind="Internal").ap()
    k.merged = nc.dram_tensor("merged", (D, S), F32, kind="Internal").ap()
    k.window = nc.dram_tensor("window", (3, S, ROW), F32, kind="Internal").ap()
    k.mix = nc.dram_tensor("mix", (Y_TILES * P, S), F32, kind="Internal").ap()
    with ExitStack() as ctx:
        def sb(name, shape, dt=F32):
            return ctx.enter_context(nc.sbuf_tensor(name, shape, dt))

        k.ident = sb("ident", [P, P])
        k.ones = sb("ones", [P, P])
        k.headsum = sb("headsum", [P, P])
        k.reach = sb("reach", [P, P])
        k.cols = sb("cols", [P, P])
        k.taps = sb("taps", [P, 2, 31])
        k.mod = sb("mod", [P, N_MOD])
        k.scale1 = sb("scale1", [P, KT])
        k.scale2 = sb("scale2", [P, KT])
        k.eps = sb("eps", [P, 1])
        with ExitStack() as front:
            k.h_hi = front.enter_context(nc.sbuf_tensor("h_hi", [P, KT, S], F32R))
            k.h_lo = front.enter_context(nc.sbuf_tensor("h_lo", [P, KT, S], F32R))
            with nc.sbuf_tensor("xT", [P, KT, S], F32) as xT:
                stage_prepare(nc, k, a["x"], a["c"], a["w_ada"], a["b_ada"], a["g_mix"], a["g_mlp"], a["conv_w"], a["conv_b"],
                              a["conv_ln_g"], a["conv_ln_b"], a["gla_b_gate"], a["gla_o_gain"], a["q_gain"], a["k_gain"], xT)
            stage_project(nc, k, a["w_in"], a["w_ada"])
            stage_mixers(nc, k, a)
            recycle_semaphores(nc)
            with nc.sbuf_tensor("y_hi", [P, Y_TILES, S], F32R) as k.y_hi, nc.sbuf_tensor("y_lo", [P, Y_TILES, S], F32R) as k.y_lo:
                stage_split(nc, k, "sy", k.mix, Y_TILES, k.y_hi, k.y_lo)
                stage_merge(nc, k, a["w_in"], [a["w_br_a"], a["w_br_b"], a["w_br_c"], a["w_br_d"]])
        x1T = sb("x1T", [P, KT, S])
        with nc.sbuf_tensor("m_hi", [P, KT, S], F32R) as m_hi, nc.sbuf_tensor("m_lo", [P, KT, S], F32R) as m_lo:
            stage_split(nc, k, "sm", k.merged, KT, m_hi, m_lo)
            stage_out(nc, k, a["w_out"], m_hi, m_lo, x1T)
        with nc.sbuf_tensor("h2_hi", [P, KT, S], F32R) as h2_hi, nc.sbuf_tensor("h2_lo", [P, KT, S], F32R) as h2_lo:
            stage_norm(nc, k, "n2", x1T, k.scale2, k.mod[:, M_SH2:M_SH2 + KT], h2_hi, h2_lo)
            stage_mlp(nc, k, a["w_up"], a["w_down"], h2_hi, h2_lo, x1T, out)


_INS = ["x", "c", "w_ada", "b_ada", "g_mix", "w_in", "q_gain", "k_gain", "conv_w", "conv_b", "conv_ln_g", "conv_ln_b",
        "gla_w_gate", "gla_b_gate", "gla_o_gain", "w_br_a", "w_br_b", "w_br_c", "w_br_d", "w_out", "g_mlp", "w_up", "w_down"]


def kernel(**inputs):
    import numpy as np
    import concourse.bacc as bacc
    from concourse.bass_utils import run_bass_kernel_spmd as run

    nc = bacc.Bacc("TRN2", target_bir_lowering=False, num_devices=1)
    arrays, aps = {}, {}
    for name in _INS:
        arrays[f"{name}_dram"] = np.ascontiguousarray(inputs[name])
        aps[name] = nc.dram_tensor(f"{name}_dram", arrays[f"{name}_dram"].shape, F32, kind="ExternalInput").ap()
    out = nc.dram_tensor("out_dram", (1, S, D), F32, kind="ExternalOutput").ap()
    build(nc, aps, out)
    r = run(nc, [arrays], core_ids=[0])
    return r.results[0]["out_dram"]
```

```python
from contextlib import ExitStack

import concourse.bass as bass
from concourse import mybir

F32 = mybir.dt.float32
F32R = mybir.dt.float32r
U8 = mybir.dt.uint8
I32 = mybir.dt.int32
ACT = mybir.ActivationFunctionType
ALU = mybir.AluOpType
AX = mybir.AxisListType

P = 128
D = 1024
S = 1024
KT = D // P
HALF = 512
NH = S // HALF
EPS = 1e-6
D_FF = 4 * D

A_TILES = 6
RANK = 16
COL_LOW = 34 * P
COL_D = COL_LOW + RANK
COL_GATES = COL_D + 6 * P
R_AQ, R_AK, R_AV, R_CONV, R_CQ, R_CK, R_CV, R_CR, R_DQ, R_DK, R_DV, R_LOW = 0, 6, 12, 18, 22, 24, 26, 30, 34, 36, 38, 40
PROJ_ROWS = 40 * P + RANK
Y_A, Y_B, Y_C, Y_D = 0, 2, 4, 8
Y_TILES = 10
Y_FIRST = [Y_A, Y_B, Y_C, Y_D, Y_TILES]

V_BADA, V_GMIX, V_GMLP, V_CB, V_LNG, V_LNB, V_BG, V_OG, V_QG, V_KG, V_C = 0, 48, 56, 64, 66, 68, 70, 72, 73, 74, 75
V_ROWS = V_C + KT
N_MOD = 48
M_SH1, M_SC1, M_GT1, M_SH2, M_SC2, M_GT2 = 0, 8, 16, 24, 32, 40


class Kernel:

    in_use = []


def sems(nc, ctx, *names):
    Kernel.in_use += [nc.alloc_semaphore(n) for n in names]
    return Kernel.in_use[-len(names):]


def recycle_semaphores(nc):
    nc.clear_and_free_semaphores(Kernel.in_use)
    Kernel.in_use = []
    nc.all_engine_barrier()


def feature_tiles(ap):
    return ap.rearrange("(t p) c -> p t c", p=P)


ADA_FIRST = 2 * KT
ADA_CHUNK = 2


def stage_prepare(nc, k, x, c, w_ada, b_ada, g_mix, g_mlp, conv_w, conv_b, ln_g, ln_b, b_gate, o_gain, q_gain, k_gain, xT, rinv):
    with ExitStack() as ctx:
        x_rows = ctx.enter_context(nc.sbuf_tensor("x_rows", [P, 2, D], F32))
        vec_rows = ctx.enter_context(nc.sbuf_tensor("vec_rows", [P, P], F32))
        convw_rows = ctx.enter_context(nc.sbuf_tensor("convw_rows", [31, 2 * P], F32))
        ada = ctx.enter_context(nc.sbuf_tensor("ada", [P, 2, KT, HALF], F32))
        ada_sum = ctx.enter_context(nc.sbuf_tensor("ada_sum", [P, 4, HALF], F32))
        ps_t = ctx.enter_context(nc.psum_tensor("ps_t", [P, 4, HALF], F32))
        ps_v = ctx.enter_context(nc.psum_tensor("ps_v", [P, HALF], F32))
        ps_m = ctx.enter_context(nc.psum_tensor("ps_m", [P, HALF], F32))
        vec_zeroed, vec_in = sems(nc, ctx, "vec_zeroed", "vec_in")
        x_in = sems(nc, ctx, "x_in0", "x_in1")
        ada_in = sems(nc, ctx, "ada_in0", "ada_in1")
        const_step, const_ready, turned, taken, vec_turned, vec_taken, ada_step, ada_done, mod_done, xt_out = sems(
            nc, ctx, "const_step", "const_ready", "turned", "taken", "vec_turned", "vec_taken", "ada_step", "ada_done", "mod_done", "xt_out")
        sq = ctx.enter_context(nc.sbuf_tensor("n1_sq", [P, 2, S], F32))
        ps_sq = ctx.enter_context(nc.psum_tensor("n1_ps_sq", [P, NH, HALF], F32))
        squared, sq_summed, logged = sems(nc, ctx, "n1_squared", "n1_sq_summed", "n1_logged")
        block = ctx.enter_context(nc.Block())
        x_view = x[0].rearrange("(t p) d -> p t d", p=P)
        ada_view = w_ada[0].rearrange("(t p) n -> p t n", p=P)
        vec = [
            (V_C, c[0].rearrange("(r p) -> r p", p=P)),
            (V_BADA, b_ada[0].rearrange("(r p) -> r p", p=P)), (V_GMIX, g_mix[0].rearrange("(r p) -> r p", p=P)),
            (V_GMLP, g_mlp[0].rearrange("(r p) -> r p", p=P)), (V_CB, conv_b[0].rearrange("(r p) -> r p", p=P)),
            (V_LNG, ln_g[0].rearrange("(r p) -> r p", p=P)), (V_LNB, ln_b[0].rearrange("(r p) -> r p", p=P)),
            (V_BG, b_gate[0].rearrange("(r p) -> r p", p=P)), (V_OG, o_gain),
        ]
        n_vec = len(vec) + 4 + 1
        N_ADA = ADA_FIRST * P // HALF

        @block.sync
        def _(sp):
            for t in range(2):
                sp.dma_start(x_rows[:, t], x_view[:, t]).then_inc(x_in[t], 16)
            sp.dma_start(ada[:, 0], ada_view[:, :, 0:HALF]).then_inc(ada_in[0], 16)
            for t in range(2, KT):
                sp.wait_ge(turned, 2 * (t - 1))
                sp.dma_start(x_rows[:, t % 2], x_view[:, t]).then_inc(x_in[t % 2], 16)
                if t == 3:
                    sp.dma_start(ada[:, 1], ada_view[:, :, HALF:2 * HALF]).then_inc(ada_in[1], 16)
            for n in range(2, N_ADA):
                sp.wait_ge(ada_step, KT * (n - 1))
                sp.dma_start(ada[:, n % 2], ada_view[:, :, n * HALF:(n + 1) * HALF]).then_inc(ada_in[n % 2], 16)
            sp.wait_ge(taken, 2 * KT)
            sp.dma_start(feature_tiles(k.xT_dram), xT[:, :, :]).then_inc(xt_out, 16)
            sp.wait_ge(xt_out, 16)

        @block.gpsimd
        def _(pool):
            nc.gpsimd.memset(k.ident[:, :], 0.0)
            nc.gpsimd.memset(k.ones[:, :], 1.0)
            nc.gpsimd.memset(k.eps[:, :], EPS)
            nc.gpsimd.memset(k.reach[:, :], 1.0).then_inc(const_step, 1)
            pool.wait_ge(const_step, 1)
            nc.gpsimd.affine_select(out=k.ident[:, :], in_=k.ident[:, :], compare_op=ALU.not_equal, fill=1.0,
                                    base=0, pattern=[[-1, P]], channel_multiplier=1).then_inc(const_ready, 1)
            nc.gpsimd.affine_select(out=k.reach[:, :], in_=k.reach[:, :], compare_op=ALU.is_ge, fill=0.0,
                                    base=0, pattern=[[-1, P]], channel_multiplier=1).then_inc(const_ready, 1)

        @block.scalar
        def _(act):
            act.wait_ge(vec_zeroed, 1)
            for row, src in vec:
                act.dma_start(vec_rows[row:row + src.shape[0], :], src).then_inc(vec_in, 16)
            for row, src in ((V_QG, q_gain), (V_KG, k_gain)):
                for h in range(2):
                    act.dma_start(vec_rows[row:row + 1, 64 * h:64 * h + 64], src).then_inc(vec_in, 16)
            act.dma_start(convw_rows[:, :], conv_w[0]).then_inc(vec_in, 16)
            for g in range(2 * KT):
                act.wait_ge(turned, g + 1)
                tt, q = g // 2, g % 2
                nc.scalar.activation(xT[:, 4 * q:4 * q + 4, tt * P:(tt + 1) * P],
                                     ps_t[:, g % 4, :].rearrange("p (a b) -> p a b", a=4), ACT.Copy).then_inc(taken, 1)
            act.wait_ge(taken, 2 * KT)
            nc.scalar.preload_act_table_set("natural_log_exp_and_others")
            for t in range(KT):
                if t >= 2:
                    act.wait_ge(sq_summed, t - 1)
                nc.scalar.activation(sq[:, t % 2], xT[:, t, :], ACT.Square).then_inc(squared, 1)
            act.wait_ge(sq_summed, KT)
            nc.scalar.activation(rinv[:, :], ps_sq[:, :, :].rearrange("p h c -> p (h c)"), ACT.Ln, scale=1.0 / D, bias=k.eps[:, 0:1]).then_inc(logged, 1)
            act.wait_ge(logged, 1)
            nc.scalar.activation(rinv[:, :], rinv[:, :], ACT.Exp, scale=-0.5)

        @block.vector
        def _(dve):
            nc.vector.memset(vec_rows[:, :], 0.0).then_inc(vec_zeroed, 1)
            for a in range(2):
                for b in range(2):
                    nc.vector.memset(k.headsum[64 * a:64 * a + 64, 64 * b:64 * b + 64], 1.0 if a == b else 0.0)
            dve.wait_ge(vec_turned, 1)
            nc.vector.tensor_copy(k.cols[:, :], ps_v[:, 0:P]).then_inc(vec_taken, 1)
            dve.wait_ge(vec_turned, 2)
            nc.vector.tensor_copy(k.taps[:, :, :], ps_v[:, P:P + 64].rearrange("p (c j) -> p c j", c=2)[:, :, 0:31]).then_inc(vec_taken, 1)
            dve.wait_ge(vec_taken, 1)
            for n in range(N_ADA):
                dve.wait_ge(ada_in[n % 2], 16 * (n // 2 + 1))
                for kt in range(KT):
                    ck = k.cols[:, V_C + kt:V_C + kt + 1]
                    if kt == 0:
                        ins = nc.vector.tensor_scalar(ada_sum[:, n], ada[:, n % 2, kt], ck, None, ALU.mult)
                    else:
                        dve.wait_ge(ada_step, KT * n + kt)
                        ins = nc.vector.scalar_tensor_tensor(out=ada_sum[:, n], in0=ada[:, n % 2, kt], scalar=ck, in1=ada_sum[:, n],
                                                             op0=ALU.mult, op1=ALU.add)
                    ins.then_inc(ada_step, 1)
            dve.wait_ge(ada_done, 1)
            nc.vector.tensor_tensor(k.mod[:, 0:ADA_FIRST], ps_m[:, 0:ADA_FIRST], k.cols[:, V_BADA:V_BADA + ADA_FIRST], ALU.add).then_inc(mod_done, 1)
            dve.wait_ge(mod_done, 1)
            nc.vector.scalar_tensor_tensor(out=k.scale1[:, :], in0=k.mod[:, M_SC1:M_SC1 + KT], scalar=1.0,
                                           in1=k.cols[:, V_GMIX:V_GMIX + KT], op0=ALU.add, op1=ALU.mult)

        @block.tensor
        def _(pe):
            pe.wait_ge(const_ready, 2)
            pe.wait_ge(vec_in, 16 * n_vec)
            nc.tensor.transpose(ps_v[:, 0:P], vec_rows[:, :], k.ident[:, :]).then_inc(vec_turned, 1)
            pe.wait_ge(vec_taken, 1)
            for c2 in range(2):
                last = nc.tensor.transpose(ps_v[:, P + 32 * c2:P + 32 * c2 + 31], convw_rows[:, c2 * P:(c2 + 1) * P], k.ident[0:31, 0:31])
            last.then_inc(vec_turned, 1)
            for g in range(2 * KT):
                if g % 2 == 0:
                    pe.wait_ge(x_in[g // 2 % 2], 16 * (g // 4 + 1))
                if g >= 4:
                    pe.wait_ge(taken, g - 3)
                for a in range(4):
                    last = nc.tensor.transpose(ps_t[:, g % 4, a * P:(a + 1) * P],
                                               x_rows[:, g // 2 % 2, (4 * (g % 2) + a) * P:(4 * (g % 2) + a + 1) * P], k.ident[:, :])
                last.then_inc(turned, 1)
            for t in range(KT):
                pe.wait_ge(squared, t + 1)
                for h in range(NH):
                    last = nc.tensor.matmul(ps_sq[:, h, :], k.ones[:, :], sq[:, t % 2, h * HALF:(h + 1) * HALF], start=(t == 0), stop=(t == KT - 1))
                last.then_inc(sq_summed, 1)
            pe.wait_ge(ada_step, KT * N_ADA)
            for m in range(ADA_FIRST):
                last = nc.tensor.matmul(ps_m[:, m:m + 1], ada_sum[:, m // 4, (m % 4) * P:(m % 4 + 1) * P], k.ones[:, 0:1], start=True, stop=True)
            last.then_inc(ada_done, 1)


def apply_norm(nc, ctx, name, xT, rinv, scale, shift, h_hi, h_lo, xn, hf):
    scaled, hi_ready, full_ready, lo_ready = sems(nc, ctx, *(f"{name}_{s}" for s in ("scaled", "hi_ready", "full_ready", "lo_ready")))

    class Parts:
        def scalar(self, act):
            for t in range(KT):
                act.wait_ge(scaled, t + 1)
                nc.scalar.activation(h_hi[:, t, :], xn[:, t % 2], ACT.Identity, scale=scale[:, t:t + 1], bias=shift[:, t:t + 1]).then_inc(hi_ready, 1)

        def vector(self, dve):
            for t in range(KT):
                if t >= 2:
                    dve.wait_ge(hi_ready, t - 1)
                nc.vector.tensor_tensor(xn[:, t % 2], xT[:, t, :], rinv[:, :], ALU.mult).then_inc(scaled, 1)
                dve.wait_ge(scaled, t + 1)
                if t >= 2:
                    dve.wait_ge(lo_ready, t - 1)
                nc.vector.tensor_scalar(hf[:, t % 2], xn[:, t % 2], scale[:, t:t + 1], shift[:, t:t + 1], ALU.mult, ALU.add).then_inc(full_ready, 1)

        def gpsimd(self, pool):
            for t in range(KT):
                pool.wait_ge(full_ready, t + 1)
                pool.wait_ge(hi_ready, t + 1)
                nc.gpsimd.tensor_tensor(h_lo[:, t, :], hf[:, t % 2], h_hi[:, t, :].bitcast(F32), ALU.subtract).then_inc(lo_ready, 1)

    parts = Parts()
    parts.lo_ready = lo_ready
    return parts


CONV_CH = 256
CONV_WIDTH = 31


def stage_project(nc, k, w_in, w_ada, xT, rinv_x):
    PAD = CONV_WIDTH - 1
    C = CONV_CH // P
    CONV_PAIRS = R_CONV // 2 + C
    with ExitStack() as ctx:
        raw = ctx.enter_context(nc.sbuf_tensor("pj_raw", [P, 2, KT, P], F32))
        w_hi = ctx.enter_context(nc.sbuf_tensor("pj_w_hi", [P, 2, KT, P], F32R))
        w_lo = ctx.enter_context(nc.sbuf_tensor("pj_w_lo", [P, 2, KT, P], F32R))
        out = ctx.enter_context(nc.sbuf_tensor("pj_out", [P, 2, S], F32))
        ada = ctx.enter_context(nc.sbuf_tensor("pj_ada", [P, KT, ADA_CHUNK * P], F32))
        ada_sum = ctx.enter_context(nc.sbuf_tensor("pj_ada_sum", [P, ADA_CHUNK * P], F32))
        ps_m = ctx.enter_context(nc.psum_tensor("pj_ps_m", [P, HALF], F32))
        ada_in, ada_step, ada_done, mod_ready = sems(nc, ctx, "pj_ada_in", "pj_ada_step", "pj_ada_done", "pj_mod_ready")
        ada_view = w_ada[0].rearrange("(t p) n -> p t n", p=P)
        ps = ctx.enter_context(nc.psum_tensor("pj_ps", [P, 2, NH, HALF], F32))
        raw_in = [sems(nc, ctx, f"pj_raw_in{s}")[0] for s in range(2)]
        stored = [sems(nc, ctx, f"pj_stored{s}")[0] for s in range(2)]
        a_g = ctx.enter_context(nc.sbuf_tensor("cv_in", [P, 2 * C, S], F32))
        padded = ctx.enter_context(nc.sbuf_tensor("cv_padded", [P, C, PAD + S], F32))
        acc = ctx.enter_context(nc.sbuf_tensor("cv_acc", [P, C, S], F32))
        centred = ctx.enter_context(nc.sbuf_tensor("cv_centred", [P, C, S], F32))
        sq = ctx.enter_context(nc.sbuf_tensor("cv_sq", [P, C, S], F32))
        rinv = ctx.enter_context(nc.sbuf_tensor("cv_rinv", [P, S], F32))
        ps_stat = ctx.enter_context(nc.psum_tensor("cv_ps_stat", [P, NH, HALF], F32))
        cv_loaded, gated, padding, tapped, mean_done, var_done, centred_ready, squared, rooted, normed, scaled, swished, cv_out, cv_stored = sems(
            nc, ctx, "cv_loaded", "cv_gated", "cv_padding", "cv_tapped", "cv_mean_done", "cv_var_done", "cv_centred_ready", "cv_squared",
            "cv_rooted", "cv_normed", "cv_scaled", "cv_swished", "cv_out", "cv_stored")
        norm = apply_norm(nc, ctx, "n1", xT, rinv_x, k.scale1, k.mod[:, M_SH1:M_SH1 + KT], k.h_hi, k.h_lo, acc, sq)
        flat = "p c s -> p (c s)"
        gate = a_g[:, C:2 * C, :].rearrange(flat)
        hi_ready = sems(nc, ctx, "pj_hi_ready")[0]
        lo_ready = sems(nc, ctx, "pj_lo_ready")[0]
        multiplied = sems(nc, ctx, "pj_multiplied")[0]
        copied = sems(nc, ctx, "pj_copied")[0]
        block = ctx.enter_context(nc.Block())
        w_view = w_in[0].rearrange("(t p) n -> p t n", p=P)
        proj = k.proj

        def pairs(eng, body, after_loop=None, before_last=None):
            body(0, 0, P, first=True, mod=True)
            with eng.Fori(1, 16) as i:
                body(i, 0, P, mod=True)
            if after_loop:
                after_loop()
            body(16, 0, P)
            with eng.Fori(17, 20) as i:
                body(i, RANK, P)
            if before_last:
                before_last()
            body(20, None, RANK)

        @block.sync
        def _(sp):
            def store(i, s, width):
                sp.wait_ge(copied, i * 4 + 2 * s + 2)
                sp.dma_start(proj[bass.ds(i * (2 * P) + s * P, width), :], out[0:width, s]).then_inc(stored[s], 16)

            def body(i, skip, width, first=False, mod=False):
                if mod:
                    ada_column = sp.snap(i * (ADA_CHUNK * P) + ADA_FIRST * P)
                for s in range(2 if width == P else 1):
                    if mod and s == 0 and not first:
                        sp.wait_ge(ada_step, i * KT)
                    if not first:
                        sp.wait_ge(lo_ready, i * 2 + s - 1)
                    src = COL_LOW if skip is None else i * (2 * P) + (s * P + skip)
                    sp.dma_start(raw[:, s, :, 0:width], w_view[:, :, bass.ds(src, width)]).then_inc(raw_in[s], 16)
                    if mod and s == 0:
                        sp.dma_start(ada[:, :, :], ada_view[:, :, bass.ds(ada_column, ADA_CHUNK * P)]).then_inc(ada_in, 16)
                    if not first:
                        store(i - 1, s, P)
                        if width < P:
                            store(i - 1, 1, P)
                            store(i, 0, width)

            def load_conv():
                for s in range(2):
                    sp.wait_ge(stored[s], 16 * CONV_PAIRS)
                sp.dma_start(a_g[:, :, :], feature_tiles(proj[R_CONV * P:(R_CONV + 2 * C) * P, :])).then_inc(cv_loaded, 16)

            pairs(sp, body, after_loop=load_conv)
            sp.wait_ge(cv_out, C)
            sp.dma_start(feature_tiles(k.mix[Y_B * P:Y_C * P, :]), acc[:, :, :]).then_inc(cv_stored, 16)
            sp.wait_ge(cv_stored, 16)
            sp.wait_ge(stored[0], 16 * 21)
            sp.wait_ge(stored[1], 16 * 20)

        @block.scalar
        def _(act):
            def split(i, s, width, first=False):
                act.wait_ge(raw_in[s], i * 16 + 16)
                if not first:
                    act.wait_ge(multiplied, i * 4 + 2 * s - 2)
                nc.scalar.activation(w_hi[:, s, :, 0:width], raw[:, s, :, 0:width], ACT.Copy).then_inc(hi_ready, 1)

            def copy(i, s, width, first=False):
                if not first:
                    act.wait_ge(stored[s], i * 16)
                for h in range(NH):
                    act.wait_ge(multiplied, i * 4 + 2 * s + h + 1)
                    nc.scalar.activation(out[0:width, s, h * HALF:(h + 1) * HALF], ps[0:width, s, h, :], ACT.Copy).then_inc(copied, 1)

            def body(i, first=False):
                for s in range(2):
                    copy(i - 1, s, P, first)
                    split(i, s, P)

            split(0, 0, P, first=True)
            split(0, 1, P, first=True)
            norm.scalar(act)
            body(1, first=True)
            with act.Fori(2, 17) as i:
                body(i)
            act.wait_ge(cv_loaded, 16)
            nc.scalar.activation(gate, gate, ACT.Sigmoid).then_inc(gated, 1)
            with act.Fori(17, 20) as i:
                body(i)
            copy(19, 0, P)
            split(20, 0, RANK)
            copy(19, 1, P)
            act.wait_ge(centred_ready, C)
            nc.scalar.activation(sq[:, :, :].rearrange(flat), centred[:, :, :].rearrange(flat), ACT.Square).then_inc(squared, 1)
            copy(20, 0, RANK)
            act.wait_ge(var_done, 1)
            nc.scalar.activation(rinv[:, :], ps_stat[:, :, :].rearrange("p h c -> p (h c)"), ACT.Ln, scale=1.0 / CONV_CH,
                                 bias=k.eps[:, 0:1]).then_inc(rooted, 1)
            act.wait_ge(rooted, 1)
            nc.scalar.activation(rinv[:, :], rinv[:, :], ACT.Exp, scale=-0.5).then_inc(rooted, 1)
            for c in range(C):
                act.wait_ge(scaled, c + 1)
                nc.scalar.activation(sq[:, c, :], centred[:, c, :], ACT.Sigmoid).then_inc(swished, 1)

        @block.gpsimd
        def _(pool):
            def body(i, skip, width, first=False, mod=False):
                for s in range(2 if width == P else 1):
                    pool.wait_ge(hi_ready, i * 2 + s + 1)
                    nc.gpsimd.tensor_tensor(w_lo[:, s, :, 0:width], raw[:, s, :, 0:width],
                                            w_hi[:, s, :, 0:width].bitcast(F32), ALU.subtract).then_inc(lo_ready, 1)
                if first:
                    norm.gpsimd(pool)

            pairs(pool, body)

        @block.tensor
        def _(pe):
            def product(s, h, width, t0=0, t1=KT):
                return split_product(nc, ps[0:width, s, h, :], w_hi[:, s, t0:t1, 0:width], w_lo[:, s, t0:t1, 0:width],
                                     k.h_hi[:, t0:t1, h * HALF:(h + 1) * HALF], k.h_lo[:, t0:t1, h * HALF:(h + 1) * HALF],
                                     first=(t0 == 0), last=(t1 == KT))

            def opening():
                for t in range(KT):
                    pe.wait_ge(norm.lo_ready, t + 1)
                    for s in range(2):
                        if t == 0:
                            pe.wait_ge(lo_ready, s + 1)
                        for h in range(NH):
                            last = product(s, h, P, t, t + 1)
                            if t == KT - 1:
                                last.then_inc(multiplied, 1)

            def body(i, skip, width, first=False, mod=False):
                if first:
                    opening()
                for s in range(0 if first else 2 if width == P else 1):
                    pe.wait_ge(lo_ready, i * 2 + s + 1)
                    for h in range(NH):
                        pe.wait_ge(copied, i * 4 + 2 * s + h - 3)
                        product(s, h, width).then_inc(multiplied, 1)
                if mod:
                    pe.wait_ge(ada_step, i * KT + KT)
                    if not first:
                        pe.wait_ge(mod_ready, i)
                    for m in range(ADA_CHUNK):
                        last = nc.tensor.matmul(ps_m[:, m:m + 1], ada_sum[:, m * P:(m + 1) * P], k.ones[:, 0:1], start=True, stop=True)
                    last.then_inc(ada_done, 1)

            def statistic(values, done):
                for c in range(C):
                    for h in range(NH):
                        last = nc.tensor.matmul(ps_stat[:, h, :], k.ones[:, :], values[:, c, h * HALF:(h + 1) * HALF], start=(c == 0), stop=(c == C - 1))
                last.then_inc(done, 1)

            def mean():
                pe.wait_ge(tapped, C * CONV_WIDTH)
                statistic(acc, mean_done)

            pairs(pe, body, before_last=mean)
            pe.wait_ge(squared, 1)
            statistic(sq, var_done)

        @block.vector
        def _(dve):
            def modulation(i, first=False):
                dve.wait_ge(ada_in, i * 16 + 16)
                if not first:
                    dve.wait_ge(ada_done, i)
                for kt in range(KT):
                    ck = k.cols[:, V_C + kt:V_C + kt + 1]
                    if kt == 0:
                        ins = nc.vector.tensor_scalar(ada_sum[:, :], ada[:, kt], ck, None, ALU.mult)
                    else:
                        dve.wait_ge(ada_step, i * KT + kt)
                        ins = nc.vector.scalar_tensor_tensor(out=ada_sum[:, :], in0=ada[:, kt], scalar=ck, in1=ada_sum[:, :],
                                                             op0=ALU.mult, op1=ALU.add)
                    ins.then_inc(ada_step, 1)
                dve.wait_ge(ada_done, i + 1)
                nc.vector.tensor_tensor(k.mod[:, bass.ds(i * ADA_CHUNK + ADA_FIRST, ADA_CHUNK)], ps_m[:, 0:ADA_CHUNK],
                                        k.cols[:, bass.ds(i * ADA_CHUNK + (V_BADA + ADA_FIRST), ADA_CHUNK)], ALU.add).then_inc(mod_ready, 1)

            norm.vector(dve)
            modulation(0, first=True)
            with dve.Fori(1, 16) as i:
                modulation(i)

            nc.vector.memset(padded[:, :, 0:PAD], 0.0).then_inc(padding, 1)
            dve.wait_ge(gated, 1)
            nc.vector.tensor_tensor(padded[:, :, PAD:PAD + S], a_g[:, 0:C, :], a_g[:, C:2 * C, :], ALU.mult).then_inc(padding, 1)
            dve.wait_ge(padding, 2)
            for j in range(CONV_WIDTH):
                for c in range(C):
                    if j == 0:
                        ins = nc.vector.tensor_scalar(acc[:, c, :], padded[:, c, 0:S], k.taps[:, c, 0:1],
                                                      k.cols[:, V_CB + c:V_CB + c + 1], ALU.mult, ALU.add)
                    else:
                        dve.wait_ge(tapped, C * (j - 1) + c + 1)
                        ins = nc.vector.scalar_tensor_tensor(out=acc[:, c, :], in0=padded[:, c, j:j + S], scalar=k.taps[:, c, j:j + 1],
                                                             in1=acc[:, c, :], op0=ALU.mult, op1=ALU.add)
                    ins.then_inc(tapped, 1)
            dve.wait_ge(mean_done, 1)
            for c in range(C):
                nc.vector.scalar_tensor_tensor(out=centred[:, c, :], in0=ps_stat[:, :, :].rearrange("p h c -> p (h c)"), scalar=-1.0 / CONV_CH,
                                               in1=acc[:, c, :], op0=ALU.mult, op1=ALU.add).then_inc(centred_ready, 1)
            dve.wait_ge(rooted, 2)
            for c in range(C):
                dve.wait_ge(centred_ready, c + 1)
                nc.vector.tensor_tensor(acc[:, c, :], centred[:, c, :], rinv[:, :], ALU.mult).then_inc(normed, 1)
            dve.wait_ge(squared, 1)
            for c in range(C):
                dve.wait_ge(normed, c + 1)
                nc.vector.tensor_scalar(centred[:, c, :], acc[:, c, :], k.cols[:, V_LNG + c:V_LNG + c + 1],
                                        k.cols[:, V_LNB + c:V_LNB + c + 1], ALU.mult, ALU.add).then_inc(scaled, 1)
            for c in range(C):
                dve.wait_ge(swished, c + 1)
                nc.vector.tensor_tensor(acc[:, c, :], centred[:, c, :], sq[:, c, :], ALU.mult).then_inc(cv_out, 1)


def split_product(nc, out, w_hi, w_lo, x_hi, x_lo, first=True, last=True):
    tiles = w_hi.shape[1]
    for t in range(tiles):
        begin, end = first and t == 0, last and t == tiles - 1
        nc.tensor.matmul(out, w_hi[:, t, :], x_hi[:, t, :], start=begin, stop=False)
        nc.tensor.matmul(out, w_hi[:, t, :], x_lo[:, t, :], start=False, stop=False)
        mm = nc.tensor.matmul(out, w_lo[:, t, :], x_hi[:, t, :], start=False, stop=end)
    return mm




class LastGates:

    def __init__(self, nc, k, ctx, name, w_in, mixers):
        self.nc, self.k, self.mixers = nc, k, mixers
        self.w_view = w_in[0].rearrange("(t p) n -> p t n", p=P)
        self.raw = ctx.enter_context(nc.sbuf_tensor(f"{name}_raw", [P, 2, KT, P], F32))
        self.hi = ctx.enter_context(nc.sbuf_tensor(f"{name}_hi", [P, 2, KT, P], F32R))
        self.lo = ctx.enter_context(nc.sbuf_tensor(f"{name}_lo", [P, 2, KT, P], F32R))
        self.out = ctx.enter_context(nc.sbuf_tensor(f"{name}_out", [P, S], F32))
        self.loaded = sems(nc, ctx, f"{name}_in0", f"{name}_in1")
        self.hi_ready, self.lo_ready, self.done, self.copied, self.stored = sems(
            nc, ctx, *(f"{name}_{s}" for s in ("hi_ready", "lo_ready", "done", "copied", "stored")))

    def load(self, sp, j):
        if j >= 2:
            sp.wait_ge(self.lo_ready, j - 1)
        column = COL_GATES + (self.mixers[j] + 1) * D - P
        sp.dma_start(self.raw[:, j % 2], self.w_view[:, :, column:column + P]).then_inc(self.loaded[j % 2], 16)

    def split(self, act, j):
        act.wait_ge(self.loaded[j % 2], 16 * (j // 2 + 1))
        if j >= 2:
            act.wait_ge(self.done, j - 1)
        self.nc.scalar.activation(self.hi[:, j % 2], self.raw[:, j % 2], ACT.Copy).then_inc(self.hi_ready, 1)

    def low(self, pool, j):
        pool.wait_ge(self.hi_ready, j + 1)
        self.nc.gpsimd.tensor_tensor(self.lo[:, j % 2], self.raw[:, j % 2], self.hi[:, j % 2].bitcast(F32), ALU.subtract).then_inc(self.lo_ready, 1)

    def product(self, pe, j, banks):
        pe.wait_ge(self.lo_ready, j + 1)
        for h in range(NH):
            last = split_product(self.nc, banks[:, h, :], self.hi[:, j % 2], self.lo[:, j % 2],
                                 self.k.h_hi[:, :, h * HALF:(h + 1) * HALF], self.k.h_lo[:, :, h * HALF:(h + 1) * HALF])
        last.then_inc(self.done, 1)

    def before_copy(self, eng, j):
        eng.wait_ge(self.done, j + 1)
        if j >= 1:
            eng.wait_ge(self.stored, 16 * j)

    def copy_by_scalar(self, act, j, banks):
        self.before_copy(act, j)
        self.nc.scalar.activation(self.out[:, :], banks[:, :, :].rearrange("p h c -> p (h c)"), ACT.Copy).then_inc(self.copied, 1)

    def copy_by_vector(self, dve, j, banks):
        self.before_copy(dve, j)
        self.nc.vector.tensor_copy(self.out[:, :], banks[:, :, :].rearrange("p h c -> p (h c)")).then_inc(self.copied, 1)

    def store(self, sp, j):
        sp.wait_ge(self.copied, j + 1)
        i = self.mixers[j]
        sp.dma_start(self.k.logits[i * P:(i + 1) * P, :], self.out[:, :]).then_inc(self.stored, 16)

    def finish(self, sp):
        sp.wait_ge(self.stored, 16 * len(self.mixers))


def stage_merge(nc, k, w_in, w_br):
    Y_EARLY = Y_TILES - 4
    N_TILES = D // P
    with ExitStack() as ctx:
        g_raw = ctx.enter_context(nc.sbuf_tensor("mg_raw", [P, 2, KT, P], F32))
        g_hi = ctx.enter_context(nc.sbuf_tensor("mg_hi", [P, 2, KT, P], F32R))
        g_lo = ctx.enter_context(nc.sbuf_tensor("mg_lo", [P, 2, KT, P], F32R))
        b_raw = ctx.enter_context(nc.sbuf_tensor("mg_br_raw", [P, Y_TILES, P], F32))
        b_hi = ctx.enter_context(nc.sbuf_tensor("mg_br_hi", [P, Y_TILES, P], F32R))
        b_lo = ctx.enter_context(nc.sbuf_tensor("mg_br_lo", [P, Y_TILES, P], F32R))
        gate = ctx.enter_context(nc.sbuf_tensor("mg_gate", [P, 2, S], F32))
        merged = ctx.enter_context(nc.sbuf_tensor("mg_merged", [P, S], F32))
        ps_g = ctx.enter_context(nc.psum_tensor("mg_ps_g", [P, 2, NH, HALF], F32))
        ps_y = ctx.enter_context(nc.psum_tensor("mg_ps_y", [P, 2, NH, HALF], F32))
        y_raw = ctx.enter_context(nc.sbuf_tensor("mg_y_raw", [P, 2, S], F32))
        y_in = sems(nc, ctx, "mg_y_in0", "mg_y_in1")
        y_hi_ready, y_lo_ready = sems(nc, ctx, "mg_y_hi_ready", "mg_y_lo_ready")
        g_in = sems(nc, ctx, "mg_in0", "mg_in1")
        (b_in, g_hi_ready, g_lo_ready, b_hi_ready, b_lo_ready, gate_done, y_done, gate_ready, gated, added, stored) = sems(
            nc, ctx, "mg_b_in", "mg_hi_ready", "mg_lo_ready", "mg_b_hi_ready", "mg_b_lo_ready", "mg_gate_done", "mg_y_done",
            "mg_gate_ready", "mg_gated", "mg_added", "mg_stored")
        block = ctx.enter_context(nc.Block())
        w_view = w_in[0].rearrange("(t p) n -> p t n", p=P)

        @block.sync
        def _(sp):
            def loads(n, first=False, last=False):
                for i in range(4):
                    if first and i == 2:
                        load_y(0, Y_EARLY)
                    if first and i == 3:
                        load_y(Y_EARLY, Y_TILES)
                    column = None if last else sp.snap(n * P + (COL_GATES + i * D))
                    if last and i >= 2:
                        sp.wait_ge(gate_ready, n * 4 + i - 1)
                    elif not (first and i < 2):
                        sp.wait_ge(g_lo_ready, n * 4 + i - 1)
                    if i == 0 and not first:
                        sp.wait_ge(b_lo_ready, n)
                    if last:
                        sp.dma_start(g_raw[:, i % 2].rearrange("p t n -> p (t n)"), k.logits[i * P:(i + 1) * P, :]).then_inc(g_in[i % 2], 16)
                    else:
                        sp.dma_start(g_raw[:, i % 2], w_view[:, :, bass.ds(column, P)]).then_inc(g_in[i % 2], 16)
                    if i == 0:
                        for j in range(4):
                            sp.dma_start(b_raw[:, Y_FIRST[j]:Y_FIRST[j + 1], :],
                                         w_br[j][0].rearrange("(t p) n -> p t n", p=P)[:, :, bass.ds(n * P, P)]).then_inc(b_in, 16)
                    if i == 1 and not first:
                        store(n - 1)

            def store(n):
                sp.wait_ge(added, n * 3 + 3)
                sp.dma_start(k.merged[bass.ds(n * P, P), :], merged[:, :]).then_inc(stored, 16)

            def load_y(t0, t1):
                for t in range(t0, t1):
                    if t >= 2:
                        sp.wait_ge(y_lo_ready, t - 1)
                    sp.dma_start(y_raw[:, t % 2], k.mix[t * P:(t + 1) * P, :]).then_inc(y_in[t % 2], 16)

            loads(0, first=True)
            with sp.Fori(1, N_TILES - 1) as n:
                loads(n)
            loads(N_TILES - 1, last=True)
            store(N_TILES - 1)
            sp.wait_ge(stored, 16 * N_TILES)

        @block.scalar
        def _(act):
            def split_gate(n, i, first=False):
                act.wait_ge(g_in[i % 2], n * 32 + (16 * (i // 2) + 16))
                if not first:
                    act.wait_ge(gate_done, n * 4 + i - 1)
                nc.scalar.activation(g_hi[:, i % 2], g_raw[:, i % 2], ACT.Copy).then_inc(g_hi_ready, 1)

            def split_branch(n, first=False):
                act.wait_ge(b_in, n * 64 + 64)
                if not first:
                    act.wait_ge(y_done, n * 4)
                nc.scalar.activation(b_hi[:, :, :], b_raw[:, :, :], ACT.Copy).then_inc(b_hi_ready, 1)

            def squash(n, i, first=False, last=False):
                if last:
                    act.wait_ge(g_in[i % 2], n * 32 + 16 * (i // 2) + 16)
                else:
                    act.wait_ge(gate_done, n * 4 + i + 1)
                if i == 2:
                    act.wait_ge(gated, n * 4 + 1)
                elif not first:
                    act.wait_ge(added, n * 3 + (i - 1 if i < 2 else 1))
                logits = g_raw[:, i % 2].rearrange("p t n -> p (t n)") if last else ps_g[:, i % 2, :, :].rearrange("p h c -> p (h c)")
                nc.scalar.activation(gate[:, i % 2], logits, ACT.Sigmoid).then_inc(gate_ready, 1)

            def split_y(t0, t1):
                for t in range(t0, t1):
                    act.wait_ge(y_in[t % 2], 16 * (t // 2 + 1))
                    nc.scalar.activation(k.y_hi[:, t, :], y_raw[:, t % 2], ACT.Copy).then_inc(y_hi_ready, 1)

            def body(n, first=False, before_last=False, last=False):
                for i in range(4):
                    squash(n, i, first and i < 2, last)
                    if last:
                        continue
                    if i < 2:
                        split_gate(n, i + 2)
                        if first:
                            split_y(Y_EARLY + 2 * i, Y_EARLY + 2 * i + 2)
                    elif not before_last:
                        split_gate(n + 1, i - 2)
                if not last:
                    split_branch(n + 1)

            split_gate(0, 0, True)
            split_gate(0, 1, True)
            split_branch(0, True)
            split_y(0, Y_EARLY)
            body(0, first=True)
            with act.Fori(1, N_TILES - 2) as n:
                body(n)
            body(N_TILES - 2, before_last=True)
            body(N_TILES - 1, last=True)

        @block.gpsimd
        def _(pool):
            def lows(n, last=False):
                for i in range(2 if last else 4):
                    pool.wait_ge(g_hi_ready, n * 4 + i + 3)
                    low(i)
                pool.wait_ge(b_hi_ready, n + 2)
                low_branch()

            def low(i):
                nc.gpsimd.tensor_tensor(g_lo[:, i % 2], g_raw[:, i % 2], g_hi[:, i % 2].bitcast(F32), ALU.subtract).then_inc(g_lo_ready, 1)

            def low_branch():
                nc.gpsimd.tensor_tensor(b_lo[:, :, :], b_raw[:, :, :], b_hi[:, :, :].bitcast(F32), ALU.subtract).then_inc(b_lo_ready, 1)

            for i in range(2):
                pool.wait_ge(g_hi_ready, i + 1)
                low(i)
            pool.wait_ge(b_hi_ready, 1)
            low_branch()
            lows(0)
            with pool.Fori(1, N_TILES - 2) as n:
                lows(n)
            lows(N_TILES - 2, last=True)

        @block.tensor
        def _(pe):
            def gate_logits(n, i, first):
                pe.wait_ge(g_lo_ready, n * 4 + i + 1)
                if not (first and i < 2):
                    pe.wait_ge(gate_ready, n * 4 + i - 1)
                for h in range(NH):
                    last = split_product(nc, ps_g[:, i % 2, h, :], g_hi[:, i % 2], g_lo[:, i % 2],
                                         k.h_hi[:, :, h * HALF:(h + 1) * HALF], k.h_lo[:, :, h * HALF:(h + 1) * HALF])
                last.then_inc(gate_done, 1)

            def body(n, first=False, gates=True):
                for i in range(4):
                    if gates:
                        gate_logits(n, i, first)
                    if i == 0:
                        pe.wait_ge(b_lo_ready, n + 1)
                    if not (first and i < 2):
                        pe.wait_ge(gated, n * 4 + i - 1)
                    t0, t1 = Y_FIRST[i], Y_FIRST[i + 1]
                    if first:
                        pe.wait_ge(y_lo_ready, t1)
                    for h in range(NH):
                        last = split_product(nc, ps_y[:, i % 2, h, :], b_hi[:, t0:t1, :], b_lo[:, t0:t1, :],
                                             k.y_hi[:, t0:t1, h * HALF:(h + 1) * HALF], k.y_lo[:, t0:t1, h * HALF:(h + 1) * HALF])
                    last.then_inc(y_done, 1)

            body(0, first=True)
            with pe.Fori(1, N_TILES - 1) as n:
                body(n)
            body(N_TILES - 1, gates=False)

        @block.vector
        def _(dve):
            def low_y(t0, t1):
                for t in range(t0, t1):
                    dve.wait_ge(y_hi_ready, t + 1)
                    nc.vector.tensor_tensor(k.y_lo[:, t, :], y_raw[:, t % 2], k.y_hi[:, t, :].bitcast(F32), ALU.subtract).then_inc(y_lo_ready, 1)

            def body(n, first=False):
                for i in range(4):
                    dve.wait_ge(gate_ready, n * 4 + i + 1)
                    dve.wait_ge(y_done, n * 4 + i + 1)
                    y = ps_y[:, i % 2, :, :].rearrange("p h c -> p (h c)")
                    if i == 0:
                        if not first:
                            dve.wait_ge(stored, n * 16)
                        nc.vector.tensor_tensor(merged[:, :], y, gate[:, 0], ALU.mult).then_inc(gated, 1)
                        dve.wait_ge(gated, n * 4 + 1)
                        if first:
                            low_y(Y_EARLY, Y_EARLY + 2)
                        continue
                    nc.vector.tensor_tensor(gate[:, i % 2], y, gate[:, i % 2], ALU.mult).then_inc(gated, 1)
                    dve.wait_ge(gated, n * 4 + i + 1)
                    nc.vector.tensor_tensor(merged[:, :], merged[:, :], gate[:, i % 2], ALU.add).then_inc(added, 1)
                    dve.wait_ge(added, n * 3 + i)
                    if first and i == 1:
                        low_y(Y_EARLY + 2, Y_TILES)

            low_y(0, Y_EARLY)
            body(0, first=True)
            with dve.Fori(1, N_TILES) as n:
                body(n)


def stage_out(nc, k, w_out, m_hi, m_lo, xT, rinv):
    N_TILES = D // P
    with ExitStack() as ctx:
        raw = ctx.enter_context(nc.sbuf_tensor("wo_raw", [P, 2, KT, P], F32))
        w_hi = ctx.enter_context(nc.sbuf_tensor("wo_hi", [P, 2, KT, P], F32R))
        w_lo = ctx.enter_context(nc.sbuf_tensor("wo_lo", [P, 2, KT, P], F32R))
        m_raw = ctx.enter_context(nc.sbuf_tensor("wo_m_raw", [P, KT, S], F32))
        sq = ctx.enter_context(nc.sbuf_tensor("wo_sq", [P, 2, S], F32))
        ps = ctx.enter_context(nc.psum_tensor("wo_ps", [P, 2, NH, HALF], F32))
        ps_sq = ctx.enter_context(nc.psum_tensor("wo_ps_sq", [P, NH, HALF], F32))
        raw_in = sems(nc, ctx, "wo_in0", "wo_in1")
        m_in = sems(nc, ctx, *(f"wo_m_in{t}" for t in range(KT)))
        x_in = sems(nc, ctx, *(f"wo_x_in{t}" for t in range(KT)))
        hi_ready, lo_ready, m_hi_ready, m_lo_ready, multiplied, summed, squared, sq_summed, logged = sems(
            nc, ctx, "wo_hi_ready", "wo_lo_ready", "wo_m_hi_ready", "wo_m_lo_ready", "wo_multiplied", "wo_summed", "wo_squared",
            "wo_sq_summed", "wo_logged")
        block = ctx.enter_context(nc.Block())
        w_view = w_out[0].rearrange("(t p) n -> p t n", p=P)

        @block.sync
        def _(sp):
            def load_w(n):
                if n >= 2:
                    sp.wait_ge(lo_ready, n - 1)
                sp.dma_start(raw[:, n % 2], w_view[:, :, n * P:(n + 1) * P]).then_inc(raw_in[n % 2], 16)

            load_w(0)
            load_w(1)
            for t in range(KT):
                sp.dma_start(m_raw[:, t], k.merged[t * P:(t + 1) * P, :]).then_inc(m_in[t], 16)
                if t == KT - 2:
                    load_w(2)
            load_w(3)
            for t in range(KT):
                sp.dma_start(xT[:, t, :], k.xT_dram[t * P:(t + 1) * P, :]).then_inc(x_in[t], 16)
            for n in range(4, N_TILES):
                load_w(n)

        @block.scalar
        def _(act):
            def split(n):
                act.wait_ge(raw_in[n % 2], 16 * (n // 2 + 1))
                if n >= 2:
                    act.wait_ge(multiplied, n - 1)
                nc.scalar.activation(w_hi[:, n % 2], raw[:, n % 2], ACT.Copy).then_inc(hi_ready, 1)

            def square(n):
                act.wait_ge(summed, n + 1)
                if n >= 2:
                    act.wait_ge(sq_summed, n - 1)
                nc.scalar.activation(sq[:, n % 2], xT[:, n, :], ACT.Square).then_inc(squared, 1)

            nc.scalar.preload_act_table_set("natural_log_exp_and_others")
            split(0)
            split(1)
            for t in range(KT):
                act.wait_ge(m_in[t], 16)
                nc.scalar.activation(m_hi[:, t, :], m_raw[:, t], ACT.Copy).then_inc(m_hi_ready, 1)
            for n in range(2, N_TILES):
                split(n)
                square(n - 2)
            square(N_TILES - 2)
            square(N_TILES - 1)
            act.wait_ge(sq_summed, N_TILES)
            nc.scalar.activation(rinv[:, :], ps_sq[:, :, :].rearrange("p h c -> p (h c)"), ACT.Ln, scale=1.0 / D, bias=k.eps[:, 0:1]).then_inc(logged, 1)
            act.wait_ge(logged, 1)
            nc.scalar.activation(rinv[:, :], rinv[:, :], ACT.Exp, scale=-0.5)

        @block.gpsimd
        def _(pool):
            for n in range(N_TILES):
                pool.wait_ge(hi_ready, n + 1)
                nc.gpsimd.tensor_tensor(w_lo[:, n % 2], raw[:, n % 2], w_hi[:, n % 2].bitcast(F32), ALU.subtract).then_inc(lo_ready, 1)

        @block.tensor
        def _(pe):
            def product(n, h, t0, t1):
                return split_product(nc, ps[:, n % 2, h, :], w_hi[:, n % 2, t0:t1, :], w_lo[:, n % 2, t0:t1, :],
                                     m_hi[:, t0:t1, h * HALF:(h + 1) * HALF], m_lo[:, t0:t1, h * HALF:(h + 1) * HALF],
                                     first=(t0 == 0), last=(t1 == KT))

            def sum_squares(n):
                pe.wait_ge(squared, n + 1)
                for h in range(NH):
                    last = nc.tensor.matmul(ps_sq[:, h, :], k.ones[:, :], sq[:, n % 2, h * HALF:(h + 1) * HALF], start=(n == 0), stop=(n == N_TILES - 1))
                last.then_inc(sq_summed, 1)

            for t in range(KT):
                pe.wait_ge(m_lo_ready, t + 1)
                for n in range(2):
                    if t == 0:
                        pe.wait_ge(lo_ready, n + 1)
                    for h in range(NH):
                        last = product(n, h, t, t + 1)
                    if t == KT - 1:
                        last.then_inc(multiplied, 1)
            for n in range(2, N_TILES):
                pe.wait_ge(lo_ready, n + 1)
                pe.wait_ge(summed, n - 1)
                for h in range(NH):
                    last = product(n, h, 0, KT)
                last.then_inc(multiplied, 1)
                sum_squares(n - 2)
            sum_squares(N_TILES - 2)
            sum_squares(N_TILES - 1)

        @block.vector
        def _(dve):
            nc.vector.scalar_tensor_tensor(out=k.scale2[:, :], in0=k.mod[:, M_SC2:M_SC2 + KT], scalar=1.0,
                                           in1=k.cols[:, V_GMLP:V_GMLP + KT], op0=ALU.add, op1=ALU.mult)
            for t in range(KT):
                dve.wait_ge(m_hi_ready, t + 1)
                nc.vector.tensor_tensor(m_lo[:, t, :], m_raw[:, t], m_hi[:, t, :].bitcast(F32), ALU.subtract).then_inc(m_lo_ready, 1)
            for n in range(N_TILES):
                dve.wait_ge(x_in[n], 16)
                dve.wait_ge(multiplied, n + 1)
                nc.vector.scalar_tensor_tensor(out=xT[:, n, :], in0=ps[:, n % 2, :, :].rearrange("p h c -> p (h c)"),
                                               scalar=k.mod[:, M_GT1 + n:M_GT1 + n + 1], in1=xT[:, n, :],
                                               op0=ALU.mult, op1=ALU.add).then_inc(summed, 1)


def stage_mlp(nc, k, w_up, w_down, h_hi, h_lo, xT, rinv, scale, shift, out):
    BF = 4
    NB = D_FF // (BF * P)
    with ExitStack() as ctx:
        raw = ctx.enter_context(nc.sbuf_tensor("ff_raw", [P, 2, KT * P], F32))
        w_hi = ctx.enter_context(nc.sbuf_tensor("ff_hi", [P, 2, KT * P], F32R))
        w_lo = ctx.enter_context(nc.sbuf_tensor("ff_lo", [P, 2, KT * P], F32R))
        u_hi = ctx.enter_context(nc.sbuf_tensor("u_hi", [P, 2, BF, S], F32R))
        u_lo = ctx.enter_context(nc.sbuf_tensor("u_lo", [P, 2, BF, S], F32R))
        relu = ctx.enter_context(nc.sbuf_tensor("ff_relu", [P, 2, S], F32))
        square = ctx.enter_context(nc.sbuf_tensor("ff_square", [P, 2, S], F32))
        ps_u = ctx.enter_context(nc.psum_tensor("ff_ps_u", [P, 2, NH, HALF], F32))
        ps_d = ctx.enter_context(nc.psum_tensor("ff_ps_d", [P, 2, NH, HALF], F32))
        raw_in = sems(nc, ctx, "ff_in0", "ff_in1")
        (hi_ready, lo_ready, up_done, down_done, relu_ready, square_ready, u_hi_ready, u_lo_ready, summed, turned) = sems(
            nc, ctx, "ff_hi_ready", "ff_lo_ready", "ff_up_done", "ff_down_done", "ff_relu_ready", "ff_square_ready",
            "ff_u_hi_ready", "ff_u_lo_ready", "ff_summed", "ff_turned")
        norm = apply_norm(nc, ctx, "n2", xT, rinv, scale, shift, h_hi, h_lo, relu, square)
        out_stored = sems(nc, ctx, "ff_out_stored0", "ff_out_stored1")
        rows_ready = sems(nc, ctx, "ff_rows_ready_act", "ff_rows_ready_dve")
        block = ctx.enter_context(nc.Block())
        up_view = w_up[0].rearrange("(t p) n -> p t n", p=P)
        down_view = w_down[0].rearrange("(b t p) n -> p (b t) n", p=P, t=BF)

        def slot(t, s, width):
            return t[:, s, :].rearrange("p (t n) -> p t n", n=width)

        def all_steps(eng, step):
            step(-1, True, False)
            step(0, True, True)
            with eng.Fori(0, (NB - 2) // 2) as j:
                step(j * 2 + 1, True, True, parity=1)
                step(j * 2 + 2, True, True, parity=0)
            step(NB - 1, False, True)

        def par(b, parity):
            return b % 2 if parity is None else parity

        @block.sync
        def _(sp):
            def step(b, up, down, parity=None):
                w0 = 0 if up and not down else b * 8 + 4
                r0 = 0 if up and not down else b * 64 + 32
                n_up = BF if up else 0
                row = sp.snap(b * BF) if down else None
                for f in range(n_up + (BF if down else 0)):
                    column = sp.snap(b * (BF * P) + (BF * P + f * P)) if f < n_up else None
                    if not (up and not down and f < 2):
                        sp.wait_ge(lo_ready, w0 + (f - 1))
                    if f < n_up:
                        src = up_view[:, :, bass.ds(column, P)]
                        sp.dma_start(slot(raw, f % 2, P), src).then_inc(raw_in[f % 2], 16)
                    else:
                        q = f - n_up
                        src = down_view[:, bass.ds(row, BF), q * 2 * P:(q + 1) * 2 * P]
                        sp.dma_start(slot(raw, f % 2, 2 * P), src).then_inc(raw_in[f % 2], 16)

            all_steps(sp, step)
            for t in range(KT):
                sp.wait_ge(rows_ready[0], t + 1)
                sp.wait_ge(rows_ready[1], t + 1)
                sp.dma_start(out[0, t * P:(t + 1) * P, :], relu[:, t % 2]).then_inc(out_stored[t % 2], 16)
            for turn in out_stored:
                sp.wait_ge(turn, 16 * KT // 2)

        @block.scalar
        def _(act):
            def split(s):
                nc.scalar.activation(w_hi[:, s], raw[:, s], ACT.Copy).then_inc(hi_ready, 1)

            def split_up(b, f, kind):
                s = f % 2
                if kind == "first":
                    act.wait_ge(raw_in[s], 16 * (f // 2 + 1))
                    if f >= 2:
                        act.wait_ge(up_done, f - 1)
                else:
                    act.wait_ge(raw_in[s], b * 64 + (32 + 16 * (f // 2) + 16))
                    if f >= 2:
                        act.wait_ge(up_done, b * 4 + (4 + f - 1))
                    elif kind == "second":
                        act.wait_ge(up_done, f + 3)
                    else:
                        act.wait_ge(down_done, b * 8 + (2 * f - 2))
                split(s)

            def split_down(b, q, kind=None):
                s = q % 2
                if kind == "last":
                    act.wait_ge(raw_in[s], 64 * b + 32 + 16 * (q // 2) + 16)
                    act.wait_ge(down_done, 8 * b + 2 * q - 2)
                else:
                    act.wait_ge(raw_in[s], b * 64 + (32 + 32 + 16 * (q // 2) + 16))
                    if q >= 2:
                        act.wait_ge(down_done, b * 8 + (2 * q - 2))
                    else:
                        act.wait_ge(up_done, b * 4 + (4 + q + 3))
                split(s)

            def hidden(b, f, free, slot_u, recycled):
                act.wait_ge(up_done, b * 4 + (4 + f + 1))
                if free:
                    act.wait_ge(square_ready, b * 4 + (4 + f - 1))
                nc.scalar.activation(relu[:, f % 2], ps_u[:, f % 2, :, :].rearrange("p h c -> p (h c)"), ACT.Relu).then_inc(relu_ready, 1)
                act.wait_ge(relu_ready, b * 4 + (4 + f + 1))
                if recycled:
                    act.wait_ge(down_done, b * 8)
                nc.scalar.activation(u_hi[:, slot_u, f, :], relu[:, f % 2], ACT.Square).then_inc(u_hi_ready, 1)

            def step(b, up, down, parity=None):
                peeled = parity is None
                if up and not down:
                    split_up(-1, 0, "first")
                    split_up(-1, 1, "first")
                    norm.scalar(act)
                for f in range(BF if up else 0):
                    hidden(b, f, not (peeled and b == -1 and f < 2), 1 - par(b, parity), not (peeled and b <= 0))
                    if f < 2:
                        split_up(b, f + 2, "first" if not down else "later")
                    elif down:
                        split_down(b, f - 2)
                    else:
                        split_up(0, f - 2, "second")
                for q in range(BF if down else 0):
                    if up and q < 2:
                        split_down(b, q + 2)
                    elif not up:
                        if q < 2:
                            split_down(b, q + 2, "last")
                    elif peeled or parity == 1:
                        split_up(b + 1, q - 2, "later")
                    else:
                        split_next(b, q - 2)

            def split_next(b, f):
                act.wait_ge(raw_in[f], b * 64 + (64 + 32 + 16))
                act.wait_ge(down_done, b * 8 + (8 + 2 * f - 2))
                split(f)

            all_steps(act, step)
            for t in range(KT):
                act.wait_ge(turned, 2 * t + 1)
                if t >= 2:
                    act.wait_ge(out_stored[t % 2], 16 * (t // 2))
                nc.scalar.activation(relu[:, t % 2, 0:HALF], ps_u[:, t % 2, 0, :], ACT.Copy).then_inc(rows_ready[0], 1)

        @block.gpsimd
        def _(pool):
            def low(s, count):
                pool.wait_ge(hi_ready, count)
                nc.gpsimd.tensor_tensor(w_lo[:, s], raw[:, s], w_hi[:, s].bitcast(F32), ALU.subtract).then_inc(lo_ready, 1)

            def step(b, up, down, parity=None):
                w0 = 0 if up and not down else b * 8 + 4
                if up and not down:
                    low(0, 1)
                    low(1, 2)
                    norm.gpsimd(pool)
                n_up = BF if up else 0
                n = n_up + (BF if down else 0)
                for f in range(n):
                    if f < n_up:
                        pool.wait_ge(square_ready, b * 4 + (4 + f + 1))
                        pool.wait_ge(u_hi_ready, b * 4 + (4 + f + 1))
                        su = 1 - par(b, parity)
                        nc.gpsimd.tensor_tensor(u_lo[:, su, f, :], square[:, f % 2], u_hi[:, su, f, :].bitcast(F32),
                                                ALU.subtract).then_inc(u_lo_ready, 1)
                    if up or f < 2:
                        low(f % 2, w0 + (f + 3))

            all_steps(pool, step)

        @block.tensor
        def _(pe):
            def step(b, up, down, parity=None):
                w0 = 0 if up and not down else b * 8 + 4
                n_up = BF if up else 0
                opening = up and not down
                for t in range(KT if opening else 0):
                    pe.wait_ge(norm.lo_ready, t + 1)
                    for f in range(2):
                        if t == 0:
                            pe.wait_ge(lo_ready, f + 1)
                        for h in range(NH):
                            last = split_product(nc, ps_u[:, f, h, :], slot(w_hi, f, P)[:, t:t + 1, :], slot(w_lo, f, P)[:, t:t + 1, :],
                                                 h_hi[:, t:t + 1, h * HALF:(h + 1) * HALF], h_lo[:, t:t + 1, h * HALF:(h + 1) * HALF],
                                                 first=(t == 0), last=(t == KT - 1))
                        if t == KT - 1:
                            last.then_inc(up_done, 1)
                for f in range(2 if opening else 0, n_up):
                    pe.wait_ge(lo_ready, w0 + (f + 1))
                    pe.wait_ge(relu_ready, b * 4 + (4 + f - 1))
                    for h in range(NH):
                        last = split_product(nc, ps_u[:, f % 2, h, :], slot(w_hi, f % 2, P), slot(w_lo, f % 2, P),
                                             h_hi[:, :, h * HALF:(h + 1) * HALF], h_lo[:, :, h * HALF:(h + 1) * HALF])
                    last.then_inc(up_done, 1)
                if not down:
                    return
                su = par(b, parity)
                pe.wait_ge(u_lo_ready, b * 4 + 4)
                for q in range(BF):
                    pe.wait_ge(lo_ready, w0 + (n_up + q + 1))
                    hi, lo = slot(w_hi, q % 2, 2 * P), slot(w_lo, q % 2, 2 * P)
                    for m in range(2):
                        if not (parity is None and b == 0 and q == 0):
                            pe.wait_ge(summed, b * 8 + (2 * q + m - 1))
                        for h in range(NH):
                            last = split_product(nc, ps_d[:, m, h, :], hi[:, :, m * P:(m + 1) * P], lo[:, :, m * P:(m + 1) * P],
                                                 u_hi[:, su, :, h * HALF:(h + 1) * HALF], u_lo[:, su, :, h * HALF:(h + 1) * HALF])
                        last.then_inc(down_done, 1)

            all_steps(pe, step)
            pe.wait_ge(summed, 8 * NB)
            for t in range(KT):
                for g in range(2):
                    if t >= 2:
                        pe.wait_ge(rows_ready[g], t - 1)
                    bank = (ps_u if g == 0 else ps_d)[:, t % 2, 0, :]
                    for a in range(4):
                        last = nc.tensor.transpose(bank[:, a * P:(a + 1) * P], xT[:, 4 * g + a, t * P:(t + 1) * P], k.ident[:, :])
                    last.then_inc(turned, 1)

        @block.vector
        def _(dve):
            def step(b, up, down, parity=None):
                for f in range(BF if up else 0):
                    dve.wait_ge(relu_ready, b * 4 + (4 + f + 1))
                    if not (up and not down and f < 2):
                        dve.wait_ge(u_lo_ready, b * 4 + (4 + f - 1))
                    nc.vector.tensor_tensor(square[:, f % 2], relu[:, f % 2], relu[:, f % 2], ALU.mult).then_inc(square_ready, 1)
                for n in range(KT if down else 0):
                    dve.wait_ge(down_done, b * 8 + (n + 1))
                    if not (parity is None and b == 0):
                        dve.wait_ge(summed, b * 8 + (n - 7))
                    nc.vector.scalar_tensor_tensor(out=xT[:, n, :], in0=ps_d[:, n % 2, :, :].rearrange("p h c -> p (h c)"),
                                                   scalar=k.mod[:, M_GT2 + n:M_GT2 + n + 1], in1=xT[:, n, :],
                                                   op0=ALU.mult, op1=ALU.add).then_inc(summed, 1)

            norm.vector(dve)
            all_steps(dve, step)
            for t in range(KT):
                dve.wait_ge(turned, 2 * t + 2)
                if t >= 2:
                    dve.wait_ge(out_stored[t % 2], 16 * (t // 2))
                nc.vector.tensor_copy(relu[:, t % 2, HALF:D], ps_d[:, t % 2, 0, :]).then_inc(rows_ready[1], 1)


GATES_IN_WINDOW, GATES_IN_GLA = [0, 1], [2, 3]

UNIT_STEP = (1, 4, 8)
A_HEADS = 4
E = 64
MASKED = -1e30
ROW = A_HEADS * E + 2 * A_HEADS


def query_tokens(ap, g, u):
    if g == 0:
        return ap[..., u * P:(u + 1) * P]
    if g == 1:
        r, b = u // 2, u % 2
        return ap[..., bass.ds(r + 4 * P * b, P, step=4)]
    return ap[..., bass.ds(u, P, step=8)]


def key_tokens(ap, g, u):
    if key_tiles(g, u) == 1:
        return query_tokens(ap, g, u)
    if g == 0:
        return ap[..., (u - 1) * P:(u + 1) * P]
    return ap[..., bass.ds(u // 2, 2 * P, step=4)]


def head_slot(h):
    return 2 * (h % 2) + h // 2


def key_tiles(g, u):
    return 2 if (g == 0 and u > 0) or (g == 1 and u % 2 == 1) else 1


def stage_window(nc, k, w_in):
    UNITS = [(g, u) for g in range(3) for u in range(8)]
    slopes = [2.0 ** (-8.0 * (i + 1) / 12) for i in range(12)]
    with ExitStack() as outer:
        qk = outer.enter_context(nc.sbuf_tensor("wa_qk", [P, 2 * A_TILES, S], F32))
        v_tok = outer.enter_context(nc.sbuf_tensor("wa_v_tok", [P, len(UNITS), A_HEADS * E], F32))
        bias = outer.enter_context(nc.sbuf_tensor("wa_bias", [P, 12, 2 * P], F32))
        with ExitStack() as ctx:
            vT = ctx.enter_context(nc.sbuf_tensor("wa_vT", [P, A_TILES, S], F32))
            sq = ctx.enter_context(nc.sbuf_tensor("wa_sq", [P, 2, S], F32))
            rinv = ctx.enter_context(nc.sbuf_tensor("wa_rinv", [P, 2, S], F32))
            rel = ctx.enter_context(nc.sbuf_tensor("wa_rel", [P, 2 * P], F32))
            odd = ctx.enter_context(nc.sbuf_tensor("wa_odd", [P, 2 * P], I32))
            other = ctx.enter_context(nc.sbuf_tensor("wa_other", [P, 2 * P], F32))
            odd_step, = sems(nc, ctx, "wa_odd_step")
            qk_in = sems(nc, ctx, *(f"wa_qk_in{m}" for m in range(A_TILES)))
            v_in = sems(nc, ctx, *(f"wa_v_in{g}" for g in range(3)))
            ps_n = ctx.enter_context(nc.psum_tensor("wa_ps_n", [P, 2, NH, HALF], F32))
            ps_v = ctx.enter_context(nc.psum_tensor("wa_ps_v", [P, 2, HALF], F32))
            squared, summed, logged, rooted, normed, turned, v_copied, rel_ready, bias_scaled, bias_cut = sems(
                nc, ctx, "wa_squared", "wa_summed", "wa_logged", "wa_rooted", "wa_normed",
                "wa_turned", "wa_v_copied", "wa_rel_ready", "wa_bias_scaled", "wa_bias_cut")
            block = ctx.enter_context(nc.Block())

            @block.sync
            def _(sp):
                for g in range(3):
                    row = (R_AV + 2 * g) * P
                    sp.dma_start(vT[:, 2 * g:2 * g + 2, :], feature_tiles(k.proj[row:row + 2 * P, :])).then_inc(v_in[g], 16)
                for m in range(A_TILES):
                    row = (R_AQ + 2 * m) * P
                    sp.dma_start(qk[:, 2 * m:2 * m + 2, :], feature_tiles(k.proj[row:row + 2 * P, :])).then_inc(qk_in[m], 16)

            @block.scalar
            def _(act):
                nc.scalar.preload_act_table_set("natural_log_exp_and_others")

                for t in range(2 * A_TILES):
                    act.wait_ge(summed, t + 1)
                    if t >= 2:
                        act.wait_ge(normed, t - 1)
                    nc.scalar.activation(rinv[:, t % 2], ps_n[:, t % 2, :, :].rearrange("p h c -> p (h c)"), ACT.Ln,
                                         scale=1.0 / E, bias=k.eps[:, 0:1]).then_inc(logged, 1)
                    act.wait_ge(logged, t + 1)
                    nc.scalar.activation(rinv[:, t % 2], rinv[:, t % 2], ACT.Exp, scale=-0.5).then_inc(rooted, 1)

            @block.tensor
            def _(pe):
                for n in range(len(UNITS) // 2):
                    if n % 4 == 0:
                        pe.wait_ge(v_in[n // 4], 16)
                    if n >= 2:
                        pe.wait_ge(v_copied, n - 1)
                    for a in range(2):
                        g, u = UNITS[2 * n + a]
                        for c in range(2):
                            last = nc.tensor.transpose(ps_v[:, n % 2, (2 * a + c) * P:(2 * a + c + 1) * P],
                                                       query_tokens(vT[:, 2 * g + c, :], g, u), k.ident[:, :])
                    last.then_inc(turned, 1)
                for t in range(2 * A_TILES):
                    pe.wait_ge(squared, t + 1)
                    if t >= 2:
                        pe.wait_ge(logged, t - 1)
                    for h in range(NH):
                        last = nc.tensor.matmul(ps_n[:, t % 2, h, :], k.headsum[:, :], sq[:, t % 2, h * HALF:(h + 1) * HALF], start=True, stop=True)
                    last.then_inc(summed, 1)

            @block.vector
            def _(dve):
                dve.wait_ge(rel_ready, 2)
                nc.vector.tensor_scalar(odd[:, :], odd[:, :], 1, None, ALU.bitwise_and).then_inc(odd_step, 1)
                dve.wait_ge(odd_step, 1)
                nc.vector.tensor_scalar(other[:, :], odd[:, :], MASKED, None, ALU.mult).then_inc(odd_step, 1)
                dve.wait_ge(odd_step, 2)
                for i in range(12):
                    at = 4 * (i // 4) + head_slot(i % 4)
                    slope = -slopes[i] * UNIT_STEP[i // 4] * E ** 0.5
                    if i < 8:
                        ins = nc.vector.tensor_scalar(bias[:, at, :], rel[:, :], slope, None, ALU.mult)
                    else:
                        ins = nc.vector.scalar_tensor_tensor(out=bias[:, at, :], in0=rel[:, :], scalar=slope, in1=other[:, :],
                                                             op0=ALU.mult, op1=ALU.add)
                    ins.then_inc(bias_scaled, 1)
                for n in range(len(UNITS) // 2):
                    dve.wait_ge(turned, n + 1)
                    nc.vector.tensor_copy(v_tok[:, 2 * n:2 * n + 2, :].rearrange("p u e -> p (u e)"), ps_v[:, n % 2, :]).then_inc(v_copied, 1)
                for t in range(2 * A_TILES):
                    dve.wait_ge(rooted, t + 1)
                    gain = k.cols[:, (V_QG if t < A_TILES else V_KG):(V_QG if t < A_TILES else V_KG) + 1]
                    nc.vector.scalar_tensor_tensor(out=qk[:, t, :], in0=qk[:, t, :], scalar=gain, in1=rinv[:, t % 2],
                                                   op0=ALU.mult, op1=ALU.mult).then_inc(normed, 1)

            @block.gpsimd
            def _(pool):
                nc.gpsimd.iota(rel[:, :], pattern=[[-1, 2 * P]], base=P, channel_multiplier=1,
                               allow_small_or_imprecise_dtypes=True).then_inc(rel_ready, 1)
                nc.gpsimd.iota(odd[:, :], pattern=[[1, 2 * P]], base=0, channel_multiplier=1).then_inc(rel_ready, 1)
                for t in range(2 * A_TILES):
                    pool.wait_ge(qk_in[t // 2], 16)
                    if t >= 2:
                        pool.wait_ge(summed, t - 1)
                    nc.gpsimd.tensor_tensor(sq[:, t % 2], qk[:, t, :], qk[:, t, :], ALU.mult).then_inc(squared, 1)
                pool.wait_ge(bias_scaled, 12)
                nc.gpsimd.affine_select(out=bias[:, :, :], in_=bias[:, :, :], compare_op=ALU.is_ge, fill=MASKED, base=P,
                                        pattern=[[0, 12], [-1, 2 * P]], channel_multiplier=1).then_inc(bias_cut, 1)
                pool.wait_ge(bias_cut, 1)
                nc.gpsimd.affine_select(out=bias[:, :, :], in_=bias[:, :, :], compare_op=ALU.is_ge, fill=MASKED, base=0,
                                        pattern=[[0, 12], [1, 2 * P]], channel_multiplier=-1).then_inc(bias_cut, 2)

        with ExitStack() as ctx:
            ROWS = 6
            prob = ctx.enter_context(nc.sbuf_tensor("wa_prob", [P, 3, A_HEADS, 2 * P], F32))
            probT = ctx.enter_context(nc.sbuf_tensor("wa_probT", [P, 2, A_HEADS * 2, P], F32))
            row = ctx.enter_context(nc.sbuf_tensor("wa_row", [P, ROWS, ROW], F32))
            negmax = ctx.enter_context(nc.sbuf_tensor("wa_negmax", [P, 2, A_HEADS], F32))
            ps_s = ctx.enter_context(nc.psum_tensor("wa_ps_s", [P, 2, A_HEADS, 2 * P], F32))
            ps_t = ctx.enter_context(nc.psum_tensor("wa_ps_t", [P, A_HEADS * 2, P], F32))
            ps_o = ctx.enter_context(nc.psum_tensor("wa_ps_o", [P, 2, HALF], F32))
            scored, biased, max_ready, negmax_ready, exped, p_turned, p_copied, o_done, o_copied = sems(
                nc, ctx, "wa_scored", "wa_biased", "wa_max_ready", "wa_negmax_ready", "wa_exped", "wa_p_turned", "wa_p_copied",
                "wa_o_done", "wa_o_copied")
            stored = sems(nc, ctx, *(f"wa_stored{i}" for i in range(ROWS)))
            block = ctx.enter_context(nc.Block())
            N = len(UNITS)

            def span(n):
                return slice(2 * P - P * key_tiles(*UNITS[n]), 2 * P)

            @block.tensor
            def _(pe):
                def scores(n):
                    g, u = UNITS[n]
                    if n >= 2:
                        pe.wait_ge(biased, n - 1)
                    for h in range(A_HEADS):
                        rows = slice(E * (h % 2), E * (h % 2) + E)
                        last = nc.tensor.matmul(ps_s[:, n % 2, head_slot(h), span(n)], query_tokens(qk[rows, 2 * g + h // 2, :], g, u),
                                                key_tokens(qk[rows, A_TILES + 2 * g + h // 2, :], g, u), start=True, stop=True)
                    last.then_inc(scored, 1)

                def turn(n):
                    kt = key_tiles(*UNITS[n])
                    pe.wait_ge(exped, A_HEADS * (n + 1))
                    if n >= 1:
                        pe.wait_ge(p_copied, n)
                    for h in range(A_HEADS):
                        for j in range(kt):
                            last = nc.tensor.transpose(ps_t[:, h * kt + j, :], prob[:, n % 3, head_slot(h), (2 - kt + j) * P:(3 - kt + j) * P], k.ident[:, :])
                    last.then_inc(p_turned, 1)

                def values(n):
                    kt = key_tiles(*UNITS[n])
                    pe.wait_ge(p_copied, n + 1)
                    if n >= 2:
                        pe.wait_ge(o_copied, n - 1)
                    for h in range(A_HEADS):
                        for j in range(kt):
                            last = nc.tensor.matmul(ps_o[:, n % 2, h * E:(h + 1) * E], probT[:, n % 2, h * kt + j, :],
                                                    v_tok[:, n - kt + 1 + j, h * E:(h + 1) * E], start=(j == 0), stop=(j == kt - 1))
                    last.then_inc(o_done, 1)

                for n in range(N + 3):
                    if n < N:
                        scores(n)
                    if 2 <= n < N + 2:
                        turn(n - 2)
                    if n >= 3:
                        values(n - 3)

            @block.vector
            def _(dve):
                for n in range(N + 3):
                    if n < N:
                        g, u = UNITS[n]
                        dve.wait_ge(scored, n + 1)
                        if n >= 3:
                            dve.wait_ge(p_turned, n - 2)
                        if n >= ROWS:
                            dve.wait_ge(stored[n % ROWS], 16 * (n // ROWS))
                        nc.vector.tensor_tensor(prob[:, n % 3, :, span(n)], ps_s[:, n % 2, :, span(n)],
                                                bias[:, 4 * g:4 * g + 4, span(n)], ALU.add).then_inc(biased, 1)
                        dve.wait_ge(biased, n + 1)
                        nc.vector.tensor_reduce(row[:, n % ROWS, A_HEADS * E:A_HEADS * E + A_HEADS].rearrange("p (c r) -> p r c", r=2),
                                                prob[:, n % 3, :, span(n)].rearrange("p (r c) k -> p r c k", r=2),
                                                AX.X, ALU.max).then_inc(max_ready, 1)
                        dve.wait_ge(max_ready, n + 1)
                        if n >= 2:
                            dve.wait_ge(exped, A_HEADS * (n - 1))
                        nc.vector.tensor_scalar(negmax[:, n % 2, :], row[:, n % ROWS, A_HEADS * E:A_HEADS * E + A_HEADS],
                                                -(E ** -0.5), None, ALU.mult).then_inc(negmax_ready, 1)
                    if n >= 3:
                        m = n - 3
                        dve.wait_ge(o_done, m + 1)
                        nc.vector.tensor_copy(row[:, m % ROWS, 0:A_HEADS * E], ps_o[:, m % 2, 0:A_HEADS * E]).then_inc(o_copied, 1)

            @block.scalar
            def _(act):
                for n in range(N + 2):
                    if n >= 2:
                        m = n - 2
                        act.wait_ge(p_turned, m + 1)
                        if m >= 2:
                            act.wait_ge(o_done, m - 1)
                        cols = A_HEADS * key_tiles(*UNITS[m])
                        nc.scalar.activation(probT[:, m % 2, 0:cols, :], ps_t[:, 0:cols, :], ACT.Copy).then_inc(p_copied, 1)
                    if n < N:
                        act.wait_ge(negmax_ready, n + 1)
                        for h in range(A_HEADS):
                            nc.scalar.activation(prob[:, n % 3, head_slot(h), span(n)], prob[:, n % 3, head_slot(h), span(n)], ACT.Exp,
                                                 bias=negmax[:, n % 2, h:h + 1], scale=E ** -0.5,
                                                 accum_out=row[:, n % ROWS, A_HEADS * E + A_HEADS + h:A_HEADS * E + A_HEADS + h + 1]).then_inc(exped, 1)

            @block.sync
            def _(sp):
                for n, (g, u) in enumerate(UNITS):
                    sp.wait_ge(o_copied, n + 1)
                    sp.wait_ge(exped, A_HEADS * (n + 1))
                    tokens = k.window[g].rearrange("(m r) c -> r m c", r=UNIT_STEP[g])
                    stream, first = ((0, u * P), (u // 2, (u % 2) * P), (u, 0))[g]
                    sp.dma_start(tokens[stream, first:first + P, :], row[:, n % ROWS, :]).then_inc(stored[n % ROWS], 16)
                for turn in stored:
                    sp.wait_ge(turn, 16 * N // ROWS)

    with ExitStack() as ctx:
        TT = S // P
        G = 3
        part = ctx.enter_context(nc.sbuf_tensor("wm_part", [P, TT, G, ROW], F32))
        top = ctx.enter_context(nc.sbuf_tensor("wm_top", [P, TT, A_HEADS], F32))
        below = ctx.enter_context(nc.sbuf_tensor("wm_below", [P, G, TT, A_HEADS], F32))
        weight = ctx.enter_context(nc.sbuf_tensor("wm_weight", [P, G, TT, A_HEADS], F32))
        total = ctx.enter_context(nc.sbuf_tensor("wm_total", [P, TT, A_HEADS], F32))
        yT = ctx.enter_context(nc.sbuf_tensor("wm_yT", [P, 2, S], F32))
        ps = ctx.enter_context(nc.psum_tensor("wm_ps", [P, 4, HALF], F32))
        part_in, step, exped, turned, copied, stored = sems(nc, ctx, "wm_part_in", "wm_step", "wm_exped", "wm_turned", "wm_copied", "wm_stored")
        ps_g = ctx.enter_context(nc.psum_tensor("wm_ps_gates", [P, 2, NH, HALF], F32))
        gates = LastGates(nc, k, ctx, "wg", w_in, GATES_IN_WINDOW)
        block = ctx.enter_context(nc.Block())
        HE = A_HEADS * E

        @block.gpsimd
        def _(pool):
            for j in range(len(GATES_IN_WINDOW)):
                gates.low(pool, j)

        @block.sync
        def _(sp):
            gates.load(sp, 0)
            for g in range(G):
                sp.dma_start(part[:, :, g, :], k.window[g].rearrange("(t p) c -> p t c", p=P)).then_inc(part_in, 16)
            for j in range(1, len(GATES_IN_WINDOW)):
                gates.load(sp, j)
            gates.store(sp, 0)
            sp.wait_ge(copied, 4)
            sp.dma_start(feature_tiles(k.mix[Y_A * P:Y_B * P, :]), yT[:, :, :]).then_inc(stored, 16)
            for j in range(1, len(GATES_IN_WINDOW)):
                gates.store(sp, j)
            gates.finish(sp)
            sp.wait_ge(stored, 16)

        @block.vector
        def _(dve):
            count = [0]

            def link(ins):
                count[0] += 1
                ins.then_inc(step, 1)
                dve.wait_ge(step, count[0])

            dve.wait_ge(part_in, 16 * G)
            peak = [part[:, :, g, HE:HE + A_HEADS] for g in range(G)]
            link(nc.vector.tensor_tensor(top[:, :, :], peak[0], peak[1], ALU.max))
            link(nc.vector.tensor_tensor(top[:, :, :], top[:, :, :], peak[2], ALU.max))
            for g in range(G):
                last = nc.vector.tensor_tensor(below[:, g], peak[g], top[:, :, :], ALU.subtract)
            link(last)
            dve.wait_ge(exped, 1)
            for g in range(G):
                last = nc.vector.tensor_tensor(below[:, g], weight[:, g], part[:, :, g, HE + A_HEADS:ROW], ALU.mult)
            link(last)
            link(nc.vector.tensor_tensor(total[:, :, :], below[:, 0], below[:, 1], ALU.add))
            link(nc.vector.tensor_tensor(total[:, :, :], total[:, :, :], below[:, 2], ALU.add))
            link(nc.vector.reciprocal(total[:, :, :], total[:, :, :]))
            for g in range(G):
                last = nc.vector.tensor_tensor(weight[:, g], weight[:, g], total[:, :, :], ALU.mult)
            link(last)
            for g in range(G):
                o = part[:, :, g, 0:HE].rearrange("p t (h e) -> p t h e", e=E)
                last = nc.vector.tensor_tensor(o, o, weight[:, g].unsqueeze(3).to_broadcast([P, TT, A_HEADS, E]), ALU.mult)
            link(last)
            link(nc.vector.tensor_tensor(part[:, :, 0, 0:HE], part[:, :, 0, 0:HE], part[:, :, 1, 0:HE], ALU.add))
            link(nc.vector.tensor_tensor(part[:, :, 0, 0:HE], part[:, :, 0, 0:HE], part[:, :, 2, 0:HE], ALU.add))
            k.window_merged = count[0]
            for n in range(4):
                dve.wait_ge(turned, n + 1)
                nc.vector.tensor_copy(yT[:, n // 2, (n % 2) * HALF:(n % 2 + 1) * HALF], ps[:, n, :]).then_inc(copied, 1)

        @block.scalar
        def _(act):
            gates.split(act, 0)
            gates.split(act, 1)
            act.wait_ge(step, 3)
            nc.scalar.activation(weight[:, :, :, :].rearrange("p g t h -> p (g t h)"), below[:, :, :, :].rearrange("p g t h -> p (g t h)"),
                                 ACT.Exp, scale=E ** -0.5).then_inc(exped, 1)
            for j in range(len(GATES_IN_WINDOW)):
                if j + 2 < len(GATES_IN_WINDOW):
                    gates.split(act, j + 2)
                gates.copy_by_scalar(act, j, ps_g[:, j % 2])

        @block.tensor
        def _(pe):
            for j in range(2):
                gates.product(pe, j, ps_g[:, j])
            pe.wait_ge(step, k.window_merged)
            for n in range(4):
                for a in range(4):
                    last = nc.tensor.transpose(ps[:, n, a * P:(a + 1) * P], part[:, (n % 2) * 4 + a, 0, (n // 2) * P:(n // 2 + 1) * P], k.ident[:, :])
                last.then_inc(turned, 1)
            for j in range(2, len(GATES_IN_WINDOW)):
                pe.wait_ge(gates.copied, j - 1)
                gates.product(pe, j, ps_g[:, j % 2])


GLA_HEADS = 4
GLA_TAU = 16.0
CH = P
N_CH = S // CH
LEVELS = 7


def stage_gla(nc, k, w_gate, w_in):
    with ExitStack() as outer:
        def hold(name, shape, dt=F32):
            return outer.enter_context(nc.sbuf_tensor(name, shape, dt))

        q = hold("gl_q", [P, 2, S])
        kk = hold("gl_k", [P, 2, S])
        cum = hold("gl_cum", [P, 2, S])
        q_in = hold("gl_q_decayed", [P, 2, S])
        k_tok = hold("gl_k_tok", [P, N_CH, 2 * P])
        v_tok = hold("gl_v_tok", [P, N_CH, GLA_HEADS * P])
        last_decay = hold("gl_last", [P, 2, N_CH])
        with ExitStack() as ctx:
            low = ctx.enter_context(nc.sbuf_tensor("gl_low", [RANK, S], F32))
            wg = ctx.enter_context(nc.sbuf_tensor("gl_wg", [RANK, 2 * P], F32))
            vT = ctx.enter_context(nc.sbuf_tensor("gl_vT", [P, GLA_HEADS, S], F32))
            pre = ctx.enter_context(nc.sbuf_tensor("gl_pre", [P, 2, S], F32))
            mag = ctx.enter_context(nc.sbuf_tensor("gl_mag", [P, 2, S], F32))
            carry = ctx.enter_context(nc.sbuf_tensor("gl_carry", [P, 2, N_CH, CH], F32))
            kd = ctx.enter_context(nc.sbuf_tensor("gl_kd", [P, 2, S], F32))
            ps = ctx.enter_context(nc.psum_tensor("gl_ps", [P, 2, NH, HALF], F32))
            ps_t = ctx.enter_context(nc.psum_tensor("gl_ps_t", [P, 2, HALF], F32))
            ps_g = ctx.enter_context(nc.psum_tensor("gl_ps_gates", [P, NH, HALF], F32))
            gates = LastGates(nc, k, ctx, "gg", w_in, GATES_IN_GLA)
            g_banks = [ps_g, ps[:, 0]]
            low_in, qk_in, v_in, pre_done, act_step, dve_step, carry_ready, turned, copied = sems(
                nc, ctx, "gl_low_in", "gl_qk_in", "gl_v_in", "gl_pre_done", "gl_act_step", "gl_dve_step", "gl_carry_ready", "gl_turned", "gl_copied")
            block = ctx.enter_context(nc.Block())
            flat = "p c s -> p (c s)"

            @block.sync
            def _(sp):
                sp.dma_start(low[:, :], k.proj[R_LOW * P:R_LOW * P + RANK, :]).then_inc(low_in, 16)
                sp.dma_start(wg[:, :], w_gate[0]).then_inc(low_in, 16)
                gates.load(sp, 0)
                sp.dma_start(vT[:, :, :], feature_tiles(k.proj[R_CV * P:(R_CV + 4) * P, :])).then_inc(v_in, 16)
                sp.dma_start(q[:, :, :], feature_tiles(k.proj[R_CQ * P:(R_CQ + 2) * P, :])).then_inc(qk_in, 16)
                sp.dma_start(kk[:, :, :], feature_tiles(k.proj[R_CK * P:(R_CK + 2) * P, :])).then_inc(qk_in, 16)
                for j in range(1, len(GATES_IN_GLA)):
                    gates.load(sp, j)
                for j in range(len(GATES_IN_GLA)):
                    gates.store(sp, j)
                gates.finish(sp)

            @block.gpsimd
            def _(pool):
                nc.gpsimd.memset(carry[:, :, :, :].rearrange("p c n t -> p (c n t)"), 1.0).then_inc(carry_ready, 1)
                for j in range(len(GATES_IN_GLA)):
                    gates.low(pool, j)

            @block.tensor
            def _(pe):
                pe.wait_ge(low_in, 32)
                for c in range(2):
                    for h in range(NH):
                        last = nc.tensor.matmul(ps[:, c, h, :], wg[:, c * P:(c + 1) * P], low[:, h * HALF:(h + 1) * HALF], start=True, stop=True)
                last.then_inc(pre_done, 1)
                pe.wait_ge(v_in, 16)
                for n in range(N_CH):
                    if n >= 2:
                        pe.wait_ge(copied, n - 1)
                    for h in range(GLA_HEADS):
                        last = nc.tensor.transpose(ps_t[:, n % 2, h * P:(h + 1) * P], vT[:, h, n * CH:(n + 1) * CH], k.ident[:, :])
                    last.then_inc(turned, 1)
                for j in range(len(GATES_IN_GLA)):
                    if j == 1:
                        pe.wait_ge(act_step, 1)
                    gates.product(pe, j, g_banks[j])
                pe.wait_ge(dve_step, 7)
                for n in range(N_CH // 2):
                    pe.wait_ge(copied, N_CH + n - 1)
                    for a in range(4):
                        last = nc.tensor.transpose(ps_t[:, n % 2, a * P:(a + 1) * P], kd[:, a % 2, (2 * n + a // 2) * CH:(2 * n + a // 2 + 1) * CH], k.ident[:, :])
                    last.then_inc(turned, 1)

            @block.scalar
            def _(act):
                count = [0]

                def link(ins):
                    count[0] += 1
                    ins.then_inc(act_step, 1)
                    act.wait_ge(act_step, count[0])

                gates.split(act, 0)
                act.wait_ge(pre_done, 1)
                for c in range(2):
                    last = nc.scalar.activation(pre[:, c, :], ps[:, c, :, :].rearrange("p h c -> p (h c)"), ACT.Identity,
                                                bias=k.cols[:, V_BG + c:V_BG + c + 1])
                link(last)
                link(nc.scalar.activation(mag[:, :, :].rearrange(flat), pre[:, :, :].rearrange(flat), ACT.Abs))
                link(nc.scalar.activation(mag[:, :, :].rearrange(flat), mag[:, :, :].rearrange(flat), ACT.Exp, scale=-1.0))
                link(nc.scalar.activation(mag[:, :, :].rearrange(flat), mag[:, :, :].rearrange(flat), ACT.Ln, bias=1.0))
                for j in range(1, len(GATES_IN_GLA)):
                    gates.split(act, j)
                act.wait_ge(dve_step, 4)
                link(nc.scalar.activation(q_in[:, :, :].rearrange(flat), cum[:, :, :].rearrange(flat), ACT.Exp, scale=1.0 / GLA_TAU))
                link(nc.scalar.activation(kd[:, :, :].rearrange(flat), kd[:, :, :].rearrange(flat), ACT.Exp, scale=1.0 / GLA_TAU))
                nc.scalar.activation(last_decay[:, :, :], cum[:, :, :].rearrange("p c (n t) -> p c n t", t=CH)[:, :, :, CH - 1], ACT.Exp, scale=1.0 / GLA_TAU)
                for j in range(len(GATES_IN_GLA)):
                    gates.copy_by_scalar(act, j, g_banks[j])

            @block.vector
            def _(dve):
                def step(ins, n):
                    ins.then_inc(dve_step, 1)
                    dve.wait_ge(dve_step, n)

                dve.wait_ge(carry_ready, 1)
                step(nc.vector.memset(carry[:, :, :, 0:1], 0.0), 1)
                for n in range(N_CH):
                    dve.wait_ge(turned, n + 1)
                    nc.vector.tensor_copy(v_tok[:, n, :], ps_t[:, n % 2, :]).then_inc(copied, 1)
                dve.wait_ge(act_step, 4)
                step(nc.vector.scalar_tensor_tensor(out=pre[:, :, :].rearrange(flat), in0=pre[:, :, :].rearrange(flat), scalar=0.0,
                                                    in1=mag[:, :, :].rearrange(flat), op0=ALU.min, op1=ALU.subtract), 2)
                step(nc.vector.tensor_tensor_scan(cum[:, :, :].rearrange(flat), carry[:, :, :, :].rearrange("p c n t -> p (c n t)"),
                                                  pre[:, :, :].rearrange(flat), 0.0, ALU.mult, ALU.add), 3)
                chunked = "p c (n t) -> p (c n) t"
                in_chunks = cum[:, :, :].rearrange(chunked, t=CH)
                step(nc.vector.tensor_tensor(kd[:, :, :].rearrange(chunked, t=CH),
                                             in_chunks[:, :, CH - 1:CH].to_broadcast([P, 2 * N_CH, CH]), in_chunks, ALU.subtract), 4)
                dve.wait_ge(qk_in, 32)
                step(nc.vector.tensor_scalar(q[:, :, :].rearrange(flat), q[:, :, :].rearrange(flat), E ** -0.5, None, ALU.mult), 5)
                dve.wait_ge(act_step, 5)
                step(nc.vector.tensor_tensor(q_in[:, :, :].rearrange(flat), q_in[:, :, :].rearrange(flat), q[:, :, :].rearrange(flat), ALU.mult), 6)
                dve.wait_ge(act_step, 6)
                step(nc.vector.tensor_tensor(kd[:, :, :].rearrange(flat), kd[:, :, :].rearrange(flat), kk[:, :, :].rearrange(flat), ALU.mult), 7)
                for n in range(N_CH // 2):
                    dve.wait_ge(turned, N_CH + n + 1)
                    nc.vector.tensor_copy(k_tok[:, 2 * n:2 * n + 2, :].rearrange("p n k -> p (n k)"), ps_t[:, n % 2, :]).then_inc(copied, 1)

        att = hold("gl_att", [P, N_CH // 2, 2, HALF])
        with ExitStack() as ctx:
            parts = ctx.enter_context(nc.sbuf_tensor("gl_parts", [P, 2, 2 * S], F32))
            dist = ctx.enter_context(nc.sbuf_tensor("gl_dist", [P, 2, 2 * S], F32))
            pair_xor = ctx.enter_context(nc.sbuf_tensor("gl_xor", [P, P], I32))
            s_index = ctx.enter_context(nc.sbuf_tensor("gl_s_index", [P, P], I32))
            distance = ctx.enter_context(nc.sbuf_tensor("gl_parting", [P, P], F32))
            above = ctx.enter_context(nc.sbuf_tensor("gl_above", [P, LEVELS + 2, P], F32))
            mask = ctx.enter_context(nc.sbuf_tensor("gl_mask", [P, LEVELS + 1, P], I32))
            ps = ctx.enter_context(nc.psum_tensor("gl_ps_att", [P, 4, 2, HALF], F32))
            index_ready, xor_ready, parted, masks, mask_ready, dist_ready, decayed, parts_ready, scored, taken = sems(
                nc, ctx, "gl_index_ready", "gl_xor_ready", "gl_parted", "gl_masks", "gl_mask_ready", "gl_dist_ready", "gl_decayed",
                "gl_parts_ready", "gl_scored", "gl_taken")
            block = ctx.enter_context(nc.Block())

            def halves(t, j):
                v = t.rearrange("p (n two h) -> p n two h", two=2, h=2 ** (j - 1))
                return v[:, :, 0, :], v[:, :, 1, :]

            @block.gpsimd
            def _(pool):
                nc.gpsimd.iota(pair_xor[:, :], pattern=[[1, P]], base=0, channel_multiplier=0).then_inc(index_ready, 1)
                nc.gpsimd.iota(s_index[:, :], pattern=[[0, P]], base=0, channel_multiplier=1).then_inc(index_ready, 1)
                pool.wait_ge(xor_ready, 2)
                nc.gpsimd.affine_select(out=distance[:, :], in_=distance[:, :], compare_op=ALU.is_ge, fill=-1.0, base=0,
                                        pattern=[[1, P]], channel_multiplier=-1).then_inc(parted, 1)
                for j in range(1, LEVELS + 1):
                    s = j % 2
                    if j >= 3:
                        pool.wait_ge(parts_ready, 2 * (j - 2))
                    left, right = halves(cum[:, :, :].rearrange("p c s -> p (c s)"), j)
                    d_left, d_right = halves(dist[:, s, :], j)
                    h = 2 ** (j - 1)
                    ref = left[:, :, h - 1:h].to_broadcast([P, 2 * S // (2 * h), h])
                    nc.gpsimd.tensor_tensor(d_left, ref, left, ALU.subtract).then_inc(dist_ready, 1)
                    nc.gpsimd.tensor_tensor(d_right, right, ref, ALU.subtract).then_inc(dist_ready, 1)

            @block.scalar
            def _(act):
                for j in range(1, LEVELS + 1):
                    act.wait_ge(dist_ready, 2 * j)
                    nc.scalar.activation(dist[:, j % 2, :], dist[:, j % 2, :], ACT.Exp, scale=1.0 / GLA_TAU).then_inc(decayed, 1)

            @block.tensor
            def _(pe):
                for j in range(LEVELS + 1):
                    if j >= 1:
                        pe.wait_ge(parts_ready, 2 * j)
                    for m in range(N_CH // 2):
                        n = j * (N_CH // 2) + m
                        if n >= 4:
                            pe.wait_ge(taken, n - 3)
                        for r in range(2):
                            rows = slice(E * r, E * r + E)
                            for a in range(2):
                                for c in range(2):
                                    tok = slice((2 * m + a) * CH, (2 * m + a + 1) * CH)
                                    if j == 0:
                                        keys, queries = kk[rows, c, tok], q[rows, c, tok]
                                    else:
                                        keys = queries = parts[rows, j % 2, c * S + tok.start:c * S + tok.stop]
                                    last = nc.tensor.matmul(ps[:, n % 4, r, (2 * a + c) * P:(2 * a + c + 1) * P], keys, queries, start=True, stop=True)
                            last.then_inc(scored, 1)

            @block.vector
            def _(dve):
                dve.wait_ge(index_ready, 2)
                nc.vector.tensor_tensor(pair_xor[:, :], pair_xor[:, :], s_index[:, :], ALU.bitwise_xor).then_inc(xor_ready, 1)
                dve.wait_ge(xor_ready, 1)
                nc.vector.tensor_copy(distance[:, :], pair_xor[:, :]).then_inc(xor_ready, 1)
                nc.vector.memset(att[:, :, :, :].rearrange("p m r x -> p (m r x)"), 0.0)
                dve.wait_ge(parted, 1)
                for j in range(LEVELS + 2):
                    last = nc.vector.tensor_scalar(above[:, j, :], distance[:, :], float(2 ** (j - 1)) if j else 0.0, None, ALU.is_ge)
                last.then_inc(masks, 1)
                dve.wait_ge(masks, 1)
                nc.vector.tensor_tensor(mask[:, :, :], above[:, 0:LEVELS + 1, :], above[:, 1:LEVELS + 2, :], ALU.subtract).then_inc(mask_ready, 1)
                dve.wait_ge(mask_ready, 1)

                def level_parts(j):
                    dve.wait_ge(decayed, j)
                    if j >= 3:
                        dve.wait_ge(scored, (j - 1) * N_CH)
                    q_l, q_r = halves(q[:, :, :].rearrange("p c s -> p (c s)"), j)
                    k_l, k_r = halves(kk[:, :, :].rearrange("p c s -> p (c s)"), j)
                    d_l, d_r = halves(dist[:, j % 2, :], j)
                    p_l, p_r = halves(parts[:, j % 2, :], j)
                    nc.vector.tensor_tensor(p_l, k_l, d_l, ALU.mult).then_inc(parts_ready, 1)
                    nc.vector.tensor_tensor(p_r, q_r, d_r, ALU.mult).then_inc(parts_ready, 1)

                level_parts(1)
                for j in range(LEVELS + 1):
                    if 1 <= j < LEVELS:
                        level_parts(j + 1)
                    for m in range(N_CH // 2):
                        n = j * (N_CH // 2) + m
                        dve.wait_ge(scored, 2 * n + 2)
                        if n >= 4:
                            dve.wait_ge(taken, n - 3)
                        nc.vector.copy_predicated(att[:, m].rearrange("p r (x t) -> p (r x) t", t=P),
                                                  mask[:, j:j + 1, :].to_broadcast([P, 8, P]),
                                                  ps[:, n % 4].rearrange("p r (x t) -> p (r x) t", t=P)).then_inc(taken, 1)

        with ExitStack() as late:
            oT = late.enter_context(nc.sbuf_tensor("gl_oT", [P, GLA_HEADS, S], F32))
            rT = late.enter_context(nc.sbuf_tensor("gl_rT", [P, GLA_HEADS, S], F32))
            r_in, = sems(nc, late, "gl_r_in")
            with ExitStack() as ctx:
                state = ctx.enter_context(nc.sbuf_tensor("gl_state", [P, 2, 2, P], F32))
                ps_o = ctx.enter_context(nc.psum_tensor("gl_ps_o", [P, 2, 2, HALF], F32))
                ps_u = ctx.enter_context(nc.psum_tensor("gl_ps_u", [P, 2, HALF], F32))
                update_done, state_ready, o_done, o_copied = sems(nc, ctx, "gl_update_done", "gl_state_ready", "gl_o_done", "gl_o_copied")
                block = ctx.enter_context(nc.Block())

                @block.sync
                def _(sp):
                    sp.dma_start(rT[:, :, :], feature_tiles(k.proj[R_CR * P:(R_CR + 4) * P, :])).then_inc(r_in, 16)

                @block.tensor
                def _(pe):
                    def update(n):
                        if n >= 2:
                            pe.wait_ge(state_ready, 2 * (n - 1))
                        for h in range(GLA_HEADS):
                            c, r = h // 2, h % 2
                            last = nc.tensor.matmul(ps_u[E * r:E * r + E, n % 2, c * P:(c + 1) * P],
                                                    k_tok[:, n, c * P + E * r:c * P + E * r + E], v_tok[:, n, h * P:(h + 1) * P],
                                                    start=True, stop=True)
                        last.then_inc(update_done, 1)

                    for n in range(N_CH):
                        if n < N_CH - 1:
                            update(n)
                        if n >= 2:
                            pe.wait_ge(o_copied, n - 1)
                        if n >= 1:
                            pe.wait_ge(state_ready, 2 * n)
                        for h in range(GLA_HEADS):
                            c, r = h // 2, h % 2
                            dst = ps_o[:, n % 2, r, c * P:(c + 1) * P]
                            last = nc.tensor.matmul(dst, v_tok[:, n, h * P:(h + 1) * P],
                                                    att[:, n // 2, r, (2 * (n % 2) + c) * P:(2 * (n % 2) + c + 1) * P], start=True, stop=(n == 0))
                            if n >= 1:
                                last = nc.tensor.matmul(dst, state[E * r:E * r + E, n % 2, c, :], q_in[E * r:E * r + E, c, n * CH:(n + 1) * CH],
                                                        start=False, stop=True)
                        last.then_inc(o_done, 1)

                @block.vector
                def _(dve):
                    for n in range(N_CH - 1):
                        dve.wait_ge(update_done, n + 1)
                        if n >= 1:
                            dve.wait_ge(o_done, n)
                        for c in range(2):
                            new = state[:, (n + 1) % 2, c, :]
                            if n == 0:
                                ins = nc.vector.tensor_copy(new, ps_u[:, n % 2, c * P:(c + 1) * P])
                            else:
                                dve.wait_ge(state_ready, 2 * n)
                                ins = nc.vector.scalar_tensor_tensor(out=new, in0=state[:, n % 2, c, :], scalar=last_decay[:, c, n:n + 1],
                                                                     in1=ps_u[:, n % 2, c * P:(c + 1) * P], op0=ALU.mult, op1=ALU.add)
                            ins.then_inc(state_ready, 1)

                @block.scalar
                def _(act):
                    for n in range(N_CH):
                        act.wait_ge(o_done, n + 1)
                        nc.scalar.activation(oT[:, :, n * CH:(n + 1) * CH].rearrange("p (c r) t -> p r c t", r=2),
                                             ps_o[:, n % 2, :, 0:2 * P].rearrange("p r (c t) -> p r c t", t=P), ACT.Copy).then_inc(o_copied, 1)

            with ExitStack() as ctx:
                sq = ctx.enter_context(nc.sbuf_tensor("gn_sq", [P, 2, S], F32))
                rinv = ctx.enter_context(nc.sbuf_tensor("gn_rinv", [P, 2, S], F32))
                sig = ctx.enter_context(nc.sbuf_tensor("gn_sig", [P, 2, S], F32))
                ps = ctx.enter_context(nc.psum_tensor("gn_ps", [P, 2, NH, HALF], F32))
                squared, summed, act_step, used, stored = sems(nc, ctx, "gn_squared", "gn_summed", "gn_act_step", "gn_used", "gn_stored")
                block = ctx.enter_context(nc.Block())

                @block.scalar
                def _(act):
                    count = [0]

                    def link(ins):
                        count[0] += 1
                        ins.then_inc(act_step, 1)
                        act.wait_ge(act_step, count[0])

                    act.wait_ge(r_in, 16)
                    for h in range(GLA_HEADS):
                        s = h % 2
                        if h >= 2:
                            act.wait_ge(used, 3 * (h - 1))
                            act.wait_ge(summed, h - 1)
                        nc.scalar.activation(sq[:, s], oT[:, h, :], ACT.Square).then_inc(squared, 1)
                        link(nc.scalar.activation(sig[:, s], rT[:, h, :], ACT.Exp, scale=-1.0))
                        link(nc.scalar.activation(sig[:, s], sig[:, s], ACT.Ln, bias=1.0))
                        nc.scalar.activation(sig[:, s], sig[:, s], ACT.Exp, scale=-1.0)
                        act.wait_ge(summed, h + 1)
                        link(nc.scalar.activation(rinv[:, s], ps[:, s, :, :].rearrange("p h c -> p (h c)"), ACT.Ln, scale=1.0 / P, bias=k.eps[:, 0:1]))
                        link(nc.scalar.activation(rinv[:, s], rinv[:, s], ACT.Exp, scale=-0.5))

                @block.tensor
                def _(pe):
                    for h in range(GLA_HEADS):
                        pe.wait_ge(squared, h + 1)
                        if h >= 2:
                            pe.wait_ge(act_step, 4 * (h - 1))
                        for a in range(NH):
                            last = nc.tensor.matmul(ps[:, h % 2, a, :], k.ones[:, :], sq[:, h % 2, a * HALF:(a + 1) * HALF], start=True, stop=True)
                        last.then_inc(summed, 1)

                @block.vector
                def _(dve):
                    for h in range(GLA_HEADS):
                        dve.wait_ge(act_step, 4 * (h + 1))
                        nc.vector.scalar_tensor_tensor(out=oT[:, h, :], in0=oT[:, h, :], scalar=k.cols[:, V_OG:V_OG + 1], in1=rinv[:, h % 2],
                                                       op0=ALU.mult, op1=ALU.mult).then_inc(used, 1)
                        nc.vector.tensor_tensor(sig[:, h % 2], sig[:, h % 2], rT[:, h, :], ALU.mult).then_inc(used, 1)
                        dve.wait_ge(used, 3 * h + 2)
                        nc.vector.tensor_tensor(oT[:, h, :], oT[:, h, :], sig[:, h % 2], ALU.mult).then_inc(used, 1)

                @block.sync
                def _(sp):
                    for h in range(GLA_HEADS):
                        sp.wait_ge(used, 3 * h + 3)
                        sp.dma_start(k.mix[(Y_C + h) * P:(Y_C + h + 1) * P, :], oT[:, h, :]).then_inc(stored, 16)
                    sp.wait_ge(stored, 16 * GLA_HEADS)


SB_HEADS = 4


def stage_stick(nc, k):
    with ExitStack() as outer:
        qk = outer.enter_context(nc.sbuf_tensor("sb_qk", [P, 4, S], F32))
        v_tok = outer.enter_context(nc.sbuf_tensor("sb_v_tok", [P, S // P, SB_HEADS * E], F32))
        with ExitStack() as ctx:
            vT = ctx.enter_context(nc.sbuf_tensor("sb_vT", [P, 2, S], F32))
            ps = ctx.enter_context(nc.psum_tensor("sb_ps_v", [P, 4, HALF], F32))
            loaded, q_loaded, turned, copied, scaled = sems(nc, ctx, "sb_loaded", "sb_q_loaded", "sb_turned", "sb_copied", "sb_scaled")
            block = ctx.enter_context(nc.Block())

            @block.sync
            def _(sp):
                sp.dma_start(vT[:, :, :], feature_tiles(k.proj[R_DV * P:(R_DV + 2) * P, :])).then_inc(loaded, 16)
                sp.dma_start(qk[:, :, :], feature_tiles(k.proj[R_DQ * P:(R_DQ + 4) * P, :])).then_inc(q_loaded, 16)

            @block.tensor
            def _(pe):
                pe.wait_ge(loaded, 16)
                for n in range(4):
                    for a in range(4):
                        last = nc.tensor.transpose(ps[:, n, a * P:(a + 1) * P], vT[:, a % 2, (2 * n + a // 2) * P:(2 * n + a // 2 + 1) * P], k.ident[:, :])
                    last.then_inc(turned, 1)

            @block.vector
            def _(dve):
                for n in range(4):
                    dve.wait_ge(turned, n + 1)
                    nc.vector.tensor_copy(v_tok[:, 2 * n:2 * n + 2, :].rearrange("p u e -> p (u e)"), ps[:, n, :])
                dve.wait_ge(q_loaded, 16)
                nc.vector.tensor_scalar(qk[:, 0:2, :], qk[:, 0:2, :], E ** -0.5, None, ALU.mult)

        with ExitStack() as ctx:
            STEPS = [(Q, a, r) for Q in range(NH) for a in reversed(range(4 * Q + 4)) for r in range(2)]
            N = len(STEPS)
            mag = ctx.enter_context(nc.sbuf_tensor("sb_mag", [P, 2, 2, HALF], F32))
            sp_t = ctx.enter_context(nc.sbuf_tensor("sb_softplus", [P, 2, 2, HALF], F32))
            later = ctx.enter_context(nc.sbuf_tensor("sb_later", [P, 2, 2, HALF], F32))
            w = ctx.enter_context(nc.sbuf_tensor("sb_weight", [P, 2, 2, HALF], F32))
            zs = ctx.enter_context(nc.sbuf_tensor("sb_z", [P, 3, 2, HALF], F32))
            yT = ctx.enter_context(nc.sbuf_tensor("sb_yT", [P, 2, S], F32))
            ps_z = ctx.enter_context(nc.psum_tensor("sb_ps_z", [P, 2, HALF], F32))
            ps_c = ctx.enter_context(nc.psum_tensor("sb_ps_c", [P, 2, 2, HALF], F32))
            ps_o = ctx.enter_context(nc.psum_tensor("sb_ps_o", [P, 2, HALF], F32))
            (z_done, mag_ready, exped, logged, plus_ready, cut, later_ready, cum_done, arg_ready, w_ready, w_cut, o_done, o_copied, stored,
             z_read) = sems(
                nc, ctx, "sb_z_done", "sb_mag_ready", "sb_exped", "sb_logged", "sb_plus_ready", "sb_cut", "sb_later_ready", "sb_cum_done",
                "sb_arg_ready", "sb_w_ready", "sb_w_cut", "sb_o_done", "sb_o_copied", "sb_stored", "sb_z_read")
            block = ctx.enter_context(nc.Block())

            def cols(n):
                Q, a, r = STEPS[n]
                return slice(max(0, a * P - Q * HALF), HALF)

            def diagonal(n):
                Q, a, r = STEPS[n]
                return a >= 4 * Q

            cuts = [0]
            for n in range(N):
                cuts.append(cuts[-1] + diagonal(n))
            first_of_half = [STEPS[n][1] == 4 * STEPS[n][0] + 3 for n in range(N)]

            @block.tensor
            def _(pe):
                def scores(n):
                    Q, a, r = STEPS[n]
                    if n >= 1:
                        pe.wait_ge(z_read, n)
                    c = cols(n)
                    for j in range(2):
                        last = nc.tensor.matmul(ps_z[:, j, c], qk[E * r:E * r + E, 2 + j, a * P:(a + 1) * P],
                                                qk[E * r:E * r + E, j, Q * HALF + c.start:(Q + 1) * HALF], start=True, stop=True)
                    last.then_inc(z_done, 1)

                def sums(n):
                    c = cols(n)
                    pe.wait_ge(plus_ready, n + 1)
                    if diagonal(n):
                        pe.wait_ge(cut, cuts[n + 1])
                    if n >= 2:
                        pe.wait_ge(arg_ready, n - 1)
                    late = STEPS[n][1] < 4 * STEPS[n][0] + 3
                    if late:
                        pe.wait_ge(later_ready, n - 1)
                    held = slice(c.start + P, HALF) if diagonal(n) else c
                    for j in range(2):
                        if late:
                            nc.tensor.matmul(ps_c[:, n % 2, j, held], k.ones[:, :], later[:, n % 2, j, held], start=True, stop=False,
                                             skip_group_check=True)
                        last = nc.tensor.matmul(ps_c[:, n % 2, j, c], k.reach[:, :], sp_t[:, n % 2, j, c], start=not late, stop=True,
                                                skip_group_check=True)
                    last.then_inc(cum_done, 1)

                def values(n):
                    Q, a, r = STEPS[n]
                    c = cols(n)
                    pe.wait_ge(w_ready, n + 1)
                    if diagonal(n):
                        pe.wait_ge(w_cut, cuts[n + 1])
                    if first_of_half[n] and Q > 0:
                        pe.wait_ge(o_copied, 2)
                    for j in range(2):
                        last = nc.tensor.matmul(ps_o[E * j:E * j + E, r, c], v_tok[:, a, (2 * j + r) * E:(2 * j + r + 1) * E],
                                                w[:, n % 2, j, c], start=first_of_half[n], stop=(a == 0), skip_group_check=True)
                    last.then_inc(o_done, 1)

                for n in range(N + 3):
                    if n < N:
                        scores(n)
                    if 1 <= n <= N:
                        sums(n - 1)
                    if n >= 3:
                        values(n - 3)

            @block.vector
            def _(dve):
                def take_scores(n):
                    c = cols(n)
                    dve.wait_ge(z_done, n + 1)
                    if n >= 3:
                        dve.wait_ge(arg_ready, n - 2)
                        dve.wait_ge(mag_ready, n - 2)
                    nc.vector.tensor_copy(zs[:, n % 3, :, c], ps_z[:, :, c]).then_inc(z_read, 1)

                def softplus(n):
                    c = cols(n)
                    dve.wait_ge(logged, n + 1)
                    dve.wait_ge(z_read, n + 1)
                    if n >= 2:
                        dve.wait_ge(cum_done, n - 1)
                        dve.wait_ge(later_ready, n - 1)
                    nc.vector.scalar_tensor_tensor(out=sp_t[:, n % 2, :, c], in0=zs[:, n % 3, :, c], scalar=0.0, in1=mag[:, n % 2, :, c],
                                                   op0=ALU.max, op1=ALU.add).then_inc(plus_ready, 1)

                def accumulate(n):
                    c = cols(n)
                    if diagonal(n):
                        dve.wait_ge(cut, cuts[n + 1])
                    dve.wait_ge(plus_ready, n + 1)
                    dve.wait_ge(cum_done, n + 1)
                    r = n % 2
                    if diagonal(n):
                        own = slice(c.start, c.start + P)
                        last = nc.vector.tensor_copy(later[:, r, :, own], sp_t[:, n % 2, :, own])
                        c = slice(c.start + P, HALF)
                    if c.start < HALF:
                        last = nc.vector.tensor_tensor(later[:, r, :, c], later[:, r, :, c], sp_t[:, n % 2, :, c], ALU.add)
                    last.then_inc(later_ready, 1)

                def argument(n):
                    c = cols(n)
                    dve.wait_ge(cum_done, n + 1)
                    if n >= 2:
                        dve.wait_ge(o_done, n - 1)
                    nc.vector.tensor_tensor(w[:, n % 2, :, c], zs[:, n % 3, :, c], ps_c[:, n % 2, :, c], ALU.subtract).then_inc(arg_ready, 1)

                def take(Q):
                    last_step = [n for n in range(N) if STEPS[n][0] == Q][-1]
                    dve.wait_ge(o_done, last_step + 1)
                    for r in range(2):
                        nc.vector.tensor_copy(stage_o[:, r, Q * HALF:(Q + 1) * HALF], ps_o[:, r, :]).then_inc(o_copied, 1)

                stage_o = yT
                for n in range(N + 2):
                    if 1 <= n <= N:
                        softplus(n - 1)
                    if n < N:
                        take_scores(n)
                    if n >= 2:
                        argument(n - 2)
                        accumulate(n - 2)
                    if n == 2 * 4 + 2:
                        take(0)
                take(1)

            @block.scalar
            def _(act):
                def logs(n):
                    c = cols(n)
                    act.wait_ge(z_read, n + 1)
                    if n >= 2:
                        act.wait_ge(plus_ready, n - 1)
                    nc.scalar.activation(mag[:, n % 2, :, c], zs[:, n % 3, :, c], ACT.Abs).then_inc(mag_ready, 1)
                    act.wait_ge(mag_ready, n + 1)
                    nc.scalar.activation(mag[:, n % 2, :, c], mag[:, n % 2, :, c], ACT.Exp, scale=-1.0).then_inc(exped, 1)
                    act.wait_ge(exped, n + 1)
                    nc.scalar.activation(mag[:, n % 2, :, c], mag[:, n % 2, :, c], ACT.Ln, bias=1.0).then_inc(logged, 1)

                def weights(n):
                    c = cols(n)
                    act.wait_ge(arg_ready, n + 1)
                    nc.scalar.activation(w[:, n % 2, :, c], w[:, n % 2, :, c], ACT.Exp).then_inc(w_ready, 1)

                for n in range(N + 2):
                    if n < N:
                        logs(n)
                    if n >= 2:
                        weights(n - 2)

            @block.gpsimd
            def _(pool):
                def keep_before(tile, n):
                    c = cols(n)
                    own = tile[:, n % 2, :, c.start:c.start + P]
                    return nc.gpsimd.affine_select(out=own, in_=own, compare_op=ALU.is_gt, fill=0.0, base=0,
                                                   pattern=[[0, 2], [1, P]], channel_multiplier=-1)

                for n in range(N + 1):
                    if n < N and diagonal(n):
                        pool.wait_ge(plus_ready, n + 1)
                        keep_before(sp_t, n).then_inc(cut, 1)
                    if n >= 1 and diagonal(n - 1):
                        pool.wait_ge(w_ready, n)
                        keep_before(w, n - 1).then_inc(w_cut, 1)

            @block.sync
            def _(sp):
                sp.wait_ge(o_copied, 4)
                heads = k.mix[Y_D * P:Y_TILES * P, :].rearrange("(j r e) s -> j e r s", r=2, e=E)
                for j in range(2):
                    sp.dma_start(heads[j], yT[E * j:E * j + E, :, :]).then_inc(stored, 16)
                sp.wait_ge(stored, 32)


def stage_mixers(nc, k, a):
    stage_window(nc, k, a["w_in"])
    stage_gla(nc, k, a["gla_w_gate"], a["w_in"])
    stage_stick(nc, k)


def build(nc, a, out):
    k = Kernel()
    Kernel.in_use = []
    k.proj = nc.dram_tensor("proj", (PROJ_ROWS, S), F32, kind="Internal").ap()
    k.xT_dram = nc.dram_tensor("xT_dram", (D, S), F32, kind="Internal").ap()
    k.logits = nc.dram_tensor("logits", (4 * P, S), F32, kind="Internal").ap()
    k.merged = nc.dram_tensor("merged", (D, S), F32, kind="Internal").ap()
    k.window = nc.dram_tensor("window", (3, S, ROW), F32, kind="Internal").ap()
    k.mix = nc.dram_tensor("mix", (Y_TILES * P, S), F32, kind="Internal").ap()
    with ExitStack() as ctx:
        def sb(name, shape, dt=F32):
            return ctx.enter_context(nc.sbuf_tensor(name, shape, dt))

        k.ident = sb("ident", [P, P])
        k.ones = sb("ones", [P, P])
        k.headsum = sb("headsum", [P, P])
        k.reach = sb("reach", [P, P])
        k.cols = sb("cols", [P, P])
        k.taps = sb("taps", [P, 2, 31])
        k.mod = sb("mod", [P, N_MOD])
        k.scale1 = sb("scale1", [P, KT])
        k.scale2 = sb("scale2", [P, KT])
        k.eps = sb("eps", [P, 1])
        with ExitStack() as front:
            k.h_hi = front.enter_context(nc.sbuf_tensor("h_hi", [P, KT, S], F32R))
            k.h_lo = front.enter_context(nc.sbuf_tensor("h_lo", [P, KT, S], F32R))
            with nc.sbuf_tensor("xT", [P, KT, S], F32) as xT, nc.sbuf_tensor("rinv1", [P, S], F32) as rinv1:
                stage_prepare(nc, k, a["x"], a["c"], a["w_ada"], a["b_ada"], a["g_mix"], a["g_mlp"], a["conv_w"], a["conv_b"],
                              a["conv_ln_g"], a["conv_ln_b"], a["gla_b_gate"], a["gla_o_gain"], a["q_gain"], a["k_gain"], xT, rinv1)
                stage_project(nc, k, a["w_in"], a["w_ada"], xT, rinv1)
            stage_mixers(nc, k, a)
            recycle_semaphores(nc)
            with nc.sbuf_tensor("y_hi", [P, Y_TILES, S], F32R) as k.y_hi, nc.sbuf_tensor("y_lo", [P, Y_TILES, S], F32R) as k.y_lo:
                stage_merge(nc, k, a["w_in"], [a["w_br_a"], a["w_br_b"], a["w_br_c"], a["w_br_d"]])
        x1T = sb("x1T", [P, KT, S])
        rinv2 = sb("rinv2", [P, S])
        with nc.sbuf_tensor("m_hi", [P, KT, S], F32R) as m_hi, nc.sbuf_tensor("m_lo", [P, KT, S], F32R) as m_lo:
            stage_out(nc, k, a["w_out"], m_hi, m_lo, x1T, rinv2)
        with nc.sbuf_tensor("h2_hi", [P, KT, S], F32R) as h2_hi, nc.sbuf_tensor("h2_lo", [P, KT, S], F32R) as h2_lo:
            stage_mlp(nc, k, a["w_up"], a["w_down"], h2_hi, h2_lo, x1T, rinv2, k.scale2, k.mod[:, M_SH2:M_SH2 + KT], out)


_INS = ["x", "c", "w_ada", "b_ada", "g_mix", "w_in", "q_gain", "k_gain", "conv_w", "conv_b", "conv_ln_g", "conv_ln_b",
        "gla_w_gate", "gla_b_gate", "gla_o_gain", "w_br_a", "w_br_b", "w_br_c", "w_br_d", "w_out", "g_mlp", "w_up", "w_down"]


def kernel(**inputs):
    import numpy as np
    import concourse.bacc as bacc
    from concourse.bass_utils import run_bass_kernel_spmd as run

    nc = bacc.Bacc("TRN2", target_bir_lowering=False, num_devices=1)
    arrays, aps = {}, {}
    for name in _INS:
        arrays[f"{name}_dram"] = np.ascontiguousarray(inputs[name])
        aps[name] = nc.dram_tensor(f"{name}_dram", arrays[f"{name}_dram"].shape, F32, kind="ExternalInput").ap()
    out = nc.dram_tensor("out_dram", (1, S, D), F32, kind="ExternalOutput").ap()
    build(nc, aps, out)
    r = run(nc, [arrays], core_ids=[0])
    return r.results[0]["out_dram"]
```
